# Optimizing a Trainium2 kernel written in Bass

```python
import jax, jax.numpy as jnp
from jax import lax
import numpy as np
import math

D_MODEL = 1024
BATCH = 1
SEQ = 512
DEPTH = 2

N_META = 16
D_MIX = D_MODEL
D_CONV = D_MIX // 2
CONV_WIDTH = 31
N_HEADS = 8
HEAD_DIM = 64
D_ATTN = N_HEADS * HEAD_DIM
N_IDX_HEADS = 8
IDX_DIM = 64
TOPK_MAX = 256
ROPE_THETA = 10000.0
Q_BLOCK = 64
POS_BLOCK = 128
LN_EPS = 1e-5
IDX_SCALE = IDX_DIM ** -0.5
IDX_W_SCALE = N_IDX_HEADS ** -0.5
DEEPNORM_ALPHA = (2.0 * DEPTH) ** 0.25
DEEPNORM_BETA = (8.0 * DEPTH) ** -0.25

IN_SIZES = [D_CONV, D_CONV, D_CONV, D_ATTN, D_ATTN, D_ATTN, D_ATTN,
            N_IDX_HEADS * IDX_DIM, IDX_DIM, N_IDX_HEADS]
D_IN = sum(IN_SIZES)
IN_SPLITS = [sum(IN_SIZES[:i + 1]) for i in range(len(IN_SIZES) - 1)]


def layer_norm(x, g, b):
    xf = x.astype(jnp.float32)
    mu = jnp.mean(xf, axis=-1, keepdims=True)
    var = jnp.mean(jnp.square(xf - mu), axis=-1, keepdims=True)
    y = (xf - mu) * lax.rsqrt(var + LN_EPS) * g.astype(jnp.float32) + b.astype(jnp.float32)
    return y.astype(x.dtype)

def rope_tables(length, dim):
    inv_freq = ROPE_THETA ** (-jnp.arange(0, dim, 2, dtype=jnp.float32) / dim)
    ang = jnp.arange(length, dtype=jnp.float32)[:, None] * inv_freq[None, :]
    return jnp.cos(ang), jnp.sin(ang)

def apply_rope(x, cos, sin):
    half = x.shape[-1] // 2
    x1, x2 = x[..., :half], x[..., half:]
    out = jnp.concatenate([x1 * cos - x2 * sin, x2 * cos + x1 * sin], axis=-1)
    return out.astype(x.dtype)

def conformer_conv_branch(a, g, z, w_dw, b_dw, ln_g, ln_b):
    u = a * jax.nn.sigmoid(g)
    u = lax.conv_general_dilated(
        u, w_dw[:, None, :].astype(u.dtype), window_strides=(1,),
        padding=[(CONV_WIDTH - 1, 0)],
        dimension_numbers=('NWC', 'WIO', 'NWC'),
        feature_group_count=D_CONV) + b_dw
    u = jax.nn.silu(layer_norm(u, ln_g, ln_b))
    return u * jax.nn.silu(z)

def dsa_sparse_attention(q, k, v, qi, ki, wi, topk):
    B, L = q.shape[0], q.shape[1]
    nb = L // Q_BLOCK
    key_pos = jnp.arange(L)
    ki32 = ki.astype(jnp.float32)

    def to_blocks(t):
        return jnp.moveaxis(t.reshape((B, nb, Q_BLOCK) + t.shape[2:]), 1, 0)

    def one_block(args):
        qb, qib, wib, start = args
        q_pos = start + jnp.arange(Q_BLOCK)
        causal = key_pos[None, :] <= q_pos[:, None]
        logits = jnp.einsum('bqhd,bsd->bqhs', qib.astype(jnp.float32), ki32) * IDX_SCALE
        score = jnp.einsum('bqhs,bqh->bqs', jax.nn.relu(logits),
                           wib.astype(jnp.float32) * IDX_W_SCALE)
        score = jnp.where(causal[None], score, -jnp.inf)
        _, idx = lax.top_k(score, topk)
        valid = idx <= q_pos[None, :, None]
        kg = jax.vmap(lambda kk, ii: kk[ii])(k, idx)
        vg = jax.vmap(lambda vv, ii: vv[ii])(v, idx)
        s = jnp.einsum('bqhd,bqkhd->bqhk', qb, kg).astype(jnp.float32) * (HEAD_DIM ** -0.5)
        s = jnp.where(valid[:, :, None, :], s, -jnp.inf)
        p = jax.nn.softmax(s, axis=-1).astype(v.dtype)
        return jnp.einsum('bqhk,bqkhd->bqhd', p, vg)

    starts = jnp.arange(nb) * Q_BLOCK
    out = lax.map(one_block, (to_blocks(q), to_blocks(qi), to_blocks(wi), starts))
    return jnp.moveaxis(out, 0, 1).reshape(B, L, D_ATTN)

def first_inputs(seed: int = 0) -> dict:
    key = jax.random.key(seed)
    ks = jax.random.split(key, 10)
    f32 = jnp.float32
    x = jax.random.normal(ks[0], (BATCH, SEQ, D_MODEL), f32)
    meta_tokens = jax.random.normal(ks[1], (N_META, D_MODEL), f32)
    w_in = jax.random.normal(ks[2], (DEPTH, D_MODEL, D_IN), f32) * D_MODEL ** -0.5
    conv_w = jax.random.normal(ks[3], (DEPTH, CONV_WIDTH, D_CONV), f32) * CONV_WIDTH ** -0.5
    conv_b = 0.01 * jax.random.normal(ks[4], (DEPTH, D_CONV), f32)
    conv_ln_g = 1.0 + 0.01 * jax.random.normal(ks[5], (DEPTH, D_CONV), f32)
    conv_ln_b = 0.01 * jax.random.normal(ks[6], (DEPTH, D_CONV), f32)
    w_out = jax.random.normal(ks[7], (DEPTH, D_MIX, D_MODEL), f32) * (D_MIX ** -0.5) * DEEPNORM_BETA
    post_ln_g = 1.0 + 0.01 * jax.random.normal(ks[8], (DEPTH, D_MODEL), f32)
    post_ln_b = 0.01 * jax.random.normal(ks[9], (DEPTH, D_MODEL), f32)
    return {"x": x, "meta_tokens": meta_tokens, "w_in": w_in, "conv_w": conv_w,
            "conv_b": conv_b, "conv_ln_g": conv_ln_g, "conv_ln_b": conv_ln_b,
            "w_out": w_out, "post_ln_g": post_ln_g, "post_ln_b": post_ln_b}

def first_block(x, meta_tokens, w_in, conv_w, conv_b, conv_ln_g, conv_ln_b, w_out,
              post_ln_g, post_ln_b):
    B, S, D = x.shape
    L = S + N_META
    topk = min(TOPK_MAX, L // 4)
    Lp = -(-L // POS_BLOCK) * POS_BLOCK
    meta = jnp.broadcast_to(meta_tokens[None].astype(x.dtype), (B, N_META, D))
    h = jnp.concatenate([meta, x, jnp.zeros((B, Lp - L, D), x.dtype)], axis=1)
    cos, sin = rope_tables(Lp, HEAD_DIM)
    cos_h, sin_h = cos[:, None, :], sin[:, None, :]

    for l in range(DEPTH):
        proj = jnp.einsum('bld,de->ble', h, w_in[l])
        a, g, zc, q, k, v, za, qi, ki, wi = jnp.split(proj, IN_SPLITS, axis=-1)
        y_conv = conformer_conv_branch(a, g, zc, conv_w[l], conv_b[l], conv_ln_g[l], conv_ln_b[l])
        q = apply_rope(q.reshape(B, Lp, N_HEADS, HEAD_DIM), cos_h, sin_h)
        k = apply_rope(k.reshape(B, Lp, N_HEADS, HEAD_DIM), cos_h, sin_h)
        v = v.reshape(B, Lp, N_HEADS, HEAD_DIM)
        qi = apply_rope(qi.reshape(B, Lp, N_IDX_HEADS, IDX_DIM), cos_h, sin_h)
        ki = apply_rope(ki, cos, sin)
        y_attn = dsa_sparse_attention(q, k, v, qi, ki, wi, topk) * jax.nn.silu(za)
        y = jnp.einsum('ble,ed->bld', jnp.concatenate([y_conv, y_attn], axis=-1), w_out[l])
        h = layer_norm(DEEPNORM_ALPHA * h + y, post_ln_g[l], post_ln_b[l])

    return h[:, N_META:L]


DEPTH_2 = 1

ATT_HEADS = 8
ATT_KV_HEADS = 2
ATT_HEAD_DIM = 64
ATT_GROUP = ATT_HEADS // ATT_KV_HEADS
ATT_Q_DIM = ATT_HEADS * ATT_HEAD_DIM
ATT_KV_DIM = ATT_KV_HEADS * ATT_HEAD_DIM
WINDOW = 128
ATT_BLOCK = 128
ROPE_DIM = ATT_HEAD_DIM // 4
ROPE_THETA_2 = 500000.0

GLA_HEADS = 4
GLA_KEY_DIM = D_MODEL // 2
GLA_VAL_DIM = D_MODEL
GLA_DK = GLA_KEY_DIM // GLA_HEADS
GLA_DV = GLA_VAL_DIM // GLA_HEADS
GLA_GATE_RANK = 16
GLA_GATE_NORM = 16.0
GLA_CHUNK = 64

N_EXPERTS = 16
EXPERT_FF = D_MODEL
CAPACITY_FACTOR = 2

PLE_DIM = 256

EPS = 1e-6

IN_SIZES_2 = (ATT_Q_DIM, ATT_KV_DIM, ATT_KV_DIM,
            GLA_KEY_DIM, GLA_KEY_DIM, GLA_VAL_DIM, GLA_VAL_DIM,
            GLA_GATE_RANK, GLA_GATE_RANK, D_MODEL, D_MODEL)
IN_DIM = ATT_Q_DIM + 2 * ATT_KV_DIM + 2 * GLA_KEY_DIM + 2 * GLA_VAL_DIM + 2 * GLA_GATE_RANK + 2 * D_MODEL


def rmsnorm(x, g):
    xf = x.astype(jnp.float32)
    y = xf * lax.rsqrt(jnp.mean(xf * xf, axis=-1, keepdims=True) + EPS)
    return (y * g.astype(jnp.float32)).astype(x.dtype)

def split_columns(proj):
    parts, start = [], 0
    for size in IN_SIZES_2:
        parts.append(proj[..., start:start + size])
        start += size
    return parts

def partial_rope(t, positions):
    half = ROPE_DIM // 2
    inv_freq = ROPE_THETA_2 ** (-jnp.arange(0, ROPE_DIM, 2, dtype=jnp.float32) / ROPE_DIM)
    ang = positions.astype(jnp.float32)[..., None] * inv_freq
    cos = jnp.cos(ang)[:, :, None, :].astype(t.dtype)
    sin = jnp.sin(ang)[:, :, None, :].astype(t.dtype)
    t1 = t[..., :half]
    t2 = t[..., half:ROPE_DIM]
    rot = jnp.concatenate([t1 * cos - t2 * sin, t2 * cos + t1 * sin], axis=-1)
    return jnp.concatenate([rot, t[..., ROPE_DIM:]], axis=-1)

def windowed_gqa(q, k, v, sink):
    B, S = q.shape[0], q.shape[1]
    nb = S // ATT_BLOCK
    qb = q.reshape(B, nb, ATT_BLOCK, ATT_KV_HEADS, ATT_GROUP, ATT_HEAD_DIM)

    def band(t):
        tp = jnp.pad(t, ((0, 0), (ATT_BLOCK, ATT_BLOCK), (0, 0), (0, 0)))
        tp = tp.reshape(B, nb + 2, ATT_BLOCK, ATT_KV_HEADS, ATT_HEAD_DIM)
        return jnp.concatenate([tp[:, :-2], tp[:, 1:-1], tp[:, 2:]], axis=2)

    kb, vb = band(k), band(v)
    scores = jnp.einsum('bnqhgd,bnkhd->bnhgqk', qb, kb).astype(jnp.float32) * (ATT_HEAD_DIM ** -0.5)
    blk = jnp.arange(nb)[:, None, None]
    qi = blk * ATT_BLOCK + jnp.arange(ATT_BLOCK)[None, :, None]
    kj = (blk - 1) * ATT_BLOCK + jnp.arange(3 * ATT_BLOCK)[None, None, :]
    valid = (jnp.abs(qi - kj) <= WINDOW) & (kj >= 0) & (kj < S)
    scores = jnp.where(valid[None, :, None, None], scores, -jnp.inf)
    sink_b = sink.astype(jnp.float32).reshape(1, 1, ATT_KV_HEADS, ATT_GROUP, 1, 1)
    m = jnp.maximum(jnp.max(scores, axis=-1, keepdims=True), sink_b)
    e = jnp.exp(scores - m)
    probs = e / (jnp.sum(e, axis=-1, keepdims=True) + jnp.exp(sink_b - m))
    out = jnp.einsum('bnhgqk,bnkhd->bnqhgd', probs.astype(v.dtype), vb)
    return out.reshape(B, S, ATT_Q_DIM)

def gla_chunked(q, k, v, log_a, strict):
    B, S, H, dk = q.shape
    dv = v.shape[-1]
    nc = S // GLA_CHUNK

    def chunk(t):
        return t.reshape(B, nc, GLA_CHUNK, H, t.shape[-1])

    qc, kc, vc, ac = chunk(q), chunk(k), chunk(v), chunk(log_a)
    b = jnp.cumsum(ac, axis=2)
    g = b[:, :, -1]
    q_t = qc * jnp.exp(b)
    k_t = kc * jnp.exp(-b)
    k_end = kc * jnp.exp(g[:, :, None] - b)
    attn = jnp.einsum('bclhd,bcmhd->bchlm', q_t, k_t)
    mask = jnp.tril(jnp.ones((GLA_CHUNK, GLA_CHUNK), dtype=bool), -1 if strict else 0)
    attn = jnp.where(mask, attn, 0.0)
    o_intra = jnp.einsum('bchlm,bcmhe->bclhe', attn, vc)
    kv = jnp.einsum('bclhd,bclhe->bchde', k_end, vc)
    decay = jnp.exp(g)

    def step(state, xs):
        dec, kv_c = xs
        return dec[..., None] * state + kv_c, state

    s0 = jnp.zeros((B, H, dk, dv), dtype=jnp.float32)
    _, s_prev = lax.scan(step, s0, (jnp.moveaxis(decay, 1, 0), jnp.moveaxis(kv, 1, 0)))
    s_prev = jnp.moveaxis(s_prev, 0, 1)
    o_inter = jnp.einsum('bclhd,bchde->bclhe', q_t, s_prev)
    return (o_intra + o_inter).reshape(B, S, H, dv)

def gla_branch(gq, gk, gv, gr, z_f, z_b, up_f, bias_f, up_b, bias_b, norm_gain):
    B, S = gq.shape[0], gq.shape[1]
    f32 = jnp.float32
    q = gq.astype(f32).reshape(B, S, GLA_HEADS, GLA_DK) * (GLA_DK ** -0.5)
    k = gk.astype(f32).reshape(B, S, GLA_HEADS, GLA_DK)
    v = gv.astype(f32).reshape(B, S, GLA_HEADS, GLA_DV)
    la_f = (jax.nn.log_sigmoid(z_f.astype(f32) @ up_f.astype(f32) + bias_f.astype(f32)) / GLA_GATE_NORM).reshape(B, S, GLA_HEADS, GLA_DK)
    la_b = (jax.nn.log_sigmoid(z_b.astype(f32) @ up_b.astype(f32) + bias_b.astype(f32)) / GLA_GATE_NORM).reshape(B, S, GLA_HEADS, GLA_DK)
    o_f = gla_chunked(q, k, v, la_f, strict=False)
    flip = lambda t: jnp.flip(t, axis=1)
    o_b = flip(gla_chunked(flip(q), flip(k), flip(v), flip(la_b), strict=True))
    o = o_f + o_b
    o = o * lax.rsqrt(jnp.mean(o * o, axis=-1, keepdims=True) + EPS) * norm_gain.astype(f32).reshape(GLA_HEADS, GLA_DV)
    o = o.reshape(B, S, GLA_VAL_DIM) * jax.nn.silu(gr.astype(f32))
    return o.astype(gq.dtype)

def expert_choice_ffn(xn, w_router, w_gate, w_up, w_down):
    B, S, D = xn.shape
    cap = CAPACITY_FACTOR * S // N_EXPERTS
    aff = jax.nn.softmax(jnp.einsum('bsd,de->bse', xn, w_router).astype(jnp.float32), axis=-1)
    top_aff, top_idx = lax.top_k(jnp.swapaxes(aff, 1, 2), cap)
    bidx = jnp.arange(B)[:, None, None]
    xg = xn[bidx, top_idx]
    hid = jax.nn.silu(jnp.einsum('becd,edf->becf', xg, w_gate)) * jnp.einsum('becd,edf->becf', xg, w_up)
    y = jnp.einsum('becf,efd->becd', hid, w_down) * top_aff[..., None].astype(xn.dtype)
    return jnp.zeros((B, S, D), dtype=y.dtype).at[bidx, top_idx].add(y)

def second_inputs(seed: int = 0) -> dict:
    key = jax.random.key(seed)
    ks = jax.random.split(key, 32)
    f32 = jnp.float32
    L, D = DEPTH_2, D_MODEL

    def w(k, shape, fan_in):
        return jax.random.normal(k, shape, f32) * (fan_in ** -0.5)

    def gain(k, shape):
        return 1.0 + 0.1 * jax.random.normal(k, shape, f32)

    x = jax.random.normal(ks[0], (BATCH, SEQ, D), f32)
    p = jax.random.normal(ks[1], (L, BATCH, SEQ, PLE_DIM), f32)
    offsets = jax.random.randint(ks[2], (BATCH, 1), 0, 1024, dtype=jnp.int32)
    positions = jnp.arange(SEQ, dtype=jnp.int32)[None, :] + offsets
    return {
        "x": x,
        "p": p,
        "positions": positions,
        "norm_mix": gain(ks[3], (L, D)),
        "w_in": w(ks[4], (L, D, IN_DIM), D),
        "gla_gate_up_fwd": w(ks[5], (L, GLA_GATE_RANK, GLA_KEY_DIM), GLA_GATE_RANK),
        "gla_gate_bias_fwd": 1.0 + 0.5 * jax.random.normal(ks[6], (L, GLA_KEY_DIM), f32),
        "gla_gate_up_bwd": w(ks[7], (L, GLA_GATE_RANK, GLA_KEY_DIM), GLA_GATE_RANK),
        "gla_gate_bias_bwd": 1.0 + 0.5 * jax.random.normal(ks[8], (L, GLA_KEY_DIM), f32),
        "attn_sink": 0.5 * jax.random.normal(ks[9], (L, ATT_HEADS), f32),
        "gla_norm": gain(ks[10], (L, GLA_VAL_DIM)),
        "w_branch_attn": w(ks[11], (L, ATT_Q_DIM, D), ATT_Q_DIM),
        "w_branch_gla": w(ks[12], (L, GLA_VAL_DIM, D), GLA_VAL_DIM),
        "w_out": w(ks[13], (L, D, D), D),
        "norm_ffn": gain(ks[14], (L, D)),
        "w_router": w(ks[15], (L, D, N_EXPERTS), D),
        "w_exp_gate": w(ks[16], (L, N_EXPERTS, D, EXPERT_FF), D),
        "w_exp_up": w(ks[17], (L, N_EXPERTS, D, EXPERT_FF), D),
        "w_exp_down": w(ks[18], (L, N_EXPERTS, EXPERT_FF, D), EXPERT_FF),
        "norm_ple": gain(ks[19], (L, D)),
        "w_ple_gate": w(ks[20], (L, D, D), D),
        "w_ple": w(ks[21], (L, PLE_DIM, D), PLE_DIM),
        "norm_final": gain(ks[22], (D,)),
    }

def second_block(x, p, positions, norm_mix, w_in, gla_gate_up_fwd, gla_gate_bias_fwd,
              gla_gate_up_bwd, gla_gate_bias_bwd, attn_sink, gla_norm, w_branch_attn,
              w_branch_gla, w_out, norm_ffn, w_router, w_exp_gate, w_exp_up, w_exp_down,
              norm_ple, w_ple_gate, w_ple, norm_final):
    B, S, _ = x.shape
    h = x
    for l in range(DEPTH_2):
        a = rmsnorm(h, norm_mix[l])
        proj = a @ w_in[l]
        aq, ak, av, gq, gk, gv, gr, z_f, z_b, g_att, g_gla = split_columns(proj)
        aq = partial_rope(aq.reshape(B, S, ATT_HEADS, ATT_HEAD_DIM), positions)
        ak = partial_rope(ak.reshape(B, S, ATT_KV_HEADS, ATT_HEAD_DIM), positions)
        av = av.reshape(B, S, ATT_KV_HEADS, ATT_HEAD_DIM)
        y_att = windowed_gqa(aq, ak, av, attn_sink[l]) @ w_branch_attn[l]
        y_gla = gla_branch(gq, gk, gv, gr, z_f, z_b,
                           gla_gate_up_fwd[l], gla_gate_bias_fwd[l],
                           gla_gate_up_bwd[l], gla_gate_bias_bwd[l], gla_norm[l]) @ w_branch_gla[l]
        merged = jax.nn.sigmoid(g_att) * y_att + jax.nn.sigmoid(g_gla) * y_gla
        h = h + merged @ w_out[l]
        h = h + expert_choice_ffn(rmsnorm(h, norm_ffn[l]), w_router[l],
                                  w_exp_gate[l], w_exp_up[l], w_exp_down[l])
        ple_gate = jax.nn.sigmoid(rmsnorm(h, norm_ple[l]) @ w_ple_gate[l])
        h = h + ple_gate * (p[l] @ w_ple[l])
    return rmsnorm(h, norm_final)


def setup_inputs(seed=0):
    out = dict(first_inputs(seed))
    for name, value in second_inputs(seed + 1).items():
        if name != "x":
            out[name + "_2"] = value
    return out


def reference(
    x, meta_tokens, w_in, conv_w, conv_b, conv_ln_g, conv_ln_b, w_out, post_ln_g, post_ln_b,
    p_2, positions_2, norm_mix_2, w_in_2, gla_gate_up_fwd_2, gla_gate_bias_fwd_2,
    gla_gate_up_bwd_2, gla_gate_bias_bwd_2, attn_sink_2, gla_norm_2, w_branch_attn_2,
    w_branch_gla_2, w_out_2, norm_ffn_2, w_router_2, w_exp_gate_2, w_exp_up_2, w_exp_down_2,
    norm_ple_2, w_ple_gate_2, w_ple_2, norm_final_2,
):
    x = first_block(
        x, meta_tokens, w_in, conv_w, conv_b, conv_ln_g, conv_ln_b, w_out, post_ln_g, post_ln_b,
    )
    return second_block(
        x, p_2, positions_2, norm_mix_2, w_in_2, gla_gate_up_fwd_2, gla_gate_bias_fwd_2,
        gla_gate_up_bwd_2, gla_gate_bias_bwd_2, attn_sink_2, gla_norm_2, w_branch_attn_2,
        w_branch_gla_2, w_out_2, norm_ffn_2, w_router_2, w_exp_gate_2, w_exp_up_2, w_exp_down_2,
        norm_ple_2, w_ple_gate_2, w_ple_2, norm_final_2,
    )


_drawn_inputs = setup_inputs


def setup_inputs(seed=0):
    import zlib

    import numpy as np

    out = dict(_drawn_inputs(seed))
    spreads = {}
    factors = {'conv_b': 8.0,
     'conv_ln_g': 8.0,
     'conv_ln_b': 8.0,
     'post_ln_g': 2.948,
     'post_ln_b': 2.848,
     'attn_sink_2': 64.0,
     'norm_ple_2': 10.952,
     'gla_gate_up_fwd_2': 4.27,
     'gla_gate_bias_fwd_2': 2.753,
     'gla_gate_up_bwd_2': 5.565,
     'gla_gate_bias_bwd_2': 2.76,
     'gla_norm_2': 4.999,
     'norm_ffn_2': 3.688}
    for name, (base, spread) in spreads.items():
        noise = np.random.default_rng([zlib.crc32(name.encode()), seed]).standard_normal(out[name].shape)
        drawn = base * np.exp(spread * noise) if base else spread * noise
        out[name] = __import__('jax').numpy.asarray(drawn.astype(out[name].dtype))
    for name, factor in factors.items():
        out[name] = (out[name] * factor).astype(out[name].dtype)
    return out
```

```python
import numpy as np
import concourse.bass as bass
from concourse import mybir
from contextlib import ExitStack

P = 128
D_MODEL, SEQ, DEPTH, N_META = 1024, 512, 2, 16
L = SEQ + N_META
HALF = L // 2
KC = D_MODEL // P
D_CONV, TAPS = 512, 31
HEADS, HEAD_DIM = 8, 64
TOPK = min(256, L // 4)
DUMMIES = -TOPK % 8
ROUNDS = (TOPK + DUMMIES) // 8
ALPHA = (2.0 * DEPTH) ** 0.25
LN_EPS, RMS_EPS = 1e-5, 1e-6
COL_A, COL_G, COL_ZC, COL_Q, COL_K, COL_V, COL_ZA, COL_QI, COL_KI, COL_WI = (
    0, 512, 1024, 1536, 2048, 2560, 3072, 3584, 4096, 4160)
DUMMY_SCORE, FUTURE_SCORE, TAKEN = 3.0e38, -3.0e38, float(np.float32(-3.3e38))
HIDDEN = -1.0e30
XT = SEQ // P
TILES = XT + 1
WCOLS = 256
SLOTS = 5
NC = 15


def constants():
    i = np.arange(P)
    c = np.zeros((NC, P, P), np.float32)
    c[0] = np.eye(P)
    c[1] = 1.0
    c[2] = 1.0 / D_CONV
    for base in (0, 64):
        for d in range(32):
            c[3][base + d + 32, base + d] = -1.0
            c[3][base + d, base + d + 32] = 1.0
        for d in range(8):
            c[4][base + d + 8, base + d] = -1.0
            c[4][base + d, base + d + 8] = 1.0
    later = i[None, :] > i[:, None]
    c[5] = np.where(later, FUTURE_SCORE, 0.0)
    c[6] = np.where(later, HIDDEN, 0.0)
    same = (i[:, None] // 64) == (i[None, :] // 64)
    c[7] = (same & (i[:, None] <= i[None, :])) / 16.0
    c[8] = (same & (i[:, None] >= i[None, :])) / 16.0
    c[9] = (same & (i[:, None] > i[None, :]))
    c[10] = np.where(i[None, :] >= i[:, None], 0.0, HIDDEN)
    c[12] = np.where(i[None, :] <= i[:, None], 0.0, HIDDEN)
    c[13] = (i[:, None] <= i[None, :])
    c[14][:, 0:64] = i[None, 0:64]
    inv2 = (np.float32(500000.0) ** (-np.arange(0, 16, 2, dtype=np.float32) / np.float32(16))).astype(np.float32)
    for base in (0, 64):
        c[14][base:base + 16, 64] = np.tile(inv2, 2)
    c[14][:, 65] = np.pi / 2
    c[14][[16, 48], 66] = 1.0
    inv = (np.float32(10000.0) ** (-np.arange(0, 64, 2, dtype=np.float32) / np.float32(64))).astype(np.float32)
    ang = np.arange(L, dtype=np.float32)[None, :] * inv[:, None]
    rope = np.stack([np.tile(np.cos(ang), (4, 1)), np.tile(np.sin(ang), (4, 1))], 1).astype(np.float32)
    return np.ascontiguousarray(c.transpose(1, 0, 2)), np.ascontiguousarray(rope)


G_HEADS, G_DK, G_DV, CHUNK = 4, 128, 256, 64
EXPERTS, CAP = 16, 2 * SEQ // 16
PAIRS = EXPERTS // 2
QUARTERS = D_MODEL // WCOLS
COL2 = dict(aq=0, gq=768, gk=1280, gv=1792, gr=2816, ga=3872, gg=4896)
PLE = 256
FAR = 1.5 * 2.0 ** 23
TURN = (6.28125, 0.0019350051879882812, 3.0199159819e-7)
TAKEN_AFF = -1.0


class Steps:

    def __init__(self, base=0):
        self.base, self.n = base, 0

    def one(self):
        self.n += 1
        return 1

    def now(self):
        return self.base + self.n

    def at(self, n):
        return self.base + n


def hybrid_kernel(nc, x, meta, w_in, w_misc, conv_p, w_out, post_p, cst_d, rope_d, B, out):
    F32, U32, I32 = mybir.dt.float32, mybir.dt.uint32, mybir.dt.int32
    ALU, ACT, AX = mybir.AluOpType, mybir.ActivationFunctionType, mybir.AxisListType

    w_in_v = w_in.rearrange("l (k p) n -> l p k n", p=P)
    w_out_v = w_out.rearrange("l (k p) n -> l p k n", p=P)
    w_misc_v = w_misc.rearrange("l (k p) n -> l p k n", p=P)

    top = ExitStack()
    with top:
        def pool_of(stack):
            return lambda name, shape: stack.enter_context(nc.sbuf_tensor(name, shape, F32))

        def sem(name):
            return top.enter_context(nc.semaphore(name))

        keep = pool_of(top)
        H = keep("H", [P, TILES, D_MODEL])
        cst = keep("cst", [P, NC, P])
        ring = keep("ring", [P, SLOTS, KC, WCOLS])
        small = keep("small", [P, 512])
        few = keep("few", [P, 640])
        gains = keep("gains", [P, 4, KC])
        router = keep("router", [P, KC, EXPERTS])
        sink = keep("sink", [P, 2, HEADS])
        ident, ones, mean_w, rot = cst[:, 0, :], cst[:, 1, :], cst[:, 2, :], cst[:, 3, :]
        future_score, future_hidden = cst[:, 5, :], cst[:, 6, :]

        first = ExitStack()
        buf = pool_of(first)
        hT = buf("hT", [P, KC, L])
        rope = buf("rope", [P, 2, L])
        post = buf("post", [P, 2, D_MODEL])
        misc = buf("misc", [P, KC, 136])
        convp = buf("convp", [P, 4, TAPS + 3])
        qT = buf("qT", [P, 4, L])
        kT = buf("kT", [P, 4, L])
        zaT = buf("zaT", [P, 4, L])
        qiT = zaT
        kiT = buf("kiT", [P, L])
        V = buf("V", [P, TILES, 512])
        zcT = buf("zcT", [P, 4, L])
        uT = buf("uT", [P, 4, TAPS - 1 + L])
        yT = buf("yT", [P, 2 * 4, L])
        KEYS = [N_META + P * (t + 1) for t in range(XT)] + [N_META]
        score = [buf(f"score{t}", [P, DUMMIES + KEYS[t]]) for t in range(XT)]
        pr = buf("pr", [P, 4, L])
        prT = buf("prT", [P, 2, 4, P])
        prR = buf("prR", [N_META, 2, P])
        raw = buf("raw", [P, 2, L])
        first.close()


        second = ExitStack()
        buf = pool_of(second)
        aT = buf("aT", [P, KC, SEQ])
        attT = buf("attT", [P, 4, SEQ])
        gqk = buf("gqk", [P, 2, 4, SEQ])
        GV = buf("GV", [P, XT, D_MODEL])
        zT = buf("zT", [64, SEQ])
        up = buf("up", [64, 512])
        scope = ExitStack()
        buf = pool_of(scope)
        xn = buf("xn", [P, 2, D_MODEL])
        aqT = buf("aqT", [P, 4, SEQ])
        akT = buf("akT", [P, 2, SEQ])
        av = buf("av", [P, XT, P])
        pr2 = buf("pr2", [P, 4, 3 * P])
        pr2T = buf("pr2T", [P, 2, 3 * P])
        rope2 = buf("rope2", [P, 2, SEQ])
        raw2 = buf("raw2", [P, 2, SEQ])
        pos = buf("pos", [P, SEQ])
        angle = buf("angle", [P, SEQ])
        turns = buf("turns", [P, SEQ])
        scope.close()
        scope = ExitStack()
        buf = pool_of(scope)
        qB = buf("qB", [P, 4, SEQ])
        kE = buf("kE", [P, 2, XT, 512])
        AT = buf("AT", [P, XT, 4, P])
        O = buf("O", [P, XT, D_MODEL])
        S = buf("S", [P, 3, G_HEADS, G_DV])
        decay = [buf(n, [P, 4, P]) for n in ("cum", "exp_b", "k_t", "k_e")]
        gate = buf("gate", [P, 2, 512])
        scope.close()
        scope = ExitStack()
        buf = pool_of(scope)
        side = buf("side", [P, 6, SEQ])
        scope.close()
        second.close()
        OT = gqk[:, :, :, :].rearrange("p a c n -> p (a c) n")
        mT = GV[:, :, :].rearrange("p t (a n) -> p (t a) n", a=2)

        third = ExitStack()
        buf = pool_of(third)
        xg = buf("xg", [P, PAIRS, KC, P])
        GT = buf("GT", [P, PAIRS, SEQ])
        xe = buf("xe", [P, 2, KC, CAP])
        hid = buf("hid", [P, 2, 512])
        hidT = buf("hidT", [P, 4, P])
        final_g = buf("final_g", [P, D_MODEL])
        pT = buf("pT", [P, PLE // P, SEQ])
        scope = ExitStack()
        ring_more = scope.enter_context(nc.sbuf_tensor("ring_more", [P, 12 - SLOTS, KC, WCOLS], F32))
        scope.close()
        scope = ExitStack()
        buf = pool_of(scope)
        aT2 = buf("aT2", [P, KC, SEQ])
        XN = buf("XN", [P, XT, D_MODEL])
        sel = buf("sel", [P, XT, EXPERTS * CAP])
        selw = buf("selw", [P, 2, EXPERTS * CAP])
        scope.close()
        scope = ExitStack()
        buf = pool_of(scope)
        aT3 = buf("aT3", [P, KC, SEQ])
        xn3 = buf("xn3", [P, 2, D_MODEL])
        emb = buf("emb", [P, 2, WCOLS])
        outb = buf("outb", [P, 2, D_MODEL])
        scope.close()
        third.close()

        def few_at(a, n):
            return few[:, a:a + n]

        norm_sq, norm_std, norm_inv = few_at(0, 20), few_at(20, 20), few_at(40, 8)
        neg_max2, sum2, sink2, inv2, den2 = (few_at(64 + 32 * i, 32) for i in range(5))
        o_sq, o_std, o_inv = few_at(224, 16), few_at(240, 16), few_at(256, 16)
        dec = few_at(272, 64).rearrange("p (d t h c) -> p d t h c", d=2, t=XT, h=G_HEADS)
        soft = few_at(336, 12)
        logit = few_at(348, 64).rearrange("p (t e) -> p t e", t=XT)
        aff = few_at(412, 64).rearrange("p (t e) -> p t e", t=XT)
        mark = few_at(476, 64).rearrange("p (t e) -> p t e", t=XT)
        rank = few_at(540, 64).rearrange("p (t e) -> p t e", t=XT)
        max8 = few_at(604, 8)
        affT = hid[0:EXPERTS, 0, :]
        takenT = hid[0:EXPERTS, 1, :]
        rot2 = cst[:, 4, :]
        window = cst[:, 10:13, :].rearrange("p a n -> p (a n)")

        ps = top.enter_context(nc.psum_tensor("ps", [P, 8, 512], F32))

        wi = small[:, 0:32]
        top8 = small[:, 32:64]
        neg_max = small[:, 64:104]
        row_sum = small[:, 104:144]
        row_inv = small[:, 144:184]
        stats = small[:, 184:196]
        mean_var = small[:, 196:206]
        ln_std_v = small[:, 206:211]
        ln_inv = small[:, 211:216]
        eps_ln = small[:, 216:217]
        eps_rms = small[:, 217:218]

        def rows_of(t):
            return (P, N_META + P * t) if t < XT else (N_META, 0)

        def halves(b):
            return b.rearrange("p (a n) -> p a n", a=2)

        def pair(p):
            return ps[:, 2 * p:2 * p + 2, 0:HALF]

        def span(b, banks, rows, n):
            if n <= 512:
                return b[0:rows, 0:n], ps[0:rows, banks, 0:n]
            return halves(b[0:rows, 0:n]), ps[0:rows, banks:banks + 2, 0:n // 2]

        consts_in = sem("consts_in")
        h_in = sem("h_in")
        consts_set = sem("consts_set")
        params_in = sem("params_in")
        slot_in = [sem(f"slot_in{s}") for s in range(SLOTS)]
        turned = sem("turned")
        turned_act = sem("turned_act")
        turned_dve = sem("turned_dve")
        proj_done = sem("proj_done")
        proj_out = sem("proj_out")
        rot_done = sem("rot_done")
        raw_used = sem("raw_used")
        idx_done = sem("idx_done")
        idx_relu = sem("idx_relu")
        idx_added = sem("idx_added")
        gated = sem("gated")
        conv_done = sem("conv_done")
        cn_mean = sem("cn_mean")
        cn_centred = sem("cn_centred")
        cn_square = sem("cn_square")
        cn_var = sem("cn_var")
        cn_std = sem("cn_std")
        cn_scaled = sem("cn_scaled")
        cn_silu = sem("cn_silu")
        conv_y = sem("conv_y")
        at_score = sem("at_score")
        at_masked = sem("at_masked")
        at_exp = sem("at_exp")
        at_prob = sem("at_prob")
        at_turned = sem("at_turned")
        at_full = sem("at_full")
        at_rest = sem("at_rest")
        at_value = sem("at_value")
        attn_y = sem("attn_y")
        wo_done = sem("wo_done")
        wo_added = sem("wo_added")
        ln_var = sem("ln_var")
        ln_std = sem("ln_std")
        h_done = sem("h_done")
        dve_step = sem("dve_step")
        pool_step = sem("pool_step")
        stored = [sem(f"stored{i}") for i in range(2)]

        ITEMS = ([("ki", 0)] + [("qi", c) for c in range(4)] + [("wi", 0)] + [("a", c) for c in range(4)]
                 + [("g", c) for c in range(4)] + [("q", c) for c in range(4)] + [("k", c) for c in range(4)]
                 + [("v", b) for b in range(TILES)] + [("zc", c) for c in range(4)] + [("za", c) for c in range(4)])
        NI = len(ITEMS)
        ITEM = {item: n for n, item in enumerate(ITEMS)}
        IDX_AFTER = ITEM[("a", 3)]
        GROUPS = [(COL, h) for COL in ("qi", "a", "g", "q", "k", "v", "zc", "za") for h in range(2)]
        NG = len(GROUPS) + D_MODEL // WCOLS
        COLS = dict(qi=COL_QI, a=COL_A, g=COL_G, q=COL_Q, k=COL_K, v=COL_V, zc=COL_ZC, za=COL_ZA)
        GROUP_END = [ITEM[(k, TILES - 1 if k == "v" else 2 * h + 1)] + 1 for k, h in GROUPS]
        ROPED = [n for n, (k, _) in enumerate(ITEMS) if k in ("ki", "qi", "q", "k")]
        RAW = [n for n, (k, _) in enumerate(ITEMS) if k in ("ki", "qi", "g", "q", "k")]
        NROT, NRAW, NIDX, NATT = len(ROPED), len(RAW), XT * HEADS, TILES * HEADS

        def group_of(item):
            kind, c = ITEMS[item]
            return GROUPS.index((kind, c // 2))

        def att(j):
            t, h = divmod(j, HEADS)
            n, q0 = rows_of(t)
            return t, h, n, q0, KEYS[t], KEYS[t] // P

        passed = {e: sem(f"passed_{e}") for e in ("sp", "pe", "act", "pool", "dve")}

        def settle(engine, name):
            engine.sem_inc(passed[name], 1)


        second_in = sem("second_in")
        third_in = sem("third_in")
        more_in = [sem(f"more_in{s}") for s in range(12 - SLOTS)]
        nq_done = sem("nq_done")
        ns_done = sem("ns_done")
        xn_done = sem("xn_done")
        nt_done = sem("nt_done")
        nt_out = sem("nt_out")
        rt_arg = sem("rt_arg")
        rt_sin = sem("rt_sin")
        z_ones = sem("z_ones")
        p2_done = sem("p2_done")
        p2_out = sem("p2_out")
        rot2_done = sem("rot2_done")
        raw2_used = sem("raw2_used")
        w_score = sem("w_score")
        w_masked = sem("w_masked")
        w_exp = sem("w_exp")
        w_sink = sem("w_sink")
        w_prob = sem("w_prob")
        w_turned = sem("w_turned")
        w_out_t = sem("w_out_t")
        w_value = sem("w_value")
        w_att = sem("w_att")
        gz_done = sem("gz_done")
        gl_log = sem("gl_log")
        gl_set = sem("gl_set")
        gl_cum = sem("gl_cum")
        gl_exp = sem("gl_exp")
        gl_rest = sem("gl_rest")
        gl_rexp = sem("gl_rexp")
        gl_qk = sem("gl_qk")
        gl_att = sem("gl_att")
        gl_mask = sem("gl_mask")
        gl_turn = sem("gl_turn")
        gl_kout = sem("gl_kout")
        gl_zero = sem("gl_zero")
        kv_done = sem("kv_done")
        st_done = sem("st_done")
        o_done = sem("o_done")
        o_out = sem("o_out")
        o_sqd = sem("o_sqd")
        o_stdd = sem("o_stdd")
        gr_done = sem("gr_done")
        gr_silu = sem("gr_silu")
        gr_out = sem("gr_out")
        mg_done = sem("mg_done")
        mg_sig = sem("mg_sig")
        mg_out = sem("mg_out")
        wo2_done = sem("wo2_done")
        wo2_out = sem("wo2_out")
        rl_done = sem("rl_done")
        rl_sub = sem("rl_sub")
        rl_exp = sem("rl_exp")
        aff_done = sem("aff_done")
        affT_done = sem("affT_done")
        mark_done = sem("mark_done")
        markT_done = sem("markT_done")
        mk_done = sem("mk_done")
        rank_done = sem("rank_done")
        sel_done = sem("sel_done")
        xg_done = sem("xg_done")
        xg_out = sem("xg_out")
        selw_done = sem("selw_done")
        gt_done = sem("gt_done")
        gt_out = sem("gt_out")
        xe_set = sem("xe_set")
        e_gate = sem("e_gate")
        e_up = sem("e_up")
        e_silu = sem("e_silu")
        e_hid = sem("e_hid")
        e_turn = sem("e_turn")
        e_hidT = sem("e_hidT")
        e_down = sem("e_down")
        e_y = sem("e_y")
        e_y2 = sem("e_y2")
        cb_done = sem("cb_done")
        cb_out = sem("cb_out")
        pl_done = sem("pl_done")
        pl_sig = sem("pl_sig")
        pl_out = sem("pl_out")
        y_set = sem("y_set")
        act_step = sem("act_step")

        ITEMS2 = ([("ak", c) for c in range(2)] + [("av", 0), ("z", 0)] + [("aq", c) for c in range(4)]
                  + [("gq", c) for c in range(4)] + [("gk", c) for c in range(4)]
                  + [("gv", c) for c in range(2 * XT)])
        NI2 = len(ITEMS2)
        AT2 = {item: n for n, item in enumerate(ITEMS2)}
        ROPED2 = [AT2[("ak", 0)], AT2[("ak", 1)]] + [AT2[("aq", c)] for c in range(4)]
        BEFORE = DEPTH * (NG // SLOTS)
        D_IN2 = COL2["gg"] + D_MODEL
        GROUPS2 = ([("m0", 0), ("m1", 0)] + [(g, c) for g in ("aq", "gq", "gk") for c in range(2)]
                   + [("gv", c) for c in range(4)] + [("gr", c) for c in range(4)]
                   + [(g, c) for c in range(4) for g in ("ga", "ba", "gg", "bg")]
                   + [("wo", c) for c in range(4)])
        NG2 = len(GROUPS2)
        G2 = {g: n for n, g in enumerate(GROUPS2)}

        def last_use(g):
            kind, c = g
            if kind in ("m0", "m1"):
                return p2_done, AT2[("ak", 1) if kind == "m0" else ("z", 0)] + 1
            if kind in ("aq", "gq", "gk"):
                return p2_done, AT2[(kind, 2 * c + 1)] + 1
            if kind == "gv":
                return p2_done, AT2[("gv", XT * (c // 2) + XT - 1)] + 1
            if kind == "gr":
                return gr_done, 2 * c + 2
            if kind == "wo":
                return wo2_done, 4 * XT
            return mg_done, 8 * c + 4 + ("ga", "ba", "gg", "bg").index(kind) + 1

        def win(j):
            t, h = divmod(j, HEADS)
            k0 = max(t - 1, 0)
            return t, h, k0, min(t + 1, XT - 1) - k0 + 1

        NW = XT * HEADS
        TD = [(t, d) for t in range(XT) for d in (1, 0)]
        SCAN = {1: [(t, c) for t in reversed(range(XT)) for c in (1, 0)], 0: [(t, c) for t in range(XT) for c in (0, 1)]}

        def eslot(i):
            return ring[:, i, :, :] if i < SLOTS else ring_more[:, i - SLOTS, :, :]

        def eslot_in(i):
            return slot_in[i] if i < SLOTS else more_in[i - SLOTS]

        LOADED = [BEFORE + len(range(s, NG2, SLOTS)) for s in range(SLOTS)] + [0] * (12 - SLOTS)

        block = top.enter_context(nc.Block())

        @block.sync
        def _(sp):
            sp.dma_start(cst[:, :, :], cst_d).then_inc(consts_in, 16)
            sp.dma_start(rope[:, :, :], rope_d).then_inc(consts_in, 16)
            sp.dma_start(H[:, 0:XT, :], x.rearrange("(t p) d -> p t d", p=P)).then_inc(h_in, 16)
            sp.dma_start(H[0:N_META, XT, :], meta).then_inc(h_in, 16)
            sp.dma_start(gains[:, :, :], B["gains"]).then_inc(consts_in, 16)
            sp.dma_start(router[:, :, :], B["router"]).then_inc(consts_in, 16)
            sp.dma_start(sink[:, 0, :], B["sink"].partition_broadcast(P)).then_inc(consts_in, 16)

            with sp.Fori(0, DEPTH) as l:
                sp.wait_ge(h_done, l * TILES)
                settle(sp, "sp")
                sp.dma_start(misc[:, :, :], w_misc_v[l]).then_inc(params_in, 16)
                sp.dma_start(convp[:, :, :], conv_p[l]).then_inc(params_in, 16)
                sp.dma_start(post[:, :, :], post_p[l]).then_inc(params_in, 16)
                for n in range(NG):
                    if n == 0:
                        sp.wait_ge(proj_done, l * NI)
                    elif n < SLOTS:
                        sp.wait_ge(wo_done, l * TILES * 4)
                    else:
                        sp.wait_ge(proj_done, l * NI + GROUP_END[n - SLOTS])
                    if n < len(GROUPS):
                        kind, h = GROUPS[n]
                        src = w_in_v[l, :, :, COLS[kind] + WCOLS * h:COLS[kind] + WCOLS * (h + 1)]
                    else:
                        m = n - len(GROUPS)
                        src = w_out_v[l, :, :, WCOLS * m:WCOLS * (m + 1)]
                    settle(sp, "sp")
                    sp.dma_start(ring[:, n % SLOTS, :, :], src).then_inc(slot_in[n % SLOTS], 16)
            sp.wait_ge(h_done, DEPTH * TILES)
            sp.dma_start(up[:, :], B["up"]).then_inc(second_in, 16)
            sp.dma_start(pos[:, :].bitcast(I32), B["positions"]).then_inc(second_in, 16)
            for n, (kind, c) in enumerate(GROUPS2):
                if n == 0:
                    sp.wait_ge(proj_done, DEPTH * NI)
                elif n < SLOTS:
                    sp.wait_ge(wo_done, DEPTH * TILES * 4)
                else:
                    sp.wait_ge(*last_use(GROUPS2[n - SLOTS]))
                slot = ring[:, n % SLOTS, :, :]
                if kind in ("m0", "m1"):
                    src = B["w_misc"][:, :, 0:WCOLS] if kind == "m0" else B["w_misc"][:, :, WCOLS:WCOLS + 192]
                    slot = slot if kind == "m0" else slot[:, :, 0:192]
                elif kind == "ba":
                    slot, src = slot[:, 0:4, :], B["w_ba"][:, :, WCOLS * c:WCOLS * (c + 1)]
                elif kind in ("bg", "wo"):
                    src = B["w_" + kind][:, :, WCOLS * c:WCOLS * (c + 1)]
                else:
                    src = B["w_in"][:, :, COL2[kind] + WCOLS * c:COL2[kind] + WCOLS * (c + 1)]
                sp.dma_start(slot, src).then_inc(slot_in[n % SLOTS], 16)
            with sp.Fori(0, EXPERTS) as e:
                for i in range(12):
                    sp.wait_ge((e_gate, e_up, e_down)[i // 4], e + 1)
                    settle(sp, "sp")
                    sp.dma_start(eslot(i), B["w_exp"][i // 4][e, :, :, WCOLS * (i % 4):WCOLS * (i % 4 + 1)])\
                        .then_inc(eslot_in(i), 16)
            sp.wait_ge(xg_done, 2 * KC)
            sp.dma_start(final_g[:, :], B["final"].partition_broadcast(P)).then_inc(third_in, 16)
            sp.dma_start(pT[:, :, :], B["pT"]).then_inc(third_in, 16)
            for c in range(4):
                sp.wait_ge(e_gate, EXPERTS + 1)
                sp.dma_start(ring[:, c, :, :], B["w_pg"][:, :, WCOLS * c:WCOLS * (c + 1)]).then_inc(slot_in[c], 16)
            sp.wait_ge(e_up, EXPERTS + 1)
            sp.dma_start(ring[:, 4, :, :].rearrange("p (k a) n -> p k (a n)", k=PLE // P), B["w_p"])\
                .then_inc(slot_in[4], 16)
            for t in range(XT):
                sp.wait_ge(y_set, t + 1)
                sp.dma_start(out[P * t:P * (t + 1), :], outb[:, t % 2, :]).then_inc(stored[t % 2], 16)
            sp.wait_ge(stored[0], 16 * (XT // 2))
            sp.wait_ge(stored[1], 16 * (XT // 2))

        @block.tensor
        def _(pe):
            mm = nc.tensor.matmul

            def slot_ready(l, n):
                pe.wait_ge(slot_in[n % SLOTS], 16 * (l * (NG // SLOTS) + n // SLOTS + 1))

            def item(l, n):
                kind, c = ITEMS[n]
                p = n % 2
                pe.wait_ge(proj_out, l * NI + max(n - 1, 0))
                if kind not in ("ki", "wi") and (c % 2 == 0 or kind == "v") and not (kind == "v" and c > 0):
                    slot_ready(l, group_of(n))
                    if kind == "v":
                        slot_ready(l, group_of(n) + 1)
                if kind == "wi":
                    for t in range(XT):
                        q0 = rows_of(t)[1]
                        for k in range(KC):
                            last = mm(ps[:, 2 * p, 8 * t:8 * t + 8], hT[:, k, q0:q0 + P], misc[:, k, 128:136],
                                      start=(k == 0), stop=(k == KC - 1))
                elif kind == "v":
                    rows = min(P, L - P * c)
                    g = GROUPS.index(("v", 0))
                    for h in range(2):
                        for k in range(KC):
                            last = mm(ps[0:rows, 2 * p, WCOLS * h:WCOLS * (h + 1)], hT[:, k, P * c:P * c + rows],
                                      ring[:, (g + h) % SLOTS, k, :], start=(k == 0), stop=(k == KC - 1))
                else:
                    for k in range(KC):
                        if kind == "ki":
                            w = misc[:, k, 0:P]
                        else:
                            w = ring[:, group_of(n) % SLOTS, k, P * (c % 2):P * (c % 2 + 1)]
                        for a in range(2):
                            last = mm(ps[:, 2 * p + a, 0:HALF], w, hT[:, k, HALF * a:HALF * (a + 1)],
                                      start=(k == 0), stop=(k == KC - 1))
                last.then_inc(proj_done, 1)

            def rotate(l, r):
                n = ROPED[r]
                u = RAW.index(n)
                pe.wait_ge(proj_out, l * NI + n + 1)
                if r >= 2:
                    pe.wait_ge(raw_used, l * NRAW + RAW.index(ROPED[r - 2]) + 1)
                if r == 5:
                    pe.wait_ge(idx_relu, l * NIDX + NIDX)
                for a in range(2):
                    last = mm(ps[:, 4 + 2 * (r % 2) + a, 0:HALF], rot, raw[:, u % 2, HALF * a:HALF * (a + 1)],
                              start=True, stop=True)
                last.then_inc(rot_done, 1)

            def index_scores(l):
                pe.wait_ge(raw_used, l * NRAW + 5)
                for j in range(NIDX):
                    t, h = divmod(j, HEADS)
                    n, q0 = rows_of(t)
                    if j >= 2:
                        pe.wait_ge(idx_relu, l * NIDX + j - 1)
                    b0 = 64 * (h % 2)
                    for a in range(1 if KEYS[t] <= 512 else 2):
                        w = min(KEYS[t], 512) if KEYS[t] <= 512 else HALF
                        last = mm(ps[:, 4 + 2 * (j % 2) + a, 0:w], qiT[b0:b0 + 64, h // 2, q0:q0 + n],
                                  kiT[b0:b0 + 64, a * w:(a + 1) * w], start=True, stop=True)
                    last.then_inc(idx_done, 1)

            def at_scores(l, j):
                t, h, n, q0, keys, _ = att(j)
                if j >= 2:
                    pe.wait_ge(at_masked, l * NATT + j - 1)
                else:
                    pe.wait_ge(raw_used, l * NRAW + NRAW)
                settle(pe, "pe")
                b0 = 64 * (h % 2)
                for a in range(1 if keys <= 512 else 2):
                    w = keys if keys <= 512 else HALF
                    last = mm(ps[0:n, 4 + 2 * (j % 2) + a, 0:w], qT[b0:b0 + 64, h // 2, q0:q0 + n],
                              kT[b0:b0 + 64, h // 2, a * w:(a + 1) * w], start=True, stop=True)
                last.then_inc(at_score, 1)

            def at_turn(l, j):
                t, h, n, q0, keys, full = att(j)
                pe.wait_ge(at_prob, l * NATT + j + 1)
                if j == 0:
                    pe.wait_ge(proj_out, l * NI + NI)
                if 2 <= j < XT * HEADS:
                    pe.wait_ge(at_full, l * XT * HEADS + j - 1)
                if j >= 1:
                    pe.wait_ge(at_rest, l * NATT + j)
                settle(pe, "pe")
                for b in range(full):
                    nc.tensor.transpose(ps[:, j % 2, P * b:P * b + n], pr[0:n, j % 4, P * b:P * (b + 1)],
                                        ident[0:n, 0:n])
                nc.tensor.transpose(ps[0:N_META, 2, P * (j % 4):P * (j % 4) + n],
                                    pr[0:n, j % 4, P * full:P * full + N_META], ident[0:n, 0:n]).then_inc(at_turned, 1)

            def at_values(l, j):
                t, h, n, q0, keys, full = att(j)
                if full:
                    pe.wait_ge(at_full, l * XT * HEADS + j + 1)
                pe.wait_ge(at_rest, l * NATT + j + 1)
                if h == 0 and t > 0:
                    pe.wait_ge(attn_y, l * TILES + t)
                b0 = 64 * (h % 2)
                o = ps[b0:b0 + 64, 3, P * (h // 2):P * (h // 2) + n]
                for b in range(full):
                    mm(o, V[:, b, 64 * h:64 * (h + 1)], prT[:, j % 2, b, 0:n], start=(b == 0), stop=False)
                mm(o, V[0:N_META, full, 64 * h:64 * (h + 1)], prR[:, j % 2, 0:n], start=(full == 0),
                   stop=True).then_inc(at_value, 1)

            pe.wait_ge(consts_in, 80)
            pe.wait_ge(h_in, 32)
            with pe.Fori(0, DEPTH) as l:
                pe.wait_ge(h_done, l * TILES)
                for t in range(TILES):
                    rows, _ = rows_of(t)
                    for hf, read in enumerate((turned_act, turned_dve)):
                        if t >= 2:
                            pe.wait_ge(read, l * TILES + t - 1)
                            settle(pe, "pe")
                        for c in range(4):
                            last = nc.tensor.transpose(
                                ps[:, 4 + 2 * (t % 2) + hf, P * c:P * c + rows],
                                H[0:rows, t, P * (4 * hf + c):P * (4 * hf + c + 1)], ident[0:rows, 0:rows])
                        last.then_inc(turned, 1)
                pe.wait_ge(turned_act, l * TILES + TILES)
                pe.wait_ge(turned_dve, l * TILES + TILES)
                pe.wait_ge(params_in, 48 * (l + 1))
                r = 0
                for n in range(NI):
                    item(l, n)
                    if n >= 1 and n - 1 in ROPED:
                        rotate(l, r)
                        r += 1
                    if n == IDX_AFTER:
                        index_scores(l)
                for j in range(NATT + 3):
                    if j < NATT:
                        at_scores(l, j)
                    if 2 <= j < NATT + 2:
                        at_turn(l, j - 2)
                    if j >= 3:
                        at_values(l, j - 3)
                pe.wait_ge(conv_done, 4 * l + 4)
                pe.wait_ge(attn_y, l * TILES + TILES)
                for a in range(2):
                    for c in range(4):
                        last = mm(ps[:, a, 0:HALF], mean_w, yT[:, c, HALF * a:HALF * (a + 1)],
                                  start=(c == 0), stop=(c == 3))
                last.then_inc(cn_mean, 1)
                for c in range(4):
                    pe.wait_ge(cn_square, 4 * l + c + 1)
                    for a in range(2):
                        last = mm(ps[:, 2 + a, 0:HALF], mean_w, pr[:, c, HALF * a:HALF * (a + 1)],
                                  start=(c == 0), stop=(c == 3))
                last.then_inc(cn_var, 1)
                pe.wait_ge(conv_y, 4 * l + 4)
                for m in range(4):
                    slot_ready(l, len(GROUPS) + m)
                for t in range(TILES):
                    rows, q0 = rows_of(t)
                    for m in range(4):
                        i = 4 * t + m
                        if i >= 4:
                            pe.wait_ge(wo_added, l * 4 * TILES + i - 3)
                        for k in range(KC):
                            last = mm(ps[0:rows, 4 + i % 4, 0:WCOLS], yT[:, k, q0:q0 + rows],
                                      ring[:, (len(GROUPS) + m) % SLOTS, k, :], start=(k == 0), stop=(k == KC - 1))
                        last.then_inc(wo_done, 1)

            T = nc.tensor.transpose

            def slot2(kind, c):
                n = G2[(kind, c)]
                pe.wait_ge(slot_in[n % SLOTS], 16 * (BEFORE + n // SLOTS + 1))
                return ring[:, n % SLOTS, :, :]

            def turn_norm(w, src):
                for t in range(XT):
                    pe.wait_ge(xn_done, XT * w + t + 1)
                    for hf in range(2):
                        i = 2 * t + hf
                        if i >= 4:
                            pe.wait_ge(nt_out, 2 * XT * w + i - 3)
                        for c in range(4):
                            last = T(ps[:, 4 + i % 4, P * c:P * (c + 1)], src(t)[:, P * (4 * hf + c):P * (4 * hf + c + 1)],
                                     ident)
                        last.then_inc(nt_done, 1)
                pe.wait_ge(nt_out, 2 * XT * (w + 1))

            turn_norm(0, lambda t: xn[:, t % 2, :])

            def rotate2(r):
                n = ROPED2[r]
                pe.wait_ge(p2_out, n + 1)
                if r >= 2:
                    pe.wait_ge(raw2_used, r - 1)
                mm(ps[:, 4 + r % 2, :], rot2, raw2[:, r % 2, :], start=True, stop=True).then_inc(rot2_done, 1)

            def item2(n):
                kind, c = ITEMS2[n]
                if n >= 4:
                    pe.wait_ge(p2_out, n - 3)
                o = ps[:, n % 4, :]
                if kind == "ak":
                    w = slot2("m0", 0)[:, :, P * c:P * (c + 1)]
                elif kind in ("av", "z"):
                    w = slot2("m1", 0)
                elif kind != "gv":
                    w = slot2(kind, c // 2)[:, :, P * (c % 2):P * (c % 2 + 1)]
                if kind == "av":
                    for t in range(XT):
                        for k in range(KC):
                            last = mm(o[:, P * t:P * (t + 1)], aT[:, k, P * t:P * (t + 1)], w[:, k, 0:P],
                                      start=(k == 0), stop=(k == KC - 1))
                elif kind == "z":
                    for k in range(KC):
                        last = mm(o[0:64, :], w[:, k, P:P + 64], aT[:, k, :], start=(k == 0), stop=(k == KC - 1))
                elif kind == "gv":
                    half, t = divmod(c, XT)
                    for a in range(2):
                        w = slot2("gv", 2 * half + a)
                        for k in range(KC):
                            last = mm(o[:, WCOLS * a:WCOLS * (a + 1)], aT[:, k, P * t:P * (t + 1)], w[:, k, :],
                                      start=(k == 0), stop=(k == KC - 1))
                else:
                    for k in range(KC):
                        last = mm(o, w[:, k, :], aT[:, k, :], start=(k == 0), stop=(k == KC - 1))
                last.then_inc(p2_done, 1)

            for n in range(NI2):
                item2(n)
                if n - 1 in ROPED2:
                    rotate2(ROPED2.index(n - 1))

            def w_scores(j):
                t, h, k0, cnt = win(j)
                pe.wait_ge(w_masked, j - 1) if j >= 2 else pe.wait_ge(raw2_used, len(ROPED2))
                b0 = 64 * (h % 2)
                mm(ps[:, 4 + j % 2, 0:P * cnt], aqT[b0:b0 + 64, h // 2, P * t:P * (t + 1)],
                   akT[b0:b0 + 64, h // 4, P * k0:P * (k0 + cnt)], start=True, stop=True).then_inc(w_score, 1)

            def w_turn(j):
                t, h, k0, cnt = win(j)
                pe.wait_ge(w_prob, j + 1)
                if j >= 2:
                    pe.wait_ge(w_out_t, j - 1)
                for b in range(cnt):
                    last = T(ps[:, 6 + j % 2, P * b:P * (b + 1)], pr2[:, j % 4, P * b:P * (b + 1)], ident)
                last.then_inc(w_turned, 1)

            def w_values(j):
                t, h, k0, cnt = win(j)
                pe.wait_ge(w_out_t, j + 1)
                if h == 0 and t >= 2:
                    pe.wait_ge(w_att, t - 1)
                if j == 0:
                    pe.wait_ge(p2_out, NI2)
                b0 = 64 * (h % 2)
                for b in range(cnt):
                    last = mm(ps[b0:b0 + 64, t % 2, P * (h // 2):P * (h // 2 + 1)], av[:, k0 + b, 64 * (h // 4):64 * (h // 4 + 1)],
                              pr2T[:, j % 2, P * b:P * (b + 1)], start=(b == 0), stop=(b == cnt - 1))
                last.then_inc(w_value, 1)

            for j in range(NW + 3):
                if j < NW:
                    w_scores(j)
                if 2 <= j < NW + 2:
                    w_turn(j - 2)
                if j >= 3:
                    w_values(j - 3)

            pe.wait_ge(w_att, XT)

            def gate_z(i):
                t, d = TD[i]
                if i >= 2:
                    pe.wait_ge(gl_set, i - 1)
                if i == 0:
                    pe.wait_ge(second_in, 32)
                mm(ps[:, i % 2, :], zT[32 * d:32 * d + 17, P * t:P * (t + 1)], up[32 * d:32 * d + 17, :],
                   start=True, stop=True).then_inc(gz_done, 1)

            def gate_sums(i):
                t, d = TD[i]
                pe.wait_ge(gl_set, i + 1)
                if i >= 2:
                    pe.wait_ge(gl_exp, i - 1)
                for h in range(G_HEADS):
                    last = mm(ps[:, 2 + i % 2, P * h:P * (h + 1)], gate[:, 1, P * h:P * (h + 1)], cst[:, 7 + d, :],
                              start=True, stop=True)
                last.then_inc(gl_cum, 1)

            def gate_scores(i):
                t, d = TD[i]
                q = qB if d else gqk[:, 0, :, :]
                pe.wait_ge(gl_qk, i + 1)
                if i >= 2:
                    pe.wait_ge(gl_mask, i - 1)
                for h in range(G_HEADS):
                    last = mm(ps[:, 4 + i % 2, P * h:P * (h + 1)], decay[2][:, h, :], q[:, h, P * t:P * (t + 1)],
                              start=True, stop=True)
                last.then_inc(gl_att, 1)
                if i >= 2:
                    pe.wait_ge(gl_kout, i - 1)
                for h in range(G_HEADS):
                    last = T(ps[:, 6 + i % 2, P * h:P * (h + 1)], decay[3][:, h, :], ident)
                last.then_inc(gl_turn, 1)

            gate_z(0)
            for i in range(len(TD)):
                gate_sums(i)
                if i + 1 < len(TD):
                    gate_z(i + 1)
                gate_scores(i)

            pe.wait_ge(gl_mask, len(TD))
            pe.wait_ge(gl_kout, len(TD))
            for rnd, d in enumerate((1, 0)):
                q = qB if d else gqk[:, 0, :, :]

                def state(s):
                    t, c = SCAN[d][s]
                    if 7 * rnd + s >= 2:
                        pe.wait_ge(st_done, 7 * rnd + s - 1)
                    b0 = CHUNK * c
                    for h in range(G_HEADS):
                        last = mm(ps[:, 2 * ((7 * rnd + s) % 2) + h // 2, G_DV * (h % 2):G_DV * (h % 2 + 1)],
                                  kE[b0:b0 + CHUNK, d, t, P * h:P * (h + 1)],
                                  GV[b0:b0 + CHUNK, t, G_DV * h:G_DV * (h + 1)], start=True, stop=True)
                    last.then_inc(kv_done, 1)

                state(0)
                state(1)
                for i in range(XT):
                    for s in (2 * i + 2, 2 * i + 3):
                        if s < 7:
                            state(s)
                    t = SCAN[d][2 * i][0]
                    n = XT * rnd + i
                    pe.wait_ge(st_done, 7 * rnd + 2 * i + 1)
                    if n >= 2:
                        pe.wait_ge(o_out, n - 1)
                    for h in range(G_HEADS):
                        o = ps[:, 4 + 2 * (n % 2) + h // 2, G_DV * (h % 2):G_DV * (h % 2 + 1)]
                        if d == 0:
                            mm(o, AT[:, t, h, :], GV[:, t, G_DV * h:G_DV * (h + 1)], start=True, stop=False)
                        for s in (2 * i, 2 * i + 1):
                            c = SCAN[d][s][1]
                            q0 = P * t + CHUNK * c
                            last = mm(o[CHUNK * c:CHUNK * (c + 1), :], q[:, h, q0:q0 + CHUNK], S[:, s % 3, h, :],
                                      start=(d == 1), stop=True)
                    last.then_inc(o_done, 1)

            pe.wait_ge(o_out, 2 * XT)
            turn_norm(1, lambda t: O[:, t, :])
            for c in range(KC):
                w = slot2("gr", c // 2)
                if c >= 4:
                    pe.wait_ge(gr_silu, c - 3)
                for k in range(KC):
                    last = mm(ps[:, c % 4, :], w[:, k, P * (c % 2):P * (c % 2 + 1)], aT[:, k, :],
                              start=(k == 0), stop=(k == KC - 1))
                last.then_inc(gr_done, 1)
            pe.wait_ge(gr_silu, KC)
            pe.wait_ge(gr_out, KC)
            for c in range(KC):
                for m, kind in enumerate(("ga", "ba", "gg", "bg")):
                    if c >= 2:
                        pe.wait_ge(*((mg_sig, 2 * (c - 2) + m // 2 + 1) if m % 2 == 0
                                     else (mg_out, 2 * (c - 2) + m // 2 + 1)))
                    w = slot2(kind, c // 2)
                    src = dict(ga=aT, gg=aT, ba=attT, bg=OT)[kind]
                    nk = 4 if kind == "ba" else KC
                    for k in range(nk):
                        last = mm(ps[:, 4 * (c % 2) + m, :], w[:, k, P * (c % 2):P * (c % 2 + 1)], src[:, k, :],
                                  start=(k == 0), stop=(k == nk - 1))
                    last.then_inc(mg_done, 1)
            pe.wait_ge(mg_out, 2 * KC)
            for c in range(4):
                slot2("wo", c)
            for t in range(XT):
                for m in range(4):
                    i = 4 * t + m
                    if i >= 4:
                        pe.wait_ge(wo2_out, i - 3)
                    w = ring[:, G2[("wo", m)] % SLOTS, :, :]
                    for k in range(KC):
                        last = mm(ps[:, i % 4, 0:WCOLS], mT[:, k, P * t:P * (t + 1)], w[:, k, :],
                                  start=(k == 0), stop=(k == KC - 1))
                    last.then_inc(wo2_done, 1)

            turn_norm(2, lambda t: XN[:, t, :])
            pe.wait_ge(wo2_out, 4 * XT)
            for t in range(XT):
                for k in range(KC):
                    last = mm(ps[:, 0, EXPERTS * t:EXPERTS * (t + 1)], aT2[:, k, P * t:P * (t + 1)], router[:, k, :],
                              start=(k == 0), stop=(k == KC - 1))
            last.then_inc(rl_done, 1)
            pe.wait_ge(aff_done, 1)
            for t in range(XT):
                last = T(ps[0:EXPERTS, 1, P * t:P * (t + 1)], aff[:, t, :], ident)
            last.then_inc(affT_done, 1)
            pe.wait_ge(mark_done, 1)
            for t in range(XT):
                last = T(ps[:, 2, EXPERTS * t:EXPERTS * (t + 1)], takenT[:, P * t:P * (t + 1)],
                         ident[0:EXPERTS, 0:EXPERTS])
            last.then_inc(markT_done, 1)
            pe.wait_ge(mk_done, 1)
            for t in range(XT):
                for s in range(t + 1):
                    last = mm(ps[:, 3, EXPERTS * t:EXPERTS * (t + 1)], ones if s < t else cst[:, 13, :], mark[:, s, :],
                              start=(s == 0), stop=(s == t))
            last.then_inc(rank_done, 1)
            pe.wait_ge(sel_done, XT)
            for c in range(KC):
                for a in range(2):
                    i = 2 * c + a
                    if i >= 4:
                        pe.wait_ge(xg_out, i - 3)
                    for t in range(XT):
                        last = mm(ps[:, 4 + i % 4, :], XN[:, t, P * c:P * (c + 1)], sel[:, t, 512 * a:512 * (a + 1)],
                                  start=(t == 0), stop=(t == XT - 1))
                    last.then_inc(xg_done, 1)
            for t in range(XT):
                pe.wait_ge(selw_done, t + 1)
                for a in range(2):
                    i = 2 * t + a
                    if i >= 4:
                        pe.wait_ge(gt_out, i - 3)
                    for c in range(4):
                        last = T(ps[:, i % 4, P * c:P * (c + 1)], selw[:, t % 2, P * (4 * a + c):P * (4 * a + c + 1)],
                                 ident)
                    last.then_inc(gt_done, 1)
            pe.wait_ge(gt_out, 2 * XT)
            pe.wait_ge(xg_out, 2 * KC)
            pe.sem_inc(e_gate, 1)
            pe.sem_inc(e_up, 1)
            pe.sem_inc(e_down, 1)
            with pe.Fori(0, PAIRS) as i:
                for u in range(2):
                    pe.wait_ge(xe_set, 2 * i + u + 1)
                    for m, (bank, done) in enumerate(((u, e_gate), (2 + u, e_up))):
                        for a in range(2):
                            for x_ in range(2):
                                s = 4 * m + 2 * x_ + a
                                pe.wait_ge(eslot_in(s), 32 * i + 16 * (LOADED[s] + u + 1))
                            settle(pe, "pe")
                            for k in range(KC):
                                for x_ in range(2):
                                    last = mm(ps[64 * x_:64 * x_ + 64, bank, WCOLS * a:WCOLS * (a + 1)], xe[:, u, k, :],
                                              eslot(4 * m + 2 * x_ + a)[:, k, :], start=(k == 0), stop=(k == KC - 1))
                        last.then_inc(done, 1)
                    pe.wait_ge(e_hid, 2 * i + u + 1)
                    for c in range(4):
                        last = T(ps[:, 4, P * c:P * (c + 1)], hid[:, u, P * c:P * (c + 1)], ident)
                    last.then_inc(e_turn, 1)
                    pe.wait_ge(e_hidT, 2 * i + u + 1)
                    for a in range(2):
                        for x_ in range(2):
                            s = 8 + 2 * x_ + a
                            pe.wait_ge(eslot_in(s), 32 * i + 16 * (LOADED[s] + u + 1))
                        settle(pe, "pe")
                        for k in range(KC):
                            for x_ in range(2):
                                last = mm(ps[64 * x_:64 * x_ + 64, 5 + u, WCOLS * a:WCOLS * (a + 1)],
                                          hidT[:, k % 4, 64 * (k // 4):64 * (k // 4 + 1)],
                                          eslot(8 + 2 * x_ + a)[:, k, :], start=(k == 0), stop=(k == KC - 1))
                    last.then_inc(e_down, 1)
            pe.wait_ge(e_y, EXPERTS)
            pe.wait_ge(e_y2, EXPERTS)
            for t in range(XT):
                for a in range(2):
                    i = 2 * t + a
                    if i >= 4:
                        pe.wait_ge(cb_out, i - 3)
                    for p in range(PAIRS):
                        last = mm(ps[:, i % 4, :], GT[:, p, P * t:P * (t + 1)],
                                  xg[:, p, 4 * a:4 * a + 4, :].rearrange("p c n -> p (c n)"),
                                  start=(p == 0), stop=(p == PAIRS - 1))
                    last.then_inc(cb_done, 1)
            turn_norm(3, lambda t: xn3[:, t % 2, :])
            pe.wait_ge(cb_out, 2 * XT)
            pe.wait_ge(third_in, 32)
            for c in range(SLOTS):
                pe.wait_ge(slot_in[c], 16 * (LOADED[c] + EXPERTS + 1))
            wp = ring[:, 4, :, :].rearrange("p (k a) n -> p k (a n)", k=PLE // P)
            for t in range(XT):
                for m in range(4):
                    i = 4 * t + m
                    if i >= 4:
                        pe.wait_ge(pl_out, i - 3)
                    for k in range(KC):
                        mm(ps[:, i % 4, 0:WCOLS], aT3[:, k, P * t:P * (t + 1)], ring[:, m, k, :],
                           start=(k == 0), stop=(k == KC - 1))
                    for k in range(PLE // P):
                        last = mm(ps[:, 4 + i % 4, 0:WCOLS], pT[:, k, P * t:P * (t + 1)], wp[:, k, WCOLS * m:WCOLS * (m + 1)],
                                  start=(k == 0), stop=(k == PLE // P - 1))
                    last.then_inc(pl_done, 1)

        @block.scalar
        def _(act):
            A = nc.scalar.activation
            act.wait_ge(consts_set, 1)
            act.wait_ge(consts_in, 80)
            with act.Fori(0, DEPTH) as l:
                for t in range(TILES):
                    rows, q0 = rows_of(t)
                    act.wait_ge(turned, 2 * (l * TILES + t) + 1)
                    A(hT[:, 0:4, q0:q0 + rows],
                      ps[:, 4 + 2 * (t % 2), :].rearrange("p (c n) -> p c n", c=4)[:, :, 0:rows],
                      ACT.Copy).then_inc(turned_act, 1)

                def item(n):
                    kind, c = ITEMS[n]
                    act.wait_ge(proj_done, l * NI + n + 1)
                    src = pair(n % 2)
                    if n in RAW:
                        u = RAW.index(n)
                        if u >= 2:
                            act.wait_ge(raw_used, l * NRAW + u - 1)
                        A(halves(raw[:, u % 2, :]), src,
                          ACT.Sigmoid if kind == "g" else ACT.Copy).then_inc(proj_out, 1)
                    elif kind == "wi":
                        A(wi, ps[:, 2 * (n % 2), 0:32], ACT.Copy, scale=float(HEADS ** -0.5)).then_inc(proj_out, 1)
                    elif kind == "a":
                        A(halves(uT[:, c, TAPS - 1:TAPS - 1 + L]), src, ACT.Copy).then_inc(proj_out, 1)
                    elif kind == "v":
                        rows = min(P, L - P * c)
                        A(V[0:rows, c, :], ps[0:rows, 2 * (n % 2), :], ACT.Copy).then_inc(proj_out, 1)
                    else:
                        A(halves((zcT if kind == "zc" else zaT)[:, c, :]), src, ACT.Silu).then_inc(proj_out, 1)

                for n in range(NI):
                    item(n)
                    if n == IDX_AFTER:
                        for j in range(NIDX):
                            t = j // HEADS
                            act.wait_ge(idx_done, l * NIDX + j + 1)
                            if j >= 4:
                                act.wait_ge(idx_added, l * NIDX + j - 3)
                            dst, src = span(pr[:, j % 4, :], 4 + 2 * (j % 2), P, KEYS[t])
                            A(dst, src, ACT.Relu, scale=HEAD_DIM ** -0.5).then_inc(idx_relu, 1)
                for j in range(NATT + 2):
                    if j < NATT:
                        t, h, n, q0, keys, full = att(j)
                        act.wait_ge(at_masked, l * NATT + j + 1)
                        A(pr[0:n, j % 4, 0:keys], pr[0:n, j % 4, 0:keys], ACT.Exp, bias=neg_max[0:n, j:j + 1],
                          scale=-1.0, accum_out=row_sum[0:n, j:j + 1]).then_inc(at_exp, 1)
                    i = j - 2
                    if i >= 0 and att(i)[5]:
                        full = att(i)[5]
                        act.wait_ge(at_turned, l * NATT + i + 1)
                        if i >= 2:
                            act.wait_ge(at_value, l * NATT + i - 1)
                        A(prT[:, i % 2, 0:full, :], ps[:, i % 2, 0:P * full].rearrange("p (b n) -> p b n", n=P),
                          ACT.Copy).then_inc(at_full, 1)
                for c in range(4):
                    act.wait_ge(cn_centred, 4 * l + c + 1)
                    A(pr[:, c, :], yT[:, c, :], ACT.Square).then_inc(cn_square, 1)
                act.wait_ge(cn_var, l + 1)
                A(halves(raw[:, 0, :]), pair(1), ACT.Sqrt, bias=eps_ln).then_inc(cn_std, 1)
                for c in range(4):
                    act.wait_ge(cn_scaled, 4 * l + c + 1)
                    A(yT[:, c, :], yT[:, c, :], ACT.Silu, bias=convp[:, c, TAPS + 2:TAPS + 3],
                      scale=convp[:, c, TAPS + 1:TAPS + 2]).then_inc(cn_silu, 1)
                for t in range(TILES):
                    rows, _ = rows_of(t)
                    act.wait_ge(ln_var, l * TILES + t + 1)
                    A(ln_std_v[0:rows, t:t + 1], mean_var[0:rows, 2 * t + 1:2 * t + 2], ACT.Sqrt,
                      bias=eps_ln[0:rows, :]).then_inc(ln_std, 1)

            steps = Steps()

            def norm_square(w, t, scratch, src):
                A(scratch, src, ACT.Square, accum_out=norm_sq[:, XT * w + t:XT * w + t + 1]).then_inc(nq_done, 1)
                act.wait_ge(nq_done, XT * w + t + 1)
                A(norm_std[:, XT * w + t:XT * w + t + 1], norm_sq[:, XT * w + t:XT * w + t + 1], ACT.Sqrt,
                  bias=eps_rms, scale=1.0 / D_MODEL).then_inc(ns_done, 1)

            act.wait_ge(h_done, DEPTH * TILES)
            for t in range(XT):
                if t >= 2:
                    act.wait_ge(nt_done, 2 * (t - 1))
                norm_square(0, t, xn[:, t % 2, :], H[:, t, :])
            act.wait_ge(rt_arg, 1)
            A(rope2[:, 1, :], angle[:, :], ACT.Sin).then_inc(rt_sin, 1)
            A(rope2[:, 0, :], turns[:, :], ACT.Sin, bias=cst[:, 14, 65:66]).then_inc(rt_sin, 1)
            for n, (kind, c) in enumerate(ITEMS2):
                act.wait_ge(p2_done, n + 1)
                src = ps[:, n % 4, :]
                if n in ROPED2:
                    r = ROPED2.index(n)
                    if r >= 2:
                        act.wait_ge(raw2_used, r - 1)
                    A(raw2[:, r % 2, :], src, ACT.Copy).then_inc(p2_out, 1)
                elif kind == "av":
                    A(av[:, :, :], src.rearrange("p (t n) -> p t n", t=XT), ACT.Copy).then_inc(p2_out, 1)
                elif kind == "z":
                    A(zT[:, :], src[0:64, :], ACT.Identity, bias=cst[0:64, 14, 66:67]).then_inc(p2_out, 1)
                elif kind == "gv":
                    half, t = divmod(c, XT)
                    A(GV[:, t, 512 * half:512 * (half + 1)], src, ACT.Copy).then_inc(p2_out, 1)
                else:
                    g = 0 if kind == "gq" else 1
                    A(gqk[:, g, c, :], src, ACT.Copy, scale=G_DK ** -0.5 if g == 0 else 1.0).then_inc(p2_out, 1)
            for j in range(NW + 2):
                if j < NW:
                    t, h, k0, cnt = win(j)
                    act.wait_ge(w_masked, j + 1)
                    A(pr2[:, j % 4, 0:P * cnt], pr2[:, j % 4, 0:P * cnt], ACT.Exp, bias=neg_max2[:, j:j + 1],
                      scale=-1.0, accum_out=sum2[:, j:j + 1]).then_inc(w_exp, 1)
                    A(sink2[:, j:j + 1], sink[:, 0, h:h + 1], ACT.Exp, bias=neg_max2[:, j:j + 1])\
                        .then_inc(w_sink, 1)
                i = j - 2
                if i >= 0:
                    act.wait_ge(w_turned, i + 1)
                    if i >= 2:
                        act.wait_ge(w_value, i - 1)
                    n = P * win(i)[3]
                    A(pr2T[:, i % 2, 0:n], ps[:, 6 + i % 2, 0:n], ACT.Copy).then_inc(w_out_t, 1)

            def gate_log(i):
                act.wait_ge(gz_done, i + 1)
                if i >= 1:
                    act.wait_ge(gl_set, i)
                else:
                    act.wait_ge(w_att, XT)
                g = gate[:, 0, :]
                A(g, ps[:, i % 2, :], ACT.Abs).then_inc(act_step, steps.one())
                act.wait_ge(act_step, steps.now())
                A(g, g, ACT.Exp, scale=-1.0).then_inc(act_step, steps.one())
                act.wait_ge(act_step, steps.now())
                A(g, g, ACT.Ln, bias=ones[:, 0:1]).then_inc(gl_log, 1)

            def flat(b):
                return b[:, :, :].rearrange("p h n -> p (h n)")

            def gate_exp(i):
                act.wait_ge(gl_cum, i + 1)
                if i >= 1:
                    act.wait_ge(gl_qk, i)
                    act.wait_ge(gl_att, i)
                src = ps[:, 2 + i % 2, :]
                A(flat(decay[0]), src, ACT.Copy).then_inc(act_step, steps.one())
                A(flat(decay[1]), src, ACT.Exp).then_inc(act_step, steps.one())
                A(flat(decay[2]), src, ACT.Exp, scale=-1.0).then_inc(gl_exp, 1)

            gate_log(0)
            for i in range(len(TD)):
                gate_exp(i)
                if i + 1 < len(TD):
                    gate_log(i + 1)
                act.wait_ge(gl_rest, i + 1)
                A(flat(decay[3]), flat(decay[3]), ACT.Exp).then_inc(gl_rexp, 1)
                act.wait_ge(gl_turn, i + 1)
                t, d = TD[i]
                A(kE[:, d, t, :], ps[:, 6 + i % 2, :], ACT.Copy).then_inc(gl_kout, 1)
            for n in range(XT):
                act.wait_ge(o_out, XT + n + 1)
                for h in range(G_HEADS):
                    o = O[:, n, G_DV * h:G_DV * (h + 1)]
                    A(decay[0][:, 0:2, :].rearrange("p a n -> p (a n)") if h % 2 else
                      decay[1][:, 0:2, :].rearrange("p a n -> p (a n)"), o, ACT.Square,
                      accum_out=o_sq[:, 4 * n + h:4 * n + h + 1]).then_inc(o_sqd, 1)
                    act.wait_ge(o_sqd, 4 * n + h + 1)
                A(o_std[:, 4 * n:4 * n + 4], o_sq[:, 4 * n:4 * n + 4], ACT.Sqrt, bias=eps_rms, scale=1.0 / G_DV)\
                    .then_inc(o_stdd, 1)
            for c in range(KC):
                act.wait_ge(gr_done, c + 1)
                if c >= 2:
                    act.wait_ge(gr_out, c - 1)
                A(side[:, c % 2, :], ps[:, c % 4, :], ACT.Silu).then_inc(gr_silu, 1)
            for c in range(KC):
                for m in range(2):
                    i = 2 * c + m
                    act.wait_ge(mg_done, 4 * c + 2 * m + 1)
                    if c >= 2:
                        act.wait_ge(mg_out, i - 3)
                    A(side[:, 2 + i % 4, :], ps[:, 4 * (c % 2) + 2 * m, :], ACT.Sigmoid).then_inc(mg_sig, 1)
            for t in range(XT):
                act.wait_ge(wo2_out, 4 * (t + 1))
                norm_square(1, t, XN[:, t, :], H[:, t, :])
            act.wait_ge(rl_sub, 1)
            A(logit, logit, ACT.Exp).then_inc(rl_exp, 1)
            for c in range(KC):
                for a in range(2):
                    i = 2 * c + a
                    act.wait_ge(xg_done, i + 1)
                    A(xg[:, 4 * a:4 * a + 4, c, :], ps[:, 4 + i % 4, :].rearrange("p (i n) -> p i n", n=P), ACT.Copy,
                      scale=gains[:, 2, c:c + 1]).then_inc(xg_out, 1)
            for i in range(2 * XT):
                t, a = divmod(i, 2)
                act.wait_ge(gt_done, i + 1)
                A(GT[:, 4 * a:4 * a + 4, P * t:P * (t + 1)], ps[:, i % 4, :].rearrange("p (i n) -> p i n", n=P),
                  ACT.Copy).then_inc(gt_out, 1)
            act.wait_ge(xg_out, 2 * KC)
            with act.Fori(0, PAIRS) as i:
                for u in range(2):
                    act.wait_ge(e_gate, 2 * i + u + 2)
                    A(hid[:, u, :], ps[:, u, :], ACT.Silu).then_inc(e_silu, 1)
                    act.wait_ge(e_turn, 2 * i + u + 1)
                    A(hidT[:, :, :], ps[:, 4, :].rearrange("p (c n) -> p c n", c=4), ACT.Copy).then_inc(e_hidT, 1)
                    act.wait_ge(e_down, 2 * i + u + 2)
                    act.wait_ge(xe_set, 2 * i + 2)
                    A(xg[64 * u:64 * u + 64, i, 4:8, :],
                      ps[64:128, 5 + u, :].rearrange("p (c n) -> p c n", c=4), ACT.Copy).then_inc(e_y2, 1)
            for t in range(XT):
                act.wait_ge(cb_out, 2 * (t + 1))
                if t >= 2:
                    act.wait_ge(nt_done, 6 * XT + 2 * (t - 1))
                norm_square(2, t, xn3[:, t % 2, :], H[:, t, :])
            for i in range(4 * XT):
                act.wait_ge(pl_done, i + 1)
                if i >= 2:
                    act.wait_ge(pl_out, i - 1)
                A(emb[:, i % 2, :], ps[:, i % 4, 0:WCOLS], ACT.Sigmoid).then_inc(pl_sig, 1)
            for t in range(XT):
                act.wait_ge(pl_out, 4 * (t + 1))
                if t >= 2:
                    act.wait_ge(stored[t % 2], 16 * (t // 2))
                norm_square(3, t, outb[:, t % 2, :], H[:, t, :])

        @block.gpsimd
        def _(pool):
            nc.gpsimd.memset(uT[:, :, 0:TAPS - 1], 0.0).then_inc(pool_step, 1)

            pool.wait_ge(w_att, XT)
            nc.gpsimd.memset(AT[:, :, :, :], 0.0).then_inc(gl_zero, 1)
            pool.wait_ge(gt_out, 2 * XT)
            pool.wait_ge(xg_out, 2 * KC)
            with pool.Fori(0, PAIRS) as i:
                for u in range(2):
                    pool.wait_ge(e_up, 2 * i + u)
                    settle(pool, "pool")
                    nc.gpsimd.tensor_copy(xe[:, u, :, :], xg[:, i, :, CAP * u:CAP * (u + 1)]).then_inc(xe_set, 1)

        @block.vector
        def _(dve):
            V_ = nc.vector
            nc.vector.memset(small[:, :], 0.0).then_inc(dve_step, 1)
            dve.wait_ge(dve_step, 1)
            nc.vector.memset(eps_rms, RMS_EPS).then_inc(dve_step, 1)
            nc.vector.memset(eps_ln, LN_EPS).then_inc(consts_set, 1)
            dve.wait_ge(consts_set, 1)
            dve.wait_ge(consts_in, 80)
            dve.wait_ge(h_in, 32)
            dve.wait_ge(pool_step, 1)
            nc.vector.tensor_scalar(sink[:, 1, :], sink[:, 0, :], -1.0, None, ALU.mult).then_inc(dve_step, 1)
            STEPS1 = 361
            with dve.Fori(0, DEPTH) as l:
                k = Steps(l * STEPS1 + 3)
                for t in range(TILES):
                    rows, q0 = rows_of(t)
                    dve.wait_ge(turned, 2 * (l * TILES + t) + 2)
                    V_.tensor_copy(hT[:, 4:8, q0:q0 + rows],
                                   ps[:, 5 + 2 * (t % 2), :].rearrange("p (c n) -> p c n", c=4)[:, :, 0:rows])\
                        .then_inc(turned_dve, 1)

                def rope_item(r):
                    n = ROPED[r]
                    kind, c = ITEMS[n]
                    raw_r = raw[:, RAW.index(n) % 2, :]
                    dst = kiT[:, :] if kind == "ki" else dict(qi=qiT, q=qT, k=kT)[kind][:, c, :]
                    dve.wait_ge(rot_done, l * NROT + r + 1)
                    V_.tensor_tensor(halves(dst), pair(2 + r % 2), halves(rope[:, 1, :]), ALU.mult)\
                        .then_inc(dve_step, k.one())
                    V_.tensor_tensor(raw_r, raw_r, rope[:, 0, :], ALU.mult).then_inc(dve_step, k.one())
                    dve.wait_ge(dve_step, k.now())
                    V_.tensor_tensor(dst, dst, raw_r, ALU.add).then_inc(raw_used, 1)

                def gate_item(c):
                    n = ITEM[("g", c)]
                    dve.wait_ge(proj_out, l * NI + n + 1)
                    V_.tensor_tensor(uT[:, c, TAPS - 1:TAPS - 1 + L], uT[:, c, TAPS - 1:TAPS - 1 + L],
                                     raw[:, RAW.index(n) % 2, :], ALU.mult).then_inc(raw_used, 1)
                    if c == 3:
                        dve.wait_ge(raw_used, l * NRAW + RAW.index(n) + 1)
                        V_.memset(small[:, 500:501], 0.0).then_inc(gated, 4)

                for r in range(5):
                    rope_item(r)
                for t in range(XT):
                    V_.memset(score[t][:, 0:DUMMIES], DUMMY_SCORE).then_inc(dve_step, k.one())
                for j in range(NIDX):
                    t, h = divmod(j, HEADS)
                    s = score[t][:, DUMMIES:]
                    r_ = pr[:, j % 4, 0:KEYS[t]]
                    w = wi[:, 8 * t + h:8 * t + h + 1]
                    dve.wait_ge(idx_relu, l * NIDX + j + 1)
                    if h == 0:
                        V_.tensor_scalar(s, r_, w, None, ALU.mult).then_inc(idx_added, 1)
                    else:
                        dve.wait_ge(idx_added, l * NIDX + j)
                        V_.scalar_tensor_tensor(out=s, in0=r_, scalar=w, in1=s, op0=ALU.mult, op1=ALU.add)\
                            .then_inc(idx_added, 1)
                    if h == HEADS - 1:
                        dve.wait_ge(idx_added, l * NIDX + j + 1)
                        d = score[t][:, DUMMIES + N_META + P * t:]
                        V_.tensor_tensor(d, d, future_score, ALU.add).then_inc(dve_step, k.one())

                def top_round():
                    dve.wait_ge(dve_step, k.now())
                    settle(dve, "dve")
                    for t in range(XT):
                        V_.max(top8[:, 8 * t:8 * t + 8], score[t][:, :]).then_inc(dve_step, k.one())
                    for t in range(XT):
                        dve.wait_ge(dve_step, k.now() - XT + 1)
                        settle(dve, "dve")
                        V_.match_replace(score[t][:, :], top8[:, 8 * t:8 * t + 8], score[t][:, :], TAKEN)\
                            .then_inc(dve_step, k.one())

                conv_marks = {}

                def conv_taps(first, end):
                    for u in range(first, end):
                        j, c = divmod(u, 4)
                        done = (conv_done, 1) if j == TAPS - 1 else (dve_step, k.one())
                        if j == 0:
                            V_.tensor_scalar(yT[:, c, :], uT[:, c, 0:L], convp[:, c, 0:1],
                                             convp[:, c, TAPS:TAPS + 1], ALU.mult, ALU.add).then_inc(*done)
                        else:
                            dve.wait_ge(dve_step, k.at(conv_marks[c]))
                            V_.scalar_tensor_tensor(out=yT[:, c, :], in0=uT[:, c, j:j + L],
                                                    scalar=convp[:, c, j:j + 1], in1=yT[:, c, :],
                                                    op0=ALU.mult, op1=ALU.add).then_inc(*done)
                        conv_marks[c] = k.n

                dve.wait_ge(params_in, 48 * (l + 1))
                rounds = 0
                for n in range(NI):
                    kind, c = ITEMS[n]
                    if kind == "g":
                        gate_item(c)
                    elif kind in ("q", "k"):
                        rope_item(ROPED.index(n))
                    else:
                        continue
                    for _ in range(2):
                        if rounds < ROUNDS:
                            top_round()
                            rounds += 1
                while rounds < ROUNDS:
                    top_round()
                    rounds += 1
                dve.wait_ge(dve_step, k.now())
                for t in range(XT):
                    V_.tensor_scalar(score[t][:, :], score[t][:, :], TAKEN, HIDDEN, ALU.not_equal, ALU.mult)\
                        .then_inc(dve_step, k.one())
                dve.wait_ge(dve_step, k.now())
                d = score[0][:, DUMMIES + N_META:]
                V_.tensor_tensor(d, d, future_hidden, ALU.add).then_inc(dve_step, k.one())

                conv_taps(0, 4 * TAPS)

                def masked(j):
                    t, h, n, q0, keys, _ = att(j)
                    dve.wait_ge(at_score, l * NATT + j + 1)
                    if j >= 4:
                        dve.wait_ge(at_turned, l * NATT + j - 3)
                    if j == 0:
                        dve.wait_ge(dve_step, k.now())
                    dst, src = span(pr[:, j % 4, :], 4 + 2 * (j % 2), n, keys)
                    m = score[t][0:n, DUMMIES:] if t < XT else future_hidden[0:n, 0:N_META]
                    if keys > 512:
                        m = halves(m)
                    settle(dve, "dve")
                    V_.tensor_tensor_reduce(dst, src, m, -(HEAD_DIM ** -0.5), 3.0e38, ALU.add, ALU.min,
                                            neg_max[0:n, j:j + 1]).then_inc(at_masked, 1)

                def scaled(j):
                    t, h, n, q0, keys, _ = att(j)
                    dve.wait_ge(at_exp, l * NATT + j + 1)
                    V_.reciprocal(row_inv[0:n, j:j + 1], row_sum[0:n, j:j + 1]).then_inc(dve_step, k.one())
                    dve.wait_ge(dve_step, k.now())
                    V_.tensor_scalar(pr[0:n, j % 4, 0:keys], pr[0:n, j % 4, 0:keys], row_inv[0:n, j:j + 1], None,
                                     ALU.mult).then_inc(at_prob, 1)

                def rest(j):
                    n = att(j)[2]
                    dve.wait_ge(at_turned, l * NATT + j + 1)
                    if j >= 2:
                        dve.wait_ge(at_value, l * NATT + j - 1)
                    V_.tensor_copy(prR[:, j % 2, 0:n], ps[0:N_META, 2, P * (j % 4):P * (j % 4) + n])\
                        .then_inc(at_rest, 1)

                for j in range(NATT + 4):
                    if j < NATT:
                        masked(j)
                    if 1 <= j <= NATT:
                        scaled(j - 1)
                    if 2 <= j < NATT + 2:
                        rest(j - 2)
                    if j >= 4 and (j - 4) % HEADS == HEADS - 1:
                        t = (j - 4) // HEADS
                        n, q0 = rows_of(t)
                        dve.wait_ge(at_value, l * NATT + HEADS * (t + 1))
                        dve.wait_ge(proj_out, l * NI + NI)
                        V_.tensor_tensor(yT[:, 4:8, q0:q0 + n],
                                         ps[:, 3, :].rearrange("p (c n) -> p c n", c=4)[:, :, 0:n],
                                         zaT[:, :, q0:q0 + n], ALU.mult).then_inc(attn_y, 1)

                dve.wait_ge(cn_mean, l + 1)
                for c in range(4):
                    V_.tensor_tensor(halves(yT[:, c, :]), halves(yT[:, c, :]), pair(0), ALU.subtract)\
                        .then_inc(cn_centred, 1)
                dve.wait_ge(cn_std, l + 1)
                V_.reciprocal(raw[:, 1, :], raw[:, 0, :]).then_inc(dve_step, k.one())
                dve.wait_ge(dve_step, k.now())
                for c in range(4):
                    V_.tensor_tensor(yT[:, c, :], yT[:, c, :], raw[:, 1, :], ALU.mult).then_inc(cn_scaled, 1)
                for c in range(4):
                    dve.wait_ge(cn_silu, 4 * l + c + 1)
                    V_.tensor_tensor(yT[:, c, :], yT[:, c, :], zcT[:, c, :], ALU.mult).then_inc(conv_y, 1)
                for t in range(TILES):
                    rows, _ = rows_of(t)
                    ht = H[0:rows, t, :]
                    for m in range(4):
                        i = 4 * t + m
                        hm = H[0:rows, t, WCOLS * m:WCOLS * (m + 1)]
                        dve.wait_ge(wo_done, l * 4 * TILES + i + 1)
                        V_.scalar_tensor_tensor(out=hm, in0=hm, scalar=ALPHA, in1=ps[0:rows, 4 + i % 4, 0:WCOLS],
                                                op0=ALU.mult, op1=ALU.add).then_inc(wo_added, 1)
                    dve.wait_ge(wo_added, l * 4 * TILES + 4 * t + 4)
                    for a in range(2):
                        V_.bn_stats(stats[0:rows, 6 * a:6 * a + 6], H[0:rows, t, 512 * a:512 * (a + 1)])\
                            .then_inc(dve_step, k.one())
                    dve.wait_ge(dve_step, k.now())
                    settle(dve, "dve")
                    V_.bn_aggr(mean_var[0:rows, 2 * t:2 * t + 2], stats[0:rows, :]).then_inc(ln_var, 1)
                    dve.wait_ge(ln_std, l * TILES + t + 1)
                    V_.reciprocal(ln_inv[0:rows, t:t + 1], ln_std_v[0:rows, t:t + 1]).then_inc(dve_step, k.one())
                    dve.wait_ge(dve_step, k.now())
                    V_.tensor_scalar(ht, ht, mean_var[0:rows, 2 * t:2 * t + 1], ln_inv[0:rows, t:t + 1],
                                     ALU.subtract, ALU.mult).then_inc(dve_step, k.one())
                    dve.wait_ge(dve_step, k.now())
                    V_.tensor_tensor(ht, ht, post[0:rows, 0, :], ALU.mult).then_inc(dve_step, k.one())
                    dve.wait_ge(dve_step, k.now())
                    V_.tensor_tensor(ht, ht, post[0:rows, 1, :], ALU.add).then_inc(h_done, 1)
                assert k.n == STEPS1, k.n

            k = Steps(DEPTH * STEPS1 + 3)
            TT, TS, STT = V_.tensor_tensor, V_.tensor_scalar, V_.scalar_tensor_tensor

            def step(instruction):
                instruction.then_inc(dve_step, k.one())
                dve.wait_ge(dve_step, k.now())

            def norm_scale(w, v, t, dst, src):
                dve.wait_ge(ns_done, XT * w + t + 1)
                inv = norm_inv[:, t:t + 1]
                step(V_.reciprocal(inv, norm_std[:, XT * w + t:XT * w + t + 1]))
                TS(dst, src, inv, None, ALU.mult).then_inc(xn_done if v is not None else dve_step,
                                                           1 if v is not None else k.one())

            def norm_out(v, dst, t):
                for hf in range(2):
                    dve.wait_ge(nt_done, 2 * XT * v + 2 * t + hf + 1)
                    TT(dst[:, 4 * hf:4 * hf + 4, P * t:P * (t + 1)],
                       ps[:, 4 + (2 * t + hf) % 4, :].rearrange("p (c n) -> p c n", c=4),
                       gains[:, v, 4 * hf:4 * hf + 4].unsqueeze(2).to_broadcast([P, 4, P]), ALU.mult)\
                        .then_inc(nt_out, 1)

            dve.wait_ge(h_done, DEPTH * TILES)
            for t in range(XT):
                norm_scale(0, 0, t, xn[:, t % 2, :], H[:, t, :])
                norm_out(0, aT, t)
            dve.wait_ge(second_in, 32)
            step(V_.tensor_copy(pos[:, :], pos[:, :].bitcast(I32)))
            step(TS(angle[:, :], pos[:, :], cst[:, 14, 64:65], None, ALU.mult))
            step(TS(turns[:, :], angle[:, :], float(0.5 / np.pi), FAR, ALU.mult, ALU.add))
            step(TS(turns[:, :], turns[:, :], -FAR, None, ALU.add))
            for part in TURN:
                step(STT(out=angle[:, :], in0=turns[:, :], scalar=-part, in1=angle[:, :], op0=ALU.mult, op1=ALU.add))
            step(TS(angle[:, :], angle[:, :], 3.1415925, -3.1415925, ALU.min, ALU.max))
            dve.wait_ge(dve_step, k.now())
            STT(out=turns[:, :], in0=angle[:, :], scalar=-1.0, in1=angle[:, :], op0=ALU.mult, op1=ALU.min).then_inc(rt_arg, 1)
            dve.wait_ge(rt_sin, 2)
            for r, n in enumerate(ROPED2):
                kind, c = ITEMS2[n]
                dst = (akT if kind == "ak" else aqT)[:, c, :]
                dve.wait_ge(rot2_done, r + 1)
                TT(dst, ps[:, 4 + r % 2, :], rope2[:, 1, :], ALU.mult).then_inc(dve_step, k.one())
                step(TT(raw2[:, r % 2, :], raw2[:, r % 2, :], rope2[:, 0, :], ALU.mult))
                TT(dst, dst, raw2[:, r % 2, :], ALU.add).then_inc(raw2_used, 1)

            for j in range(NW + 4):
                if j < NW:
                    t, h, k0, cnt = win(j)
                    dve.wait_ge(w_score, j + 1)
                    if j >= 4:
                        dve.wait_ge(w_turned, j - 3)
                    m0 = P * (k0 - t + 1)
                    V_.tensor_tensor_reduce(pr2[:, j % 4, 0:P * cnt], ps[:, 4 + j % 2, 0:P * cnt],
                                            window[:, m0:m0 + P * cnt], -(HEAD_DIM ** -0.5), sink[:, 1, h:h + 1],
                                            ALU.add, ALU.min, neg_max2[:, j:j + 1]).then_inc(w_masked, 1)
                i = j - 1
                if 0 <= i < NW:
                    n = P * win(i)[3]
                    dve.wait_ge(w_exp, i + 1)
                    dve.wait_ge(w_sink, i + 1)
                    step(TT(den2[:, i:i + 1], sum2[:, i:i + 1], sink2[:, i:i + 1], ALU.add))
                    step(V_.reciprocal(inv2[:, i:i + 1], den2[:, i:i + 1]))
                    TS(pr2[:, i % 4, 0:n], pr2[:, i % 4, 0:n], inv2[:, i:i + 1], None, ALU.mult).then_inc(w_prob, 1)
                if j >= 4 and (j - 4) % HEADS == HEADS - 1:
                    t = (j - 4) // HEADS
                    dve.wait_ge(w_value, HEADS * (t + 1))
                    V_.tensor_copy(attT[:, :, P * t:P * (t + 1)], ps[:, t % 2, :].rearrange("p (c n) -> p c n", c=4))\
                        .then_inc(w_att, 1)

            def gate_set(i):
                dve.wait_ge(gl_log, i + 1)
                if i >= 1:
                    dve.wait_ge(gl_cum, i)
                STT(out=gate[:, 1, :], in0=ps[:, i % 2, :], scalar=0.0, in1=gate[:, 0, :], op0=ALU.min,
                    op1=ALU.subtract).then_inc(gl_set, 1)

            gate_set(0)
            for i, (t, d) in enumerate(TD):
                dve.wait_ge(gl_exp, i + 1)
                if i >= 1:
                    dve.wait_ge(gl_turn, i)
                edge = 0 if d else CHUNK - 1
                b = decay[0][:, :, :].rearrange("p h (c n) -> p (h c) n", c=2)
                TT(decay[3][:, :, :].rearrange("p h (c n) -> p (h c) n", c=2),
                   b[:, :, edge:edge + 1].to_broadcast([P, 8, CHUNK]), b, ALU.subtract).then_inc(gl_rest, 1)
                V_.tensor_copy(dec[:, d, t, :, :],
                               decay[1][:, :, :].rearrange("p h (c n) -> p h c n", c=2)[:, :, :, edge])\
                    .then_inc(dve_step, k.one())
                q = gqk[:, 0, :, P * t:P * (t + 1)]
                kk = gqk[:, 1, :, P * t:P * (t + 1)]
                TT(qB[:, :, P * t:P * (t + 1)] if d else q, q, decay[1][:, :, :], ALU.mult)\
                    .then_inc(dve_step, k.one())
                TT(decay[2][:, :, :], kk, decay[2][:, :, :], ALU.mult).then_inc(dve_step, k.one())
                if i + 1 < len(TD):
                    gate_set(i + 1)
                dve.wait_ge(gl_rexp, i + 1)
                TT(decay[3][:, :, :], kk, decay[3][:, :, :], ALU.mult).then_inc(gl_qk, 1)
                dve.wait_ge(gl_att, i + 1)
                dve.wait_ge(gl_zero, 1)
                if i >= 1:
                    dve.wait_ge(gl_mask, i)
                V_.copy_predicated(AT[:, t, :, :],
                                   cst[:, 9 if d else 7, :].bitcast(U32).unsqueeze(1).to_broadcast([P, 4, P]),
                                   ps[:, 4 + i % 2, :].rearrange("p (h n) -> p h n", h=4)).then_inc(gl_mask, 1)
            for rnd, d in enumerate((1, 0)):
                if rnd:
                    dve.wait_ge(o_done, XT)
                step(V_.memset(S[:, 0, :, :], 0.0))

                def update(s):
                    t, c = SCAN[d][s]
                    dve.wait_ge(kv_done, 7 * rnd + s + 1)
                    if s >= 1:
                        dve.wait_ge(st_done, 7 * rnd + s)
                    if s >= 2:
                        dve.wait_ge(o_done, XT * rnd + (s - 2) // 2 + 1)
                    for h in range(G_HEADS):
                        last = STT(out=S[:, (s + 1) % 3, h, :], in0=S[:, s % 3, h, :], scalar=dec[:, d, t, h, c:c + 1],
                                   in1=ps[:, 2 * ((7 * rnd + s) % 2) + h // 2, G_DV * (h % 2):G_DV * (h % 2 + 1)],
                                   op0=ALU.mult, op1=ALU.add)
                        if h == G_HEADS - 1:
                            last.then_inc(st_done, 1)

                def output(i):
                    t = SCAN[d][2 * i][0]
                    n = XT * rnd + i
                    dve.wait_ge(o_done, n + 1)
                    src = ps[:, 4 + 2 * (n % 2):6 + 2 * (n % 2), :]
                    dst = O[:, t, :].rearrange("p (a n) -> p a n", a=2)
                    if d:
                        V_.tensor_copy(dst, src).then_inc(o_out, 1)
                    else:
                        TT(dst, src, dst, ALU.add).then_inc(o_out, 1)

                for s in range(7):
                    if s >= 2 and s % 2 == 0:
                        output(s // 2 - 1)
                    update(s)
                output(3)

            for t in range(XT):
                dve.wait_ge(o_stdd, t + 1)
                step(V_.reciprocal(o_inv[:, 4 * t:4 * t + 4], o_std[:, 4 * t:4 * t + 4]))
                for h in range(G_HEADS):
                    o = O[:, t, G_DV * h:G_DV * (h + 1)]
                    last = TS(o, o, o_inv[:, 4 * t + h:4 * t + h + 1], None, ALU.mult)
                last.then_inc(xn_done, 1)
                if t >= 1:
                    norm_out(1, OT, t - 1)
            norm_out(1, OT, XT - 1)
            dve.wait_ge(nt_out, 4 * XT)
            for c in range(KC):
                dve.wait_ge(gr_silu, c + 1)
                TT(OT[:, c, :], OT[:, c, :], side[:, c % 2, :], ALU.mult).then_inc(gr_out, 1)
            for c in range(KC):
                for m in range(2):
                    i = 2 * c + m
                    dve.wait_ge(mg_sig, i + 1)
                    dve.wait_ge(mg_done, 4 * c + 2 * m + 2)
                    s = side[:, 2 + i % 4, :]
                    y = ps[:, 4 * (c % 2) + 2 * m + 1, :]
                    if m == 0:
                        TT(mT[:, c, :], s, y, ALU.mult).then_inc(mg_out, 1)
                    else:
                        step(TT(s, s, y, ALU.mult))
                        TT(mT[:, c, :], mT[:, c, :], s, ALU.add).then_inc(mg_out, 1)
            for t in range(XT):
                for m in range(4):
                    i = 4 * t + m
                    hm = H[:, t, WCOLS * m:WCOLS * (m + 1)]
                    dve.wait_ge(wo2_done, i + 1)
                    TT(hm, hm, ps[:, i % 4, 0:WCOLS], ALU.add).then_inc(wo2_out, 1)
                norm_scale(1, 2, t, XN[:, t, :], H[:, t, :])
            for t in range(XT):
                norm_out(2, aT2, t)

            dve.wait_ge(rl_done, 1)
            lg = ps[:, 0, 0:EXPERTS * XT].rearrange("p (t e) -> p t e", t=XT)

            def wide(v):
                return v.unsqueeze(2).to_broadcast([P, XT, EXPERTS])

            step(V_.tensor_reduce(soft[:, 0:4], lg, AX.X, ALU.max))
            TT(logit, lg, wide(soft[:, 0:4]), ALU.subtract).then_inc(rl_sub, 1)
            dve.wait_ge(rl_exp, 1)
            step(V_.tensor_reduce(soft[:, 4:8], logit, AX.X, ALU.add))
            step(V_.reciprocal(soft[:, 8:12], soft[:, 4:8]))
            TT(aff, logit, wide(soft[:, 8:12]), ALU.mult).then_inc(aff_done, 1)
            dve.wait_ge(affT_done, 1)
            step(V_.tensor_copy(affT, ps[0:EXPERTS, 1, :]))
            for _ in range(CAP // 8):
                step(V_.max(max8[0:EXPERTS, :], affT))
                step(V_.match_replace(affT, max8[0:EXPERTS, :], affT, TAKEN_AFF))
            TS(takenT, affT, TAKEN_AFF, None, ALU.is_equal).then_inc(mark_done, 1)
            dve.wait_ge(markT_done, 1)
            V_.tensor_copy(mark, ps[:, 2, 0:EXPERTS * XT].rearrange("p (t e) -> p t e", t=XT)).then_inc(mk_done, 1)
            dve.wait_ge(rank_done, 1)
            dve.wait_ge(mk_done, 1)
            step(TT(rank, ps[:, 3, 0:EXPERTS * XT].rearrange("p (t e) -> p t e", t=XT), mark, ALU.mult))
            step(TS(rank, rank, -1.0, None, ALU.add))
            slots = cst[:, 14, 0:CAP].unsqueeze(1).to_broadcast([P, EXPERTS, CAP])
            for t in range(XT):
                TT(sel[:, t, :].rearrange("p (e c) -> p e c", c=CAP), slots,
                   rank[:, t, :].unsqueeze(2).to_broadcast([P, EXPERTS, CAP]), ALU.is_equal).then_inc(sel_done, 1)
            for t in range(XT):
                if t >= 2:
                    dve.wait_ge(gt_done, 2 * (t - 1))
                dve.wait_ge(sel_done, t + 1)
                TT(selw[:, t % 2, :].rearrange("p (e c) -> p e c", c=CAP),
                   sel[:, t, :].rearrange("p (e c) -> p e c", c=CAP),
                   aff[:, t, :].unsqueeze(2).to_broadcast([P, EXPERTS, CAP]), ALU.mult).then_inc(selw_done, 1)
            with dve.Fori(0, PAIRS) as i:
                for u in range(2):
                    dve.wait_ge(e_silu, 2 * i + u + 1)
                    dve.wait_ge(e_up, 2 * i + u + 2)
                    TT(hid[:, u, :], hid[:, u, :], ps[:, 2 + u, :], ALU.mult).then_inc(e_hid, 1)
                    dve.wait_ge(e_down, 2 * i + u + 2)
                    dve.wait_ge(xe_set, 2 * i + 2)
                    V_.tensor_copy(xg[64 * u:64 * u + 64, i, 0:4, :],
                                   ps[0:64, 5 + u, :].rearrange("p (c n) -> p c n", c=4)).then_inc(e_y, 1)
            for t in range(XT):
                for a in range(2):
                    hm = H[:, t, 512 * a:512 * (a + 1)]
                    dve.wait_ge(cb_done, 2 * t + a + 1)
                    TT(hm, hm, ps[:, (2 * t + a) % 4, :], ALU.add).then_inc(cb_out, 1)
            for t in range(XT):
                norm_scale(2, 3, t, xn3[:, t % 2, :], H[:, t, :])
                if t >= 1:
                    norm_out(3, aT3, t - 1)
            norm_out(3, aT3, XT - 1)
            dve.wait_ge(third_in, 32)
            for t in range(XT):
                for m in range(4):
                    i = 4 * t + m
                    hm = H[:, t, WCOLS * m:WCOLS * (m + 1)]
                    e = emb[:, i % 2, :]
                    dve.wait_ge(pl_sig, i + 1)
                    dve.wait_ge(pl_done, i + 1)
                    step(TT(e, e, ps[:, 4 + i % 4, 0:WCOLS], ALU.mult))
                    TT(hm, hm, e, ALU.add).then_inc(pl_out, 1)
            for t in range(XT):
                norm_scale(3, None, t, outb[:, t % 2, :], H[:, t, :])
                dve.wait_ge(dve_step, k.now())
                TT(outb[:, t % 2, :], outb[:, t % 2, :], final_g[:, :], ALU.mult).then_inc(y_set, 1)


def kernel(**inputs):
    import concourse.bacc as bacc
    from concourse.bass_utils import run_bass_kernel_spmd

    g = {n: np.asarray(v) for n, v in inputs.items()}
    nc = bacc.Bacc("TRN2", target_bir_lowering=False, num_devices=1)
    arrays = {}

    def dram(name, a):
        a = np.ascontiguousarray(a)
        arrays[f"in_{name}"] = a
        return nc.dram_tensor(f"in_{name}", a.shape, mybir.dt.from_np(a.dtype), kind="ExternalInput").ap()

    def chunked(name, a):
        return dram(name, a).rearrange("(k p) n -> p k n", p=P)

    w_in, w2 = g["w_in"], g["w_in_2"][0]
    ki = w_in[:, :, COL_KI:COL_WI]
    w_misc = np.concatenate([ki, ki, w_in[:, :, COL_WI:]], -1)
    conv = np.concatenate([g["conv_w"], g["conv_b"][:, None], g["conv_ln_g"][:, None], g["conv_ln_b"][:, None]], 1)
    conv = conv.transpose(0, 2, 1).reshape(DEPTH, 4, P, TAPS + 3).transpose(0, 2, 1, 3)
    post = np.broadcast_to(np.stack([g["post_ln_g"], g["post_ln_b"]], 1)[:, None], (DEPTH, P, 2, D_MODEL))
    cst, rope = constants()
    pad = np.zeros((D_MODEL, 16), np.float32)
    kv = [w2[:, 512 + 64 * i:512 + 64 * (i + 1)] for i in range(2)]
    misc2 = np.concatenate([kv[0], kv[0], kv[1], kv[1], w2[:, 640:768], w2[:, 3840:3856], pad, w2[:, 3856:3872], pad], 1)
    up = np.zeros((64, 512), np.float32)
    for d, n in enumerate(("fwd", "bwd")):
        up[32 * d:32 * d + 16] = g[f"gla_gate_up_{n}_2"][0]
        up[32 * d + 16] = g[f"gla_gate_bias_{n}_2"][0]
    gains = np.stack([g[n][0].reshape(KC, P).T for n in ("norm_mix_2", "gla_norm_2", "norm_ffn_2", "norm_ple_2")], 1)
    B = dict(
        up=dram("up", up), positions=dram("positions", g["positions_2"][0]).partition_broadcast(P),
        gains=dram("gains", gains), router=chunked("router", g["w_router_2"][0]), sink=dram("sink", g["attn_sink_2"][0]),
        w_misc=chunked("w_misc2", misc2), w_in=chunked("w_in2", w2), w_ba=chunked("w_ba", g["w_branch_attn_2"][0]),
        w_bg=chunked("w_bg", g["w_branch_gla_2"][0]), w_wo=chunked("w_wo", g["w_out_2"][0]),
        w_exp=[dram(f"exp_{n}", g[f"w_exp_{n}_2"][0]).rearrange("e (k p) n -> e p k n", p=P)
               for n in ("gate", "up", "down")],
        final=dram("final", g["norm_final_2"]), pT=chunked("pT", g["p_2"][0, 0].T),
        w_pg=chunked("w_pg", g["w_ple_gate_2"][0]), w_p=chunked("w_p", g["w_ple_2"][0]))
    out = nc.dram_tensor("out_0", (SEQ, D_MODEL), mybir.dt.float32, kind="ExternalOutput").ap()
    hybrid_kernel(nc, dram("x", g["x"][0]), dram("meta", g["meta_tokens"]), dram("w_in1", w_in), dram("w_misc", w_misc),
                  dram("conv", conv), dram("w_out", g["w_out"]), dram("post", post), dram("cst", cst), dram("rope", rope),
                  B, out)
    r = run_bass_kernel_spmd(nc, [arrays], core_ids=[0])
    return r.results[0]["out_0"][None]
```

```python
import numpy as np
import concourse.bass as bass
from concourse import mybir
from contextlib import ExitStack

P = 128
D_MODEL, SEQ, DEPTH, N_META = 1024, 512, 2, 16
L = SEQ + N_META
HALF = L // 2
KC = D_MODEL // P
D_CONV, TAPS = 512, 31
HEADS, HEAD_DIM = 8, 64
TOPK = min(256, L // 4)
DUMMIES = -TOPK % 8
ROUNDS = (TOPK + DUMMIES) // 8
ALPHA = (2.0 * DEPTH) ** 0.25
LN_EPS, RMS_EPS = 1e-5, 1e-6
COL_A, COL_G, COL_ZC, COL_Q, COL_K, COL_V, COL_ZA, COL_QI, COL_KI, COL_WI = (
    0, 512, 1024, 1536, 2048, 2560, 3072, 3584, 4096, 4160)
DUMMY_SCORE, FUTURE_SCORE, TAKEN = 3.0e38, -3.0e38, float(np.float32(-3.3e38))
HIDDEN = -1.0e30
XT = SEQ // P
TILES = XT + 1
WCOLS = 256
SLOTS = 5
NC = 15


def constants():
    i = np.arange(P)
    c = np.zeros((NC, P, P), np.float32)
    c[0] = np.eye(P)
    c[1] = 1.0
    c[2] = 1.0 / D_CONV
    for base in (0, 64):
        for d in range(32):
            c[3][base + d + 32, base + d] = -1.0
            c[3][base + d, base + d + 32] = 1.0
        for d in range(8):
            c[4][base + d + 8, base + d] = -1.0
            c[4][base + d, base + d + 8] = 1.0
    later = i[None, :] > i[:, None]
    c[5] = np.where(later, FUTURE_SCORE, 0.0)
    c[6] = np.where(later, HIDDEN, 0.0)
    same = (i[:, None] // 64) == (i[None, :] // 64)
    c[7] = (same & (i[:, None] <= i[None, :])) / 16.0
    c[8] = (same & (i[:, None] >= i[None, :])) / 16.0
    c[9] = (same & (i[:, None] > i[None, :]))
    c[10] = np.where(i[None, :] >= i[:, None], 0.0, HIDDEN)
    c[12] = np.where(i[None, :] <= i[:, None], 0.0, HIDDEN)
    c[13] = (i[:, None] <= i[None, :])
    c[14][:, 0:64] = i[None, 0:64]
    inv2 = (np.float32(500000.0) ** (-np.arange(0, 16, 2, dtype=np.float32) / np.float32(16))).astype(np.float32)
    for base in (0, 64):
        c[14][base:base + 16, 64] = np.tile(inv2, 2)
    c[14][:, 65] = np.pi / 2
    c[14][[16, 48], 66] = 1.0
    inv = (np.float32(10000.0) ** (-np.arange(0, 64, 2, dtype=np.float32) / np.float32(64))).astype(np.float32)
    ang = np.arange(L, dtype=np.float32)[None, :] * inv[:, None]
    rope = np.stack([np.tile(np.cos(ang), (4, 1)), np.tile(np.sin(ang), (4, 1))], 1).astype(np.float32)
    return np.ascontiguousarray(c.transpose(1, 0, 2)), np.ascontiguousarray(rope)


G_HEADS, G_DK, G_DV, CHUNK = 4, 128, 256, 64
EXPERTS, CAP = 16, 2 * SEQ // 16
PAIRS = EXPERTS // 2
QUARTERS = D_MODEL // WCOLS
COL2 = dict(aq=0, gq=768, gk=1280, gv=1792, gr=2816, ga=3872, gg=4896)
PLE = 256
FAR = 1.5 * 2.0 ** 23
TURN = (6.28125, 0.0019350051879882812, 3.0199159819e-7)
TAKEN_AFF = -1.0
WO_FIRST = 1


class Steps:

    def __init__(self, base=0):
        self.base, self.n = base, 0

    def one(self):
        self.n += 1
        return 1

    def now(self):
        return self.base + self.n

    def at(self, n):
        return self.base + n


def hybrid_kernel(nc, x, meta, w_in, w_misc, conv_p, w_out, post_p, cst_d, rope_d, B, out):
    F32, U32, I32 = mybir.dt.float32, mybir.dt.uint32, mybir.dt.int32
    ALU, ACT, AX = mybir.AluOpType, mybir.ActivationFunctionType, mybir.AxisListType

    w_in_v = w_in.rearrange("l (k p) n -> l p k n", p=P)
    w_out_v = w_out.rearrange("l (k p) n -> l p k n", p=P)
    w_misc_v = w_misc.rearrange("l (k p) n -> l p k n", p=P)

    top = ExitStack()
    with top:
        def pool_of(stack):
            return lambda name, shape: stack.enter_context(nc.sbuf_tensor(name, shape, F32))

        def sem(name):
            return top.enter_context(nc.semaphore(name))

        keep = pool_of(top)
        H = keep("H", [P, TILES, D_MODEL])
        cst = keep("cst", [P, NC, P])
        ring = keep("ring", [P, SLOTS, KC, WCOLS])
        small = keep("small", [P, 512])
        few = keep("few", [P, 640])
        gains = keep("gains", [P, 4, KC])
        router = keep("router", [P, KC, EXPERTS])
        sink = keep("sink", [P, 2, HEADS])
        ident, ones, mean_w, rot = cst[:, 0, :], cst[:, 1, :], cst[:, 2, :], cst[:, 3, :]
        future_score, future_hidden = cst[:, 5, :], cst[:, 6, :]

        first = ExitStack()
        buf = pool_of(first)
        hT = buf("hT", [P, KC, L])
        rope = buf("rope", [P, 2, L])
        post = buf("post", [P, 2, D_MODEL])
        misc = buf("misc", [P, KC, 136])
        convp = buf("convp", [P, 4, TAPS + 3])
        qT = buf("qT", [P, 4, L])
        kT = buf("kT", [P, 4, L])
        zaT = buf("zaT", [P, 4, L])
        qiT = zaT
        kiT = buf("kiT", [P, L])
        V = buf("V", [P, TILES, 512])
        zcT = buf("zcT", [P, 4, L])
        uT = buf("uT", [P, 4, TAPS - 1 + L])
        yT = buf("yT", [P, 2 * 4, L])
        KEYS = [N_META + P * (t + 1) for t in range(XT)] + [N_META]
        score = [buf(f"score{t}", [P, DUMMIES + KEYS[t]]) for t in range(XT)]
        pr = buf("pr", [P, 4, L])
        prT = buf("prT", [P, 2, 4, P])
        prR = buf("prR", [N_META, 2, P])
        raw = buf("raw", [P, 2, L])
        first.close()


        second = ExitStack()
        buf = pool_of(second)
        aT = buf("aT", [P, KC, SEQ])
        attT = buf("attT", [P, 4, SEQ])
        gqk = buf("gqk", [P, 2, 4, SEQ])
        GV = buf("GV", [P, XT, D_MODEL])
        zT = buf("zT", [64, SEQ])
        up = buf("up", [64, 512])
        scope = ExitStack()
        buf = pool_of(scope)
        xn = buf("xn", [P, 2, D_MODEL])
        aqT = buf("aqT", [P, 4, SEQ])
        akT = buf("akT", [P, 2, SEQ])
        av = buf("av", [P, XT, P])
        pr2 = buf("pr2", [P, 4, 3 * P])
        pr2T = buf("pr2T", [P, 2, 3 * P])
        rope2 = buf("rope2", [P, 2, SEQ])
        raw2 = buf("raw2", [P, 2, SEQ])
        pos = buf("pos", [P, SEQ])
        angle = buf("angle", [P, SEQ])
        turns = buf("turns", [P, SEQ])
        scope.close()
        scope = ExitStack()
        buf = pool_of(scope)
        qB = buf("qB", [P, 4, SEQ])
        kE = buf("kE", [P, 2, XT, 512])
        AT = buf("AT", [P, XT, 4, P])
        O = buf("O", [P, XT, D_MODEL])
        S = buf("S", [P, 3, G_HEADS, G_DV])
        decay = [buf(n, [P, 4, P]) for n in ("cum", "exp_b", "k_t", "k_e")]
        gate = buf("gate", [P, 2, 512])
        squares = buf("squares", [P, 2, G_DV])
        zr = ([H[:, XT, 512 * a:512 * (a + 1)] for a in range(2)]
              + [b[:, :, :].rearrange("p h n -> p (h n)") for b in decay] + [gate[:, a, :] for a in range(2)])
        scope.close()
        scope = ExitStack()
        buf = pool_of(scope)
        side = buf("side", [P, 6, SEQ])
        scope.close()
        second.close()
        OT = gqk[:, :, :, :].rearrange("p a c n -> p (a c) n")
        mT = GV[:, :, :].rearrange("p t (a n) -> p (t a) n", a=2)

        third = ExitStack()
        buf = pool_of(third)
        MORE = 7
        ring_more = buf("ring_more", [P, MORE, KC, WCOLS])
        XN = buf("XN", [P, XT, D_MODEL])
        sel = buf("sel", [P, XT, EXPERTS * CAP])
        selw = buf("selw", [P, XT, P])
        GT = buf("GT", [P, SEQ])
        xe = buf("xe", [P, KC, P])
        Y = buf("Y", [P, D_MODEL])
        hid = buf("hid", [P, 2, 512])
        hidT = buf("hidT", [P, 4, P])
        final_g = buf("final_g", [P, D_MODEL])
        embedded = buf("embedded", [P, XT, D_MODEL])
        aT2 = ring_more[:, MORE - 2:MORE, :, :].rearrange("p s k n -> p (s k n)")\
            .rearrange("p (k n) -> p k n", k=KC)
        xn3 = XN[:, 0:2, :]
        outb = XN[:, 2:4, :]
        aT3 = sel[:, :, :].rearrange("p t n -> p (t n)").rearrange("p (k n) -> p k n", k=KC)
        sel_flat = sel[:, :, :].rearrange("p t n -> p (t n)")
        w_p = sel_flat[:, 0:2 * D_MODEL].rearrange("p (k n) -> p k n", k=PLE // P)
        pT = sel_flat[:, 2 * D_MODEL:2 * D_MODEL + 2 * SEQ].rearrange("p (k n) -> p k n", k=PLE // P)
        emb = Y[:, :].rearrange("p (a n) -> p a n", a=2)
        third.close()

        def few_at(a, n):
            return few[:, a:a + n]

        norm_sq, norm_std, norm_inv = few_at(0, 20), few_at(20, 20), few_at(40, 8)
        neg_max2, sum2, sink2, inv2, den2 = (few_at(64 + 32 * i, 32) for i in range(5))
        o_sq, o_std, o_inv = few_at(224, 16), few_at(240, 16), few_at(256, 16)
        dec = few_at(272, 64).rearrange("p (d t h c) -> p d t h c", d=2, t=XT, h=G_HEADS)
        soft = few_at(336, 12)
        logit = few_at(348, 64).rearrange("p (t e) -> p t e", t=XT)
        aff = few_at(412, 64).rearrange("p (t e) -> p t e", t=XT)
        mark = few_at(476, 64).rearrange("p (t e) -> p t e", t=XT)
        rank = few_at(540, 64).rearrange("p (t e) -> p t e", t=XT)
        max8 = few_at(604, 8)
        affT = hid[0:EXPERTS, 0, :]
        takenT = hid[0:EXPERTS, 1, :]
        rot2 = cst[:, 4, :]
        window = cst[:, 10:13, :].rearrange("p a n -> p (a n)")

        ps = top.enter_context(nc.psum_tensor("ps", [P, 8, 512], F32))

        wi = small[:, 0:32]
        wiT = pr[0:HEADS, 0, :]
        top8 = small[:, 32:64]
        neg_max = small[:, 64:104]
        row_sum = small[:, 104:144]
        row_inv = small[:, 144:184]
        stats = small[:, 184:196]
        mean_var = small[:, 196:206]
        ln_std_v = small[:, 206:211]
        ln_inv = small[:, 211:216]
        eps_ln = small[:, 216:217]
        eps_rms = small[:, 217:218]

        def rows_of(t):
            return (P, N_META + P * t) if t < XT else (N_META, 0)

        def halves(b):
            return b.rearrange("p (a n) -> p a n", a=2)

        def pair(p):
            return ps[:, 2 * p:2 * p + 2, 0:HALF]

        def span(b, banks, rows, n):
            if n <= 512:
                return b[0:rows, 0:n], ps[0:rows, banks, 0:n]
            return halves(b[0:rows, 0:n]), ps[0:rows, banks:banks + 2, 0:n // 2]

        consts_in = sem("consts_in")
        h_in = [sem(f"h_in{t}") for t in range(TILES)]
        turn_in = sem("turn_in")
        consts_set = sem("consts_set")
        params_in = sem("params_in")
        post_in = sem("post_in")
        slot_in = [sem(f"slot_in{s}") for s in range(SLOTS)]
        turned = sem("turned")
        turned_act = sem("turned_act")
        turned_dve = sem("turned_dve")
        proj_done = sem("proj_done")
        proj_out = sem("proj_out")
        rot_done = sem("rot_done")
        raw_used = sem("raw_used")
        idx_done = sem("idx_done")
        idx_relu = sem("idx_relu")
        idx_added = sem("idx_added")
        gated = sem("gated")
        conv_done = sem("conv_done")
        cn_mean = sem("cn_mean")
        cn_centred = sem("cn_centred")
        cn_square = sem("cn_square")
        cn_var = sem("cn_var")
        cn_std = sem("cn_std")
        cn_scaled = sem("cn_scaled")
        cn_silu = sem("cn_silu")
        conv_y = sem("conv_y")
        at_score = sem("at_score")
        at_masked = sem("at_masked")
        at_exp = sem("at_exp")
        at_prob = sem("at_prob")
        at_turned = sem("at_turned")
        at_full = sem("at_full")
        at_rest = sem("at_rest")
        at_value = sem("at_value")
        attn_y = sem("attn_y")
        wo_done = sem("wo_done")
        wo_added = sem("wo_added")
        ln_var = sem("ln_var")
        ln_std = sem("ln_std")
        h_done = sem("h_done")
        dve_step = sem("dve_step")
        pool_step = sem("pool_step")
        stored = [sem(f"stored{i}") for i in range(2)]

        ITEMS = ([("ki", 0)] + [("qi", c) for c in range(4)] + [("wi", 0), ("a", 0), ("wt", 0)] + [("a", c) for c in range(1, 4)]
                 + [("g", c) for c in range(4)] + [("q", c) for c in range(4)] + [("k", c) for c in range(4)]
                 + [("v", b) for b in range(TILES)] + [("zc", c) for c in range(4)] + [("za", c) for c in range(4)])
        NI = len(ITEMS)
        ITEM = {item: n for n, item in enumerate(ITEMS)}
        IDX_AFTER = ITEM[("a", 3)]
        GROUPS = [(COL, h) for COL in ("qi", "a", "g", "q", "k", "v", "zc", "za") for h in range(2)]
        NG = len(GROUPS) + D_MODEL // WCOLS
        COLS = dict(qi=COL_QI, a=COL_A, g=COL_G, q=COL_Q, k=COL_K, v=COL_V, zc=COL_ZC, za=COL_ZA)
        GROUP_END = [ITEM[(k, TILES - 1 if k == "v" else 2 * h + 1)] + 1 for k, h in GROUPS]
        ROPED = [n for n, (k, _) in enumerate(ITEMS) if k in ("ki", "qi", "q", "k")]
        RAW = [n for n, (k, _) in enumerate(ITEMS) if k in ("ki", "qi", "g", "q", "k")]
        NROT, NRAW, NIDX, NATT = len(ROPED), len(RAW), XT * HEADS, TILES * HEADS

        def rows256(n):
            return ring[:, n % SLOTS, :, :].rearrange("p k n -> p (k n)").rearrange("p (k n) -> p k n", k=2)

        def group_of(item):
            kind, c = ITEMS[item]
            return GROUPS.index((kind, c // 2))

        def att(j):
            t, h = divmod(j, HEADS)
            n, q0 = rows_of(t)
            return t, h, n, q0, KEYS[t], KEYS[t] // P

        passed = {e: sem(f"passed_{e}") for e in ("sp", "pe", "act", "pool", "dve")}

        def settle(engine, name):
            engine.sem_inc(passed[name], 1)


        second_in = sem("second_in")
        third_in = sem("third_in")
        more_in = [sem(f"more_in{s}") for s in range(MORE)]
        nq_done = sem("nq_done")
        ns_done = sem("ns_done")
        xn_done = sem("xn_done")
        nt_done = sem("nt_done")
        nt_out = sem("nt_out")
        rt_arg = sem("rt_arg")
        rt_sin = sem("rt_sin")
        z_ones = sem("z_ones")
        p2_done = sem("p2_done")
        p2_out = sem("p2_out")
        gv_done = sem("gv_done")
        gv_out = sem("gv_out")
        rot2_done = sem("rot2_done")
        raw2_used = sem("raw2_used")
        w_score = sem("w_score")
        w_masked = sem("w_masked")
        w_exp = sem("w_exp")
        w_sink = sem("w_sink")
        w_prob = sem("w_prob")
        w_turned = sem("w_turned")
        w_out_t = sem("w_out_t")
        w_value = sem("w_value")
        w_att = sem("w_att")
        gz_done = sem("gz_done")
        gl_log = sem("gl_log")
        gl_set = sem("gl_set")
        gl_cum = sem("gl_cum")
        gl_exp = sem("gl_exp")
        gl_rest = sem("gl_rest")
        gl_rexp = sem("gl_rexp")
        gl_qk = sem("gl_qk")
        gl_att = sem("gl_att")
        gl_mask = sem("gl_mask")
        gl_turn = sem("gl_turn")
        gl_kout = sem("gl_kout")
        gl_zero = sem("gl_zero")
        kv_done = sem("kv_done")
        st_done = sem("st_done")
        o_done = sem("o_done")
        o_out = sem("o_out")
        o_sqd = sem("o_sqd")
        o_stdd = sem("o_stdd")
        gr_done = sem("gr_done")
        gr_silu = sem("gr_silu")
        gr_out = sem("gr_out")
        mg_done = sem("mg_done")
        mg_sig = sem("mg_sig")
        mg_out = sem("mg_out")
        wo2_done = sem("wo2_done")
        wo2_out = sem("wo2_out")
        rl_done = sem("rl_done")
        rl_sub = sem("rl_sub")
        rl_exp = sem("rl_exp")
        aff_done = sem("aff_done")
        affT_done = sem("affT_done")
        mark_done = sem("mark_done")
        markT_done = sem("markT_done")
        mk_done = sem("mk_done")
        rank_done = sem("rank_done")
        sel_done = sem("sel_done")
        gather_done = sem("gather_done")
        selw_done = sem("selw_done")
        gt_done = sem("gt_done")
        gt_out = sem("gt_out")
        xe_set = sem("xe_set")
        e_gate = sem("e_gate")
        e_up = sem("e_up")
        e_silu = sem("e_silu")
        e_hid = sem("e_hid")
        e_turn = sem("e_turn")
        e_hidT = sem("e_hidT")
        e_down = sem("e_down")
        e_y = sem("e_y")
        e_y2 = sem("e_y2")
        cb_done = sem("cb_done")
        cb_out = sem("cb_out")
        em_done = sem("em_done")
        em_out = sem("em_out")
        pl_done = sem("pl_done")
        pl_sig = sem("pl_sig")
        pl_out = sem("pl_out")
        y_set = sem("y_set")
        act_step = sem("act_step")

        ITEMS2 = ([("ak", c) for c in range(2)] + [("av", 0), ("z", 0)] + [("aq", c) for c in range(4)]
                  + [("gq", c) for c in range(4)] + [("gk", c) for c in range(4)])
        WIN_FROM = 8
        NI2 = len(ITEMS2)
        AT2 = {item: n for n, item in enumerate(ITEMS2)}
        ROPED2 = [AT2[("ak", 0)], AT2[("ak", 1)]] + [AT2[("aq", c)] for c in range(4)]
        BEFORE = DEPTH * (NG // SLOTS)
        D_IN2 = COL2["gg"] + D_MODEL
        GROUPS2 = ([("m0", 0), ("m1", 0)] + [(g, c) for g in ("aq", "gq", "gk") for c in range(2)]
                   + [("gv", c) for c in range(4)] + [("gr", c) for c in range(4)]
                   + [(g, c) for c in range(4) for g in ("ga", "ba", "gg", "bg")]
                   + [("wo", c) for c in range(4)])
        NG2 = len(GROUPS2)
        G2 = {g: n for n, g in enumerate(GROUPS2)}

        def last_use(g):
            kind, c = g
            if kind in ("m0", "m1"):
                return p2_done, AT2[("ak", 1) if kind == "m0" else ("z", 0)] + 1
            if kind in ("aq", "gq", "gk"):
                return p2_done, AT2[(kind, 2 * c + 1)] + 1
            if kind == "gv":
                return gv_done, XT * (c // 2) + XT
            if kind == "gr":
                return gr_done, 2 * c + 2
            if kind == "wo":
                return wo2_done, 2 * XT
            return mg_done, 8 * c + 4 + ("ga", "ba", "gg", "bg").index(kind) + 1

        def win(j):
            t, h = divmod(j, HEADS)
            k0 = max(t - 1, 0)
            return t, h, k0, min(t + 1, XT - 1) - k0 + 1

        NW = XT * HEADS
        TD = [(t, d) for t in range(XT) for d in (1, 0)]
        SCAN = {1: [(t, c) for t in reversed(range(XT)) for c in (1, 0)], 0: [(t, c) for t in range(XT) for c in (0, 1)]}

        PLACES = [SLOTS, SLOTS + 1, SLOTS + 2, SLOTS + 3, SLOTS + 4, 0, 1, 2, 3, 4, SLOTS + 5, SLOTS + 6]

        sel_pair = sel[:, :, :].rearrange("p t (i n) -> p t i n", n=P)
        aff_pair = aff.rearrange("p t (i e) -> p t i e", e=2)

        def eslot(i):
            s = PLACES[i]
            b = ring[:, s, :, :] if s < SLOTS else ring_more[:, s - SLOTS, :, :]
            return b.rearrange("p k n -> p (k n)").rearrange("p (k n) -> p k n", k=2)

        def eslot_in(i):
            s = PLACES[i]
            return slot_in[s] if s < SLOTS else more_in[s - SLOTS]

        LOADED = [BEFORE + len(range(s, NG2, SLOTS)) if s < SLOTS else 0 for s in PLACES]

        block = top.enter_context(nc.Block())

        @block.sync
        def _(sp):
            sp.dma_start(cst[:, 0:4, :], cst_d[:, 0:4, :]).then_inc(turn_in, 16)
            for t in range(XT):
                sp.dma_start(H[:, t, :], x[P * t:P * (t + 1), :]).then_inc(h_in[t], 16)
            sp.dma_start(H[0:N_META, XT, :], meta).then_inc(h_in[XT], 16)

            with sp.Fori(0, DEPTH) as l:
                sp.wait_ge(wo_done, l * TILES * 2 + WO_FIRST)
                settle(sp, "sp")
                sp.dma_start(misc[:, :, :], w_misc_v[l]).then_inc(params_in, 16)
                sp.dma_start(convp[:, :, :], conv_p[l]).then_inc(params_in, 16)
                for n in range(NG):
                    if n >= SLOTS:
                        sp.wait_ge(proj_done, l * NI + GROUP_END[n - SLOTS])
                    if n == SLOTS:
                        settle(sp, "sp")
                        sp.dma_start(post[:, :, :], post_p[l]).then_inc(post_in, 16)
                    if n < len(GROUPS):
                        kind, h = GROUPS[n]
                        src = w_in_v[l, :, :, COLS[kind] + WCOLS * h:COLS[kind] + WCOLS * (h + 1)]
                    else:
                        m = n - len(GROUPS)
                        src = w_out_v[l, :, 2 * m:2 * m + 2, :]
                    if n > SLOTS:
                        settle(sp, "sp")
                    sp.dma_start(ring[:, n % SLOTS, :, :] if n < len(GROUPS) else rows256(n), src).then_inc(slot_in[n % SLOTS], 16)
            sp.wait_ge(h_done, TILES + DEPTH * TILES)
            sp.dma_start(up[:, :], B["up"]).then_inc(second_in, 16)
            sp.dma_start(pos[:, :].bitcast(I32), B["positions"]).then_inc(second_in, 16)
            for n, (kind, c) in enumerate(GROUPS2):
                if n == 0:
                    sp.wait_ge(proj_done, DEPTH * NI)
                elif n < SLOTS:
                    sp.wait_ge(wo_done, DEPTH * TILES * 2 + WO_FIRST)
                else:
                    sp.wait_ge(*last_use(GROUPS2[n - SLOTS]))
                slot = ring[:, n % SLOTS, :, :]
                if kind in ("m0", "m1"):
                    src = B["w_misc"][:, :, 0:WCOLS] if kind == "m0" else B["w_misc"][:, :, WCOLS:WCOLS + 192]
                    slot = slot if kind == "m0" else slot[:, :, 0:192]
                elif kind == "ba":
                    slot, src = slot[:, 0:4, :], B["w_ba"][:, :, WCOLS * c:WCOLS * (c + 1)]
                elif kind == "wo":
                    slot, src = rows256(n), B["w_wo"][:, 2 * c:2 * c + 2, :]
                elif kind == "bg":
                    src = B["w_" + kind][:, :, WCOLS * c:WCOLS * (c + 1)]
                else:
                    src = B["w_in"][:, :, COL2[kind] + WCOLS * c:COL2[kind] + WCOLS * (c + 1)]
                sp.dma_start(slot, src).then_inc(slot_in[n % SLOTS], 16)
                if kind == "ga" and c == 2:
                    sp.dma_start(w_p, B["w_p"]).then_inc(third_in, 16)
                    sp.dma_start(pT, B["pT"]).then_inc(third_in, 16)
                    sp.dma_start(final_g[:, :], B["final"].partition_broadcast(P)).then_inc(third_in, 16)
            with sp.Fori(0, EXPERTS) as e:
                for i in range(12):
                    sp.wait_ge((e_gate, e_up, e_down)[i // 4], e + 1)
                    settle(sp, "sp")
                    sp.dma_start(eslot(i), B["w_exp"][i // 4][e, :, 2 * (i % 4):2 * (i % 4) + 2, :])\
                        .then_inc(eslot_in(i), 16)
            sp.wait_ge(e_gate, EXPERTS + 1)
            for c in range(4):
                sp.dma_start(eslot(c), B["w_pg"][:, 2 * c:2 * c + 2, :]).then_inc(eslot_in(c), 16)
            for t in range(XT):
                sp.wait_ge(y_set, t + 1)
                sp.dma_start(out[P * t:P * (t + 1), :], outb[:, t % 2, :]).then_inc(stored[t % 2], 16)
            sp.wait_ge(stored[0], 16 * (XT // 2))
            sp.wait_ge(stored[1], 16 * (XT // 2))

        @block.tensor
        def _(pe):
            mm = nc.tensor.matmul

            def slot_ready(l, n):
                pe.wait_ge(slot_in[n % SLOTS], 16 * (l * (NG // SLOTS) + n // SLOTS + 1))

            def item(l, n):
                kind, c = ITEMS[n]
                p = n % 2
                if n >= 2:
                    pe.wait_ge(proj_out, l * NI + n - 1)
                if kind not in ("ki", "wi", "wt") and (c % 2 == 0 or kind == "v") and not (kind == "v" and c > 0):
                    slot_ready(l, group_of(n))
                    if kind == "v":
                        slot_ready(l, group_of(n) + 1)
                if kind == "wi":
                    for k in range(KC):
                        for a in range(2):
                            last = mm(ps[0:HEADS, 2 * p + a, 0:HALF], misc[:, k, P:P + HEADS],
                                      hT[:, k, HALF * a:HALF * (a + 1)], start=(k == 0), stop=(k == KC - 1))
                elif kind == "wt":
                    pe.wait_ge(proj_out, l * NI + ITEM[("wi", 0)] + 1)
                    settle(pe, "pe")
                    for t in range(XT):
                        q0 = rows_of(t)[1]
                        last = nc.tensor.transpose(ps[:, 2 * p, HEADS * t:HEADS * (t + 1)], wiT[:, q0:q0 + P],
                                                   ident[0:HEADS, 0:HEADS])
                elif kind == "v":
                    rows = min(P, L - P * c)
                    g = GROUPS.index(("v", 0))
                    for h in range(2):
                        for k in range(KC):
                            last = mm(ps[0:rows, 2 * p, WCOLS * h:WCOLS * (h + 1)], hT[:, k, P * c:P * c + rows],
                                      ring[:, (g + h) % SLOTS, k, :], start=(k == 0), stop=(k == KC - 1))
                else:
                    for k in range(KC):
                        if kind == "ki":
                            w = misc[:, k, 0:P]
                        else:
                            w = ring[:, group_of(n) % SLOTS, k, P * (c % 2):P * (c % 2 + 1)]
                        for a in range(2):
                            last = mm(ps[:, 2 * p + a, 0:HALF], w, hT[:, k, HALF * a:HALF * (a + 1)],
                                      start=(k == 0), stop=(k == KC - 1))
                last.then_inc(proj_done, 1)

            def rotate(l, r):
                n = ROPED[r]
                u = RAW.index(n)
                pe.wait_ge(proj_out, l * NI + n + 1)
                if r >= 2:
                    pe.wait_ge(raw_used, l * NRAW + RAW.index(ROPED[r - 2]) + 1)
                if r == 5:
                    pe.wait_ge(idx_relu, l * NIDX + NIDX)
                for a in range(2):
                    last = mm(ps[:, 4 + 2 * (r % 2) + a, 0:HALF], rot, raw[:, u % 2, HALF * a:HALF * (a + 1)],
                              start=True, stop=True)
                last.then_inc(rot_done, 1)

            def index_scores(l):
                pe.wait_ge(raw_used, l * NRAW + 5)
                for j in range(NIDX):
                    t, h = divmod(j, HEADS)
                    n, q0 = rows_of(t)
                    if j >= 2:
                        pe.wait_ge(idx_relu, l * NIDX + j - 1)
                    b0 = 64 * (h % 2)
                    for a in range(1 if KEYS[t] <= 512 else 2):
                        w = min(KEYS[t], 512) if KEYS[t] <= 512 else HALF
                        last = mm(ps[:, 4 + 2 * (j % 2) + a, 0:w], qiT[b0:b0 + 64, h // 2, q0:q0 + n],
                                  kiT[b0:b0 + 64, a * w:(a + 1) * w], start=True, stop=True)
                    last.then_inc(idx_done, 1)

            def at_scores(l, j):
                t, h, n, q0, keys, _ = att(j)
                if j >= 2:
                    pe.wait_ge(at_masked, l * NATT + j - 1)
                else:
                    pe.wait_ge(raw_used, l * NRAW + NRAW)
                settle(pe, "pe")
                b0 = 64 * (h % 2)
                for a in range(1 if keys <= 512 else 2):
                    w = keys if keys <= 512 else HALF
                    last = mm(ps[0:n, 4 + 2 * (j % 2) + a, 0:w], qT[b0:b0 + 64, h // 2, q0:q0 + n],
                              kT[b0:b0 + 64, h // 2, a * w:(a + 1) * w], start=True, stop=True)
                last.then_inc(at_score, 1)

            def at_turn(l, j):
                t, h, n, q0, keys, full = att(j)
                pe.wait_ge(at_prob, l * NATT + j + 1)
                if j == 0:
                    pe.wait_ge(proj_out, l * NI + NI)
                if 2 <= j < XT * HEADS:
                    pe.wait_ge(at_full, l * XT * HEADS + j - 1)
                if j >= 1:
                    pe.wait_ge(at_rest, l * NATT + j)
                settle(pe, "pe")
                for b in range(full):
                    nc.tensor.transpose(ps[:, j % 2, P * b:P * b + n], pr[0:n, j % 4, P * b:P * (b + 1)],
                                        ident[0:n, 0:n])
                nc.tensor.transpose(ps[0:N_META, 2, P * (j % 4):P * (j % 4) + n],
                                    pr[0:n, j % 4, P * full:P * full + N_META], ident[0:n, 0:n]).then_inc(at_turned, 1)

            def at_values(l, j):
                t, h, n, q0, keys, full = att(j)
                if full:
                    pe.wait_ge(at_full, l * XT * HEADS + j + 1)
                pe.wait_ge(at_rest, l * NATT + j + 1)
                if h == 0 and t > 0:
                    pe.wait_ge(attn_y, l * TILES + t)
                b0 = 64 * (h % 2)
                o = ps[b0:b0 + 64, 3, P * (h // 2):P * (h // 2) + n]
                for b in range(full):
                    mm(o, V[:, b, 64 * h:64 * (h + 1)], prT[:, j % 2, b, 0:n], start=(b == 0), stop=False)
                mm(o, V[0:N_META, full, 64 * h:64 * (h + 1)], prR[:, j % 2, 0:n], start=(full == 0),
                   stop=True).then_inc(at_value, 1)

            def out_product(l, t, ks):
                rows, q0 = rows_of(t)
                first, end = (4, 3) if t < 2 else (0, KC - 1)
                for a in range(2):
                    i = 2 * t + a
                    if i >= 4 and ks[0] == 0:
                        pe.wait_ge(wo_added, l * 2 * TILES + i - 3)
                    for k in ks:
                        last = mm(ps[0:rows, 4 + i % 4, :], yT[:, k, q0:q0 + rows],
                                  rows256(len(GROUPS) + k // 2)[:, k % 2, 512 * a:512 * (a + 1)],
                                  start=(k == first), stop=(k == end))
                    if end in ks:
                        last.then_inc(wo_done, 1)

            pe.sem_inc(wo_done, WO_FIRST)
            pe.wait_ge(turn_in, 16)
            with pe.Fori(0, DEPTH) as l:
                for t in range(TILES):
                    rows, _ = rows_of(t)
                    pe.wait_ge(h_done, l * TILES + t + 1)
                    settle(pe, "pe")
                    for hf, read in enumerate((turned_act, turned_dve)):
                        if t >= 2:
                            pe.wait_ge(read, l * TILES + t - 1)
                            settle(pe, "pe")
                        for c in range(4):
                            last = nc.tensor.transpose(
                                ps[:, 2 * (t % 2) + hf, P * c:P * c + rows],
                                H[0:rows, t, P * (4 * hf + c):P * (4 * hf + c + 1)], ident[0:rows, 0:rows])
                        last.then_inc(turned, 1)
                pe.wait_ge(turned_act, l * TILES + TILES)
                pe.wait_ge(turned_dve, l * TILES + TILES)
                pe.wait_ge(params_in, 32 * (l + 1))
                r = 0
                for n in range(NI):
                    item(l, n)
                    if n >= 1 and n - 1 in ROPED:
                        rotate(l, r)
                        r += 1
                    if n == IDX_AFTER:
                        index_scores(l)
                for j in range(NATT + 3):
                    if j < NATT:
                        at_scores(l, j)
                    if 2 <= j < NATT + 2:
                        at_turn(l, j - 2)
                    if j >= 3:
                        at_values(l, j - 3)
                pe.wait_ge(conv_done, 4 * l + 4)
                pe.wait_ge(attn_y, l * TILES + TILES)
                for a in range(2):
                    for c in range(4):
                        last = mm(ps[:, a, 0:HALF], mean_w, yT[:, c, HALF * a:HALF * (a + 1)],
                                  start=(c == 0), stop=(c == 3))
                last.then_inc(cn_mean, 1)
                for m in range(4):
                    slot_ready(l, len(GROUPS) + m)
                out_product(l, 0, range(4, KC))
                for c in range(4):
                    pe.wait_ge(cn_square, 4 * l + c + 1)
                    for a in range(2):
                        last = mm(ps[:, 2 + a, 0:HALF], mean_w, pr[:, c, HALF * a:HALF * (a + 1)],
                                  start=(c == 0), stop=(c == 3))
                last.then_inc(cn_var, 1)
                out_product(l, 1, range(4, KC))
                pe.wait_ge(conv_y, 4 * l + 4)
                out_product(l, 0, range(4))
                out_product(l, 1, range(4))
                for t in range(2, TILES):
                    out_product(l, t, range(KC))

            T = nc.tensor.transpose

            def slot2(kind, c):
                n = G2[(kind, c)]
                pe.wait_ge(slot_in[n % SLOTS], 16 * (BEFORE + n // SLOTS + 1))
                return ring[:, n % SLOTS, :, :]

            def turn_norm(w, src):
                for t in range(XT):
                    pe.wait_ge(xn_done, XT * w + t + 1)
                    for hf in range(2):
                        i = 2 * t + hf
                        if i >= 4:
                            pe.wait_ge(nt_out, 2 * XT * w + i - 3)
                        for c in range(4):
                            last = T(ps[:, 4 + i % 4, P * c:P * (c + 1)], src(t)[:, P * (4 * hf + c):P * (4 * hf + c + 1)],
                                     ident)
                        last.then_inc(nt_done, 1)
                pe.wait_ge(nt_out, 2 * XT * (w + 1))

            turn_norm(0, lambda t: xn[:, t % 2, :])

            def rotate2(r):
                n = ROPED2[r]
                pe.wait_ge(p2_out, n + 1)
                if r >= 2:
                    pe.wait_ge(raw2_used, r - 1)
                mm(ps[:, 4 + r % 2, :], rot2, raw2[:, r % 2, :], start=True, stop=True).then_inc(rot2_done, 1)

            def item2(n):
                kind, c = ITEMS2[n]
                if n >= 4:
                    pe.wait_ge(p2_out, n - 3)
                o = ps[:, n % 4, :]
                if kind == "ak":
                    w = slot2("m0", 0)[:, :, P * c:P * (c + 1)]
                elif kind in ("av", "z"):
                    w = slot2("m1", 0)
                else:
                    w = slot2(kind, c // 2)[:, :, P * (c % 2):P * (c % 2 + 1)]
                if kind == "av":
                    for t in range(XT):
                        for k in range(KC):
                            last = mm(o[:, P * t:P * (t + 1)], aT[:, k, P * t:P * (t + 1)], w[:, k, 0:P],
                                      start=(k == 0), stop=(k == KC - 1))
                elif kind == "z":
                    for k in range(KC):
                        last = mm(o[0:64, :], w[:, k, P:P + 64], aT[:, k, :], start=(k == 0), stop=(k == KC - 1))
                else:
                    for k in range(KC):
                        last = mm(o, w[:, k, :], aT[:, k, :], start=(k == 0), stop=(k == KC - 1))
                last.then_inc(p2_done, 1)

            for n in range(WIN_FROM):
                item2(n)
                if n - 1 in ROPED2:
                    rotate2(ROPED2.index(n - 1))
            rotate2(ROPED2.index(WIN_FROM - 1))

            def item2_quarter(n, part):
                kind, c = ITEMS2[n]
                if part == 0:
                    pe.wait_ge(p2_out, n - 1)
                w = slot2(kind, c // 2)[:, :, P * (c % 2):P * (c % 2 + 1)]
                for k in (2 * part, 2 * part + 1):
                    last = mm(ps[:, 2 + n % 2, :], w[:, k, :], aT[:, k, :], start=(k == 0), stop=(k == KC - 1))
                if part == 3:
                    last.then_inc(p2_done, 1)

            def w_scores(j):
                t, h, k0, cnt = win(j)
                pe.wait_ge(w_masked, j - 1) if j >= 2 else pe.wait_ge(raw2_used, len(ROPED2))
                b0 = 64 * (h % 2)
                mm(ps[:, 4 + j % 2, 0:P * cnt], aqT[b0:b0 + 64, h // 2, P * t:P * (t + 1)],
                   akT[b0:b0 + 64, h // 4, P * k0:P * (k0 + cnt)], start=True, stop=True).then_inc(w_score, 1)

            def w_turn(j):
                t, h, k0, cnt = win(j)
                pe.wait_ge(w_prob, j + 1)
                if j >= 2:
                    pe.wait_ge(w_out_t, j - 1)
                for b in range(cnt):
                    last = T(ps[:, 6 + j % 2, P * b:P * (b + 1)], pr2[:, j % 4, P * b:P * (b + 1)], ident)
                last.then_inc(w_turned, 1)

            def w_values(j):
                t, h, k0, cnt = win(j)
                pe.wait_ge(w_out_t, j + 1)
                if h == 0 and t >= 2:
                    pe.wait_ge(w_att, t - 1)
                if j == 0:
                    pe.wait_ge(p2_out, WIN_FROM)
                b0 = 64 * (h % 2)
                for b in range(cnt):
                    last = mm(ps[b0:b0 + 64, t % 2, P * (h // 2):P * (h // 2 + 1)], av[:, k0 + b, 64 * (h // 4):64 * (h // 4 + 1)],
                              pr2T[:, j % 2, P * b:P * (b + 1)], start=(b == 0), stop=(b == cnt - 1))
                last.then_inc(w_value, 1)

            for j in range(NW + 3):
                if j < NW:
                    w_scores(j)
                if 2 <= j < NW + 2:
                    w_turn(j - 2)
                if j >= 3:
                    w_values(j - 3)
                if j < NW:
                    item2_quarter(WIN_FROM + j // 4, j % 4)

            pe.wait_ge(w_att, XT)

            def gate_z(i):
                t, d = TD[i]
                if i >= 1:
                    pe.wait_ge(gl_set, i)
                if i == 0:
                    pe.wait_ge(second_in, 32)
                mm(ps[:, 0, :], zT[32 * d:32 * d + 17, P * t:P * (t + 1)], up[32 * d:32 * d + 17, :],
                   start=True, stop=True).then_inc(gz_done, 1)

            def gate_sums(i):
                t, d = TD[i]
                pe.wait_ge(gl_set, i + 1)
                if i >= 2:
                    pe.wait_ge(gl_exp, i - 1)
                for h in range(G_HEADS):
                    last = mm(ps[:, 2 + i % 2, P * h:P * (h + 1)], gate[:, 1, P * h:P * (h + 1)], cst[:, 7 + d, :],
                              start=True, stop=True)
                last.then_inc(gl_cum, 1)

            def gate_scores(i):
                t, d = TD[i]
                q = qB if d else gqk[:, 0, :, :]
                pe.wait_ge(gl_qk, i + 1)
                if i >= 2:
                    pe.wait_ge(gl_mask, i - 1)
                for h in range(G_HEADS):
                    last = mm(ps[:, 4 + i % 2, P * h:P * (h + 1)], decay[2][:, h, :], q[:, h, P * t:P * (t + 1)],
                              start=True, stop=True)
                last.then_inc(gl_att, 1)
                if i >= 2:
                    pe.wait_ge(gl_kout, i - 1)
                for h in range(G_HEADS):
                    last = T(ps[:, 6 + i % 2, P * h:P * (h + 1)], decay[3][:, h, :], ident)
                last.then_inc(gl_turn, 1)

            def values_item(i):
                half, t = divmod(i, XT)
                if i >= 1:
                    pe.wait_ge(gv_out, i)
                for a in range(2):
                    w = slot2("gv", 2 * half + a)
                    for k in range(KC):
                        last = mm(ps[:, 1, WCOLS * a:WCOLS * (a + 1)], aT[:, k, P * t:P * (t + 1)], w[:, k, :],
                                  start=(k == 0), stop=(k == KC - 1))
                last.then_inc(gv_done, 1)

            gate_z(0)
            pe.wait_ge(p2_out, NI2)
            for i in range(len(TD)):
                gate_sums(i)
                if i + 1 < len(TD):
                    gate_z(i + 1)
                values_item(i)
                gate_scores(i)

            def gr_item(c):
                w = slot2("gr", c // 2)
                if c >= 2:
                    pe.wait_ge(gr_silu, c - 1)
                for k in range(KC):
                    last = mm(ps[:, 6 + c % 2, :], w[:, k, P * (c % 2):P * (c % 2 + 1)], aT[:, k, :],
                              start=(k == 0), stop=(k == KC - 1))
                last.then_inc(gr_done, 1)

            pe.wait_ge(gl_mask, len(TD))
            pe.wait_ge(gl_kout, len(TD))
            pe.wait_ge(gv_out, 2 * XT)
            for rnd, d in enumerate((1, 0)):
                q = qB if d else gqk[:, 0, :, :]

                def state(s):
                    t, c = SCAN[d][s]
                    if 7 * rnd + s >= 2:
                        pe.wait_ge(st_done, 7 * rnd + s - 1)
                    b0 = CHUNK * c
                    for h in range(G_HEADS):
                        last = mm(ps[:, 2 * ((7 * rnd + s) % 2) + h // 2, G_DV * (h % 2):G_DV * (h % 2 + 1)],
                                  kE[b0:b0 + CHUNK, d, t, P * h:P * (h + 1)],
                                  GV[b0:b0 + CHUNK, t, G_DV * h:G_DV * (h + 1)], start=True, stop=True)
                    last.then_inc(kv_done, 1)

                state(0)
                state(1)
                for i in range(XT):
                    for s in (2 * i + 2, 2 * i + 3):
                        if s < 7:
                            state(s)
                    t = SCAN[d][2 * i][0]
                    n = XT * rnd + i
                    pe.wait_ge(st_done, 7 * rnd + 2 * i + 1)
                    if n >= 1:
                        pe.wait_ge(o_out, n)
                    for h in range(G_HEADS):
                        o = ps[:, 4 + h // 2, G_DV * (h % 2):G_DV * (h % 2 + 1)]
                        if d == 0:
                            mm(o, AT[:, t, h, :], GV[:, t, G_DV * h:G_DV * (h + 1)], start=True, stop=False)
                        for s in (2 * i, 2 * i + 1):
                            c = SCAN[d][s][1]
                            q0 = P * t + CHUNK * c
                            last = mm(o[CHUNK * c:CHUNK * (c + 1), :], q[:, h, q0:q0 + CHUNK], S[:, s % 3, h, :],
                                      start=(d == 1), stop=True)
                    last.then_inc(o_done, 1)
                    gr_item(n)

            pe.wait_ge(o_out, 2 * XT)
            pe.wait_ge(gr_silu, KC)
            turn_norm(1, lambda t: O[:, t, :])
            pe.wait_ge(gr_out, KC)
            for c in range(KC):
                for m, kind in enumerate(("ga", "ba", "gg", "bg")):
                    if c >= 2:
                        pe.wait_ge(*((mg_sig, 2 * (c - 2) + m // 2 + 1) if m % 2 == 0
                                     else (mg_out, 2 * (c - 2) + m // 2 + 1)))
                    w = slot2(kind, c // 2)
                    src = dict(ga=aT, gg=aT, ba=attT, bg=OT)[kind]
                    nk = 4 if kind == "ba" else KC
                    for k in range(nk):
                        last = mm(ps[:, 4 * (c % 2) + m, :], w[:, k, P * (c % 2):P * (c % 2 + 1)], src[:, k, :],
                                  start=(k == 0), stop=(k == nk - 1))
                    last.then_inc(mg_done, 1)
            pe.wait_ge(mg_out, 2 * KC)
            pe.sem_inc(e_gate, 1)
            for c in range(4):
                slot2("wo", c)
            for i in range(2 * XT):
                t, a = divmod(i, 2)
                if i >= 4:
                    pe.wait_ge(wo2_out, i - 3)
                for k in range(KC):
                    last = mm(ps[:, i % 4, :], mT[:, k, P * t:P * (t + 1)],
                              rows256(G2[("wo", k // 2)])[:, k % 2, 512 * a:512 * (a + 1)],
                              start=(k == 0), stop=(k == KC - 1))
                last.then_inc(wo2_done, 1)

            turn_norm(2, lambda t: XN[:, t, :])
            pe.wait_ge(wo2_out, 2 * XT)
            pe.sem_inc(e_up, 1)
            for t in range(XT):
                for k in range(KC):
                    last = mm(ps[:, 0, EXPERTS * t:EXPERTS * (t + 1)], aT2[:, k, P * t:P * (t + 1)], router[:, k, :],
                              start=(k == 0), stop=(k == KC - 1))
            last.then_inc(rl_done, 1)
            pe.wait_ge(aff_done, 1)
            pe.sem_inc(e_down, 1)
            for t in range(XT):
                last = T(ps[0:EXPERTS, 1, P * t:P * (t + 1)], aff[:, t, :], ident)
            last.then_inc(affT_done, 1)
            pe.wait_ge(third_in, 48)
            for n in range(2 * XT):
                t, a = divmod(n, 2)
                if n >= 4:
                    pe.wait_ge(em_out, n - 3)
                for k in range(PLE // P):
                    last = mm(ps[:, 4 + n % 4, :], pT[:, k, P * t:P * (t + 1)], w_p[:, k, 512 * a:512 * (a + 1)],
                              start=(k == 0), stop=(k == PLE // P - 1))
                last.then_inc(em_done, 1)
            pe.wait_ge(mark_done, 1)
            for t in range(XT):
                last = T(ps[:, 2, EXPERTS * t:EXPERTS * (t + 1)], takenT[:, P * t:P * (t + 1)],
                         ident[0:EXPERTS, 0:EXPERTS])
            last.then_inc(markT_done, 1)
            pe.wait_ge(mk_done, 1)
            for t in range(XT):
                for s in range(t + 1):
                    last = mm(ps[:, 3, EXPERTS * t:EXPERTS * (t + 1)], ones if s < t else cst[:, 13, :], mark[:, s, :],
                              start=(s == 0), stop=(s == t))
            last.then_inc(rank_done, 1)
            def gather(i):
                for c in range(KC):
                    for t in range(XT):
                        last = mm(ps[:, c // 4, P * (c % 4):P * (c % 4 + 1)], XN[:, t, P * c:P * (c + 1)],
                                  sel_pair[:, t, i, :], start=(t == 0), stop=(t == XT - 1))
                    if c % 4 == 3:
                        last.then_inc(gather_done, 1)

            def experts(i):
                for u in range(2):
                    if u == 0:
                        pe.wait_ge(xe_set, 2 * i + 2)
                    for m, (bank, done) in enumerate(((u, e_gate), (2 + u, e_up))):
                        if u == 0 and m == 1:
                            pe.wait_ge(selw_done, XT * i + XT)
                        for b in range(4):
                            pe.wait_ge(eslot_in(4 * m + b), 32 * i + 16 * (LOADED[4 * m + b] + u + 1))
                            settle(pe, "pe")
                            for k in (2 * b, 2 * b + 1):
                                for x_ in range(2):
                                    last = mm(ps[64 * x_:64 * x_ + 64, bank, :], xe[:, k, CAP * u:CAP * (u + 1)],
                                              eslot(4 * m + b)[:, k % 2, 512 * x_:512 * (x_ + 1)],
                                              start=(k == 0), stop=(k == KC - 1))
                        last.then_inc(done, 1)
                    if u == 0:
                        for t in range(XT):
                            last = T(ps[:, 7, P * t:P * (t + 1)], selw[:, t, :], ident)
                        last.then_inc(gt_done, 1)
                    pe.wait_ge(e_hid, 2 * i + u + 1)
                    for c in range(4):
                        last = T(ps[:, 4, P * c:P * (c + 1)], hid[:, u, P * c:P * (c + 1)], ident)
                    last.then_inc(e_turn, 1)
                    pe.wait_ge(e_hidT, 2 * i + u + 1)
                    for b in range(4):
                        pe.wait_ge(eslot_in(8 + b), 32 * i + 16 * (LOADED[8 + b] + u + 1))
                        settle(pe, "pe")
                        for k in (2 * b, 2 * b + 1):
                            for x_ in range(2):
                                last = mm(ps[64 * x_:64 * x_ + 64, 5 + u, :],
                                          hidT[:, k % 4, 64 * (k // 4):64 * (k // 4 + 1)],
                                          eslot(8 + b)[:, k % 2, 512 * x_:512 * (x_ + 1)],
                                          start=(k == 0), stop=(k == KC - 1))
                    last.then_inc(e_down, 1)

            def combine(i):
                pe.wait_ge(e_y, 2 * i + 2)
                pe.wait_ge(e_y2, 2 * i + 2)
                pe.wait_ge(gt_out, i + 1)
                for n in range(2 * XT):
                    t, a = divmod(n, 2)
                    if n >= 4:
                        pe.wait_ge(cb_out, 2 * XT * i + n - 3)
                        settle(pe, "pe")
                    mm(ps[:, (2, 3, 4, 7)[n % 4], :], GT[:, P * t:P * (t + 1)], Y[:, 512 * a:512 * (a + 1)],
                       start=True, stop=True).then_inc(cb_done, 1)

            pe.wait_ge(sel_done, XT)
            pe.wait_ge(em_out, 2 * XT)
            gather(0)
            with pe.Fori(0, PAIRS - 1) as i:
                experts(i)
                gather(i + 1)
                combine(i)
            experts(PAIRS - 1)
            combine(PAIRS - 1)
            turn_norm(3, lambda t: xn3[:, t % 2, :])
            pe.wait_ge(cb_out, 2 * XT * PAIRS)
            for c in range(4):
                pe.wait_ge(eslot_in(c), 16 * (LOADED[c] + EXPERTS + 1))
            for n in range(2 * XT):
                t, a = divmod(n, 2)
                if n >= 4:
                    pe.wait_ge(pl_out, n - 3)
                for k in range(KC):
                    last = mm(ps[:, n % 4, :], aT3[:, k, P * t:P * (t + 1)], eslot(k // 2)[:, k % 2, 512 * a:512 * (a + 1)],
                       start=(k == 0), stop=(k == KC - 1))
                last.then_inc(pl_done, 1)

        @block.scalar
        def _(act):
            A = nc.scalar.activation
            act.wait_ge(consts_set, 1)
            act.dma_start(rope[:, :, :], rope_d).then_inc(consts_in, 16)
            act.dma_start(cst[:, 4:NC, :], cst_d[:, 4:NC, :]).then_inc(consts_in, 16)
            act.dma_start(gains[:, :, :], B["gains"]).then_inc(consts_in, 16)
            act.dma_start(router[:, :, :], B["router"]).then_inc(consts_in, 16)
            act.dma_start(sink[:, 0, :], B["sink"].partition_broadcast(P)).then_inc(consts_in, 16)
            with act.Fori(0, DEPTH) as l:
                for t in range(TILES):
                    rows, q0 = rows_of(t)
                    act.wait_ge(turned, 2 * (l * TILES + t) + 1)
                    A(hT[:, 0:4, q0:q0 + rows],
                      ps[:, 2 * (t % 2), :].rearrange("p (c n) -> p c n", c=4)[:, :, 0:rows],
                      ACT.Copy).then_inc(turned_act, 1)

                def item(n):
                    kind, c = ITEMS[n]
                    act.wait_ge(proj_done, l * NI + n + 1)
                    src = pair(n % 2)
                    if n in RAW:
                        u = RAW.index(n)
                        if u >= 2:
                            act.wait_ge(raw_used, l * NRAW + u - 1)
                        A(halves(raw[:, u % 2, :]), src,
                          ACT.Sigmoid if kind == "g" else ACT.Copy).then_inc(proj_out, 1)
                    elif kind == "wi":
                        A(halves(wiT), src[0:HEADS], ACT.Copy, scale=float(HEADS ** -0.5)).then_inc(proj_out, 1)
                    elif kind == "wt":
                        A(wi, ps[:, 2 * (n % 2), 0:32], ACT.Copy).then_inc(proj_out, 1)
                    elif kind == "a":
                        A(halves(uT[:, c, TAPS - 1:TAPS - 1 + L]), src, ACT.Copy).then_inc(proj_out, 1)
                    elif kind == "v":
                        rows = min(P, L - P * c)
                        A(V[0:rows, c, :], ps[0:rows, 2 * (n % 2), :], ACT.Copy).then_inc(proj_out, 1)
                    else:
                        A(halves((zcT if kind == "zc" else zaT)[:, c, :]), src, ACT.Silu).then_inc(proj_out, 1)

                for n in range(NI):
                    item(n)
                    if n == IDX_AFTER:
                        for j in range(NIDX):
                            t = j // HEADS
                            act.wait_ge(idx_done, l * NIDX + j + 1)
                            if j >= 4:
                                act.wait_ge(idx_added, l * NIDX + j - 3)
                            dst, src = span(pr[:, j % 4, :], 4 + 2 * (j % 2), P, KEYS[t])
                            A(dst, src, ACT.Relu, scale=HEAD_DIM ** -0.5).then_inc(idx_relu, 1)
                for j in range(NATT + 2):
                    if j < NATT:
                        t, h, n, q0, keys, full = att(j)
                        act.wait_ge(at_masked, l * NATT + j + 1)
                        A(pr[0:n, j % 4, 0:keys], pr[0:n, j % 4, 0:keys], ACT.Exp, bias=neg_max[0:n, j:j + 1],
                          scale=-1.0, accum_out=row_sum[0:n, j:j + 1]).then_inc(at_exp, 1)
                    i = j - 2
                    if i >= 0 and att(i)[5]:
                        full = att(i)[5]
                        act.wait_ge(at_turned, l * NATT + i + 1)
                        if i >= 2:
                            act.wait_ge(at_value, l * NATT + i - 1)
                        A(prT[:, i % 2, 0:full, :], ps[:, i % 2, 0:P * full].rearrange("p (b n) -> p b n", n=P),
                          ACT.Copy).then_inc(at_full, 1)
                for c in range(4):
                    act.wait_ge(cn_centred, 4 * l + c + 1)
                    A(pr[:, c, :], yT[:, c, :], ACT.Square).then_inc(cn_square, 1)
                act.wait_ge(cn_var, l + 1)
                A(halves(raw[:, 0, :]), pair(1), ACT.Sqrt, bias=eps_ln).then_inc(cn_std, 1)
                for c in range(4):
                    act.wait_ge(cn_scaled, 4 * l + c + 1)
                    A(yT[:, c, :], yT[:, c, :], ACT.Silu, bias=convp[:, c, TAPS + 2:TAPS + 3],
                      scale=convp[:, c, TAPS + 1:TAPS + 2]).then_inc(cn_silu, 1)
                for t in range(TILES):
                    rows, _ = rows_of(t)
                    act.wait_ge(ln_var, l * TILES + t + 1)
                    A(ln_std_v[0:rows, t:t + 1], mean_var[0:rows, 2 * t + 1:2 * t + 2], ACT.Sqrt,
                      bias=eps_ln[0:rows, :]).then_inc(ln_std, 1)

            steps = Steps()

            def norm_square(w, t, scratch, src):
                A(scratch, src, ACT.Square, accum_out=norm_sq[:, XT * w + t:XT * w + t + 1]).then_inc(nq_done, 1)
                act.wait_ge(nq_done, XT * w + t + 1)
                A(norm_std[:, XT * w + t:XT * w + t + 1], norm_sq[:, XT * w + t:XT * w + t + 1], ACT.Sqrt,
                  bias=eps_rms, scale=1.0 / D_MODEL).then_inc(ns_done, 1)

            for t in range(XT):
                act.wait_ge(h_done, DEPTH * TILES + t + 1)
                if t >= 2:
                    act.wait_ge(nt_done, 2 * (t - 1))
                norm_square(0, t, xn[:, t % 2, :], H[:, t, :])
            act.wait_ge(rt_arg, 1)
            A(rope2[:, 1, :], angle[:, :], ACT.Sin).then_inc(rt_sin, 1)
            A(rope2[:, 0, :], turns[:, :], ACT.Sin, bias=cst[:, 14, 65:66]).then_inc(rt_sin, 1)
            def item2_out(n):
                kind, c = ITEMS2[n]
                act.wait_ge(p2_done, n + 1)
                src = ps[:, n % 4, :]
                if n in ROPED2:
                    r = ROPED2.index(n)
                    if r >= 2:
                        act.wait_ge(raw2_used, r - 1)
                    A(raw2[:, r % 2, :], src, ACT.Copy).then_inc(p2_out, 1)
                elif kind == "av":
                    A(av[:, :, :], src.rearrange("p (t n) -> p t n", t=XT), ACT.Copy).then_inc(p2_out, 1)
                elif kind == "z":
                    A(zT[:, :], src[0:64, :], ACT.Identity, bias=cst[0:64, 14, 66:67]).then_inc(p2_out, 1)
                else:
                    g = 0 if kind == "gq" else 1
                    A(gqk[:, g, c, :], ps[:, 2 + n % 2, :], ACT.Copy,
                      scale=G_DK ** -0.5 if g == 0 else 1.0).then_inc(p2_out, 1)

            for n in range(WIN_FROM):
                item2_out(n)
            for j in range(NW + 2):
                if j % 4 == 0 and 4 <= j <= NW:
                    item2_out(WIN_FROM + j // 4 - 1)
                if j < NW:
                    t, h, k0, cnt = win(j)
                    act.wait_ge(w_masked, j + 1)
                    A(pr2[:, j % 4, 0:P * cnt], pr2[:, j % 4, 0:P * cnt], ACT.Exp, bias=neg_max2[:, j:j + 1],
                      scale=-1.0, accum_out=sum2[:, j:j + 1]).then_inc(w_exp, 1)
                    A(sink2[:, j:j + 1], sink[:, 0, h:h + 1], ACT.Exp, bias=neg_max2[:, j:j + 1])\
                        .then_inc(w_sink, 1)
                i = j - 2
                if i >= 0:
                    act.wait_ge(w_turned, i + 1)
                    if i >= 2:
                        act.wait_ge(w_value, i - 1)
                    n = P * win(i)[3]
                    A(pr2T[:, i % 2, 0:n], ps[:, 6 + i % 2, 0:n], ACT.Copy).then_inc(w_out_t, 1)

            def gate_log(i):
                act.wait_ge(gz_done, i + 1)
                if i >= 1:
                    act.wait_ge(gl_set, i)
                else:
                    act.wait_ge(w_att, XT)
                g = gate[:, 0, :]
                A(g, ps[:, 0, :], ACT.Abs).then_inc(act_step, steps.one())
                act.wait_ge(act_step, steps.now())
                A(g, g, ACT.Exp, scale=-1.0).then_inc(act_step, steps.one())
                act.wait_ge(act_step, steps.now())
                A(g, g, ACT.Ln, bias=ones[:, 0:1]).then_inc(gl_log, 1)

            def flat(b):
                return b[:, :, :].rearrange("p h n -> p (h n)")

            def gate_exp(i):
                act.wait_ge(gl_cum, i + 1)
                if i >= 1:
                    act.wait_ge(gl_qk, i)
                    act.wait_ge(gl_att, i)
                src = ps[:, 2 + i % 2, :]
                A(flat(decay[0]), src, ACT.Copy).then_inc(act_step, steps.one())
                A(flat(decay[1]), src, ACT.Exp).then_inc(act_step, steps.one())
                A(flat(decay[2]), src, ACT.Exp, scale=-1.0).then_inc(gl_exp, 1)

            gate_log(0)
            for i in range(len(TD)):
                gate_exp(i)
                act.wait_ge(gl_rest, i + 1)
                A(flat(decay[3]), flat(decay[3]), ACT.Exp).then_inc(gl_rexp, 1)
                if i + 1 < len(TD):
                    gate_log(i + 1)
                act.wait_ge(gl_turn, i + 1)
                t, d = TD[i]
                A(kE[:, d, t, :], ps[:, 6 + i % 2, :], ACT.Copy).then_inc(gl_kout, 1)
            for c in range(KC):
                act.wait_ge(gr_done, c + 1)
                A(zr[c], ps[:, 6 + c % 2, :], ACT.Silu).then_inc(gr_silu, 1)
                n = c - XT
                if n >= 0:
                    act.wait_ge(o_out, XT + n + 1)
                    for h in range(G_HEADS):
                        A(squares[:, h % 2, :], O[:, n, G_DV * h:G_DV * (h + 1)], ACT.Square,
                          accum_out=o_sq[:, 4 * n + h:4 * n + h + 1]).then_inc(o_sqd, 1)
                        act.wait_ge(o_sqd, 4 * n + h + 1)
                    A(o_std[:, 4 * n:4 * n + 4], o_sq[:, 4 * n:4 * n + 4], ACT.Sqrt, bias=eps_rms, scale=1.0 / G_DV)\
                        .then_inc(o_stdd, 1)
            for c in range(KC):
                for m in range(2):
                    i = 2 * c + m
                    act.wait_ge(mg_done, 4 * c + 2 * m + 1)
                    if c >= 2:
                        act.wait_ge(mg_out, i - 3)
                    A(side[:, 2 + i % 4, :], ps[:, 4 * (c % 2) + 2 * m, :], ACT.Sigmoid).then_inc(mg_sig, 1)
            for t in range(XT):
                act.wait_ge(wo2_out, 2 * (t + 1))
                norm_square(1, t, XN[:, t, :], H[:, t, :])
            act.wait_ge(rl_sub, 1)
            A(logit, logit, ACT.Exp).then_inc(rl_exp, 1)
            for n in range(2 * XT):
                act.wait_ge(em_done, n + 1)
                A(embedded[:, n // 2, 512 * (n % 2):512 * (n % 2 + 1)], ps[:, 4 + n % 4, :], ACT.Copy).then_inc(em_out, 1)
            with act.Fori(0, PAIRS) as i:
                for u in range(2):
                    act.wait_ge(e_gate, 2 * i + u + 2)
                    A(hid[:, u, :], ps[:, u, :], ACT.Silu).then_inc(e_silu, 1)
                    act.wait_ge(e_turn, 2 * i + u + 1)
                    A(hidT[:, :, :], ps[:, 4, :].rearrange("p (c n) -> p c n", c=4), ACT.Copy).then_inc(e_hidT, 1)
                    act.wait_ge(e_down, 2 * i + u + 2)
                    A(Y[64 * u:64 * u + 64, 512:1024], ps[64:128, 5 + u, :], ACT.Copy).then_inc(e_y2, 1)
            for t in range(XT):
                act.wait_ge(cb_out, 2 * XT * (PAIRS - 1) + 2 * (t + 1))
                if t >= 2:
                    act.wait_ge(nt_done, 6 * XT + 2 * (t - 1))
                norm_square(2, t, xn3[:, t % 2, :], H[:, t, :])
            for i in range(2 * XT):
                act.wait_ge(pl_done, i + 1)
                if i >= 2:
                    act.wait_ge(pl_out, i - 1)
                A(emb[:, i % 2, :], ps[:, i % 4, :], ACT.Sigmoid).then_inc(pl_sig, 1)
            for t in range(XT):
                act.wait_ge(pl_out, 2 * (t + 1))
                if t >= 2:
                    act.wait_ge(stored[t % 2], 16 * (t // 2))
                norm_square(3, t, outb[:, t % 2, :], H[:, t, :])

        @block.gpsimd
        def _(pool):
            nc.gpsimd.memset(uT[:, :, 0:TAPS - 1], 0.0).then_inc(pool_step, 1)

            pool.wait_ge(w_att, XT)
            nc.gpsimd.memset(AT[:, :, :, :], 0.0).then_inc(gl_zero, 1)

        @block.vector
        def _(dve):
            V_ = nc.vector
            nc.vector.memset(small[:, :], 0.0).then_inc(dve_step, 1)
            dve.wait_ge(dve_step, 1)
            nc.vector.memset(eps_rms, RMS_EPS).then_inc(dve_step, 1)
            nc.vector.memset(eps_ln, LN_EPS).then_inc(consts_set, 1)
            dve.wait_ge(consts_set, 1)
            for t in range(TILES):
                dve.wait_ge(h_in[t], 16)
                dve.sem_inc(h_done, 1)
            dve.wait_ge(pool_step, 1)
            STEPS1 = 361
            with dve.Fori(0, DEPTH) as l:
                k = Steps(l * STEPS1 + 2)
                for t in range(TILES):
                    rows, q0 = rows_of(t)
                    dve.wait_ge(turned, 2 * (l * TILES + t) + 2)
                    V_.tensor_copy(hT[:, 4:8, q0:q0 + rows],
                                   ps[:, 1 + 2 * (t % 2), :].rearrange("p (c n) -> p c n", c=4)[:, :, 0:rows])\
                        .then_inc(turned_dve, 1)

                def rope_item(r):
                    n = ROPED[r]
                    kind, c = ITEMS[n]
                    if r == 0:
                        dve.wait_ge(consts_in, 80)
                    raw_r = raw[:, RAW.index(n) % 2, :]
                    dst = kiT[:, :] if kind == "ki" else dict(qi=qiT, q=qT, k=kT)[kind][:, c, :]
                    dve.wait_ge(rot_done, l * NROT + r + 1)
                    V_.tensor_tensor(halves(dst), pair(2 + r % 2), halves(rope[:, 1, :]), ALU.mult)\
                        .then_inc(dve_step, k.one())
                    V_.tensor_tensor(raw_r, raw_r, rope[:, 0, :], ALU.mult).then_inc(dve_step, k.one())
                    dve.wait_ge(dve_step, k.now())
                    V_.tensor_tensor(dst, dst, raw_r, ALU.add).then_inc(raw_used, 1)

                def gate_item(c):
                    n = ITEM[("g", c)]
                    dve.wait_ge(proj_out, l * NI + n + 1)
                    V_.tensor_tensor(uT[:, c, TAPS - 1:TAPS - 1 + L], uT[:, c, TAPS - 1:TAPS - 1 + L],
                                     raw[:, RAW.index(n) % 2, :], ALU.mult).then_inc(raw_used, 1)
                    if c == 3:
                        dve.wait_ge(raw_used, l * NRAW + RAW.index(n) + 1)
                        V_.memset(small[:, 500:501], 0.0).then_inc(gated, 4)

                for r in range(5):
                    rope_item(r)
                for t in range(XT):
                    V_.memset(score[t][:, 0:DUMMIES], DUMMY_SCORE).then_inc(dve_step, k.one())
                for j in range(NIDX):
                    t, h = divmod(j, HEADS)
                    s = score[t][:, DUMMIES:]
                    r_ = pr[:, j % 4, 0:KEYS[t]]
                    w = wi[:, 8 * t + h:8 * t + h + 1]
                    dve.wait_ge(idx_relu, l * NIDX + j + 1)
                    if h == 0:
                        V_.tensor_scalar(s, r_, w, None, ALU.mult).then_inc(idx_added, 1)
                    else:
                        dve.wait_ge(idx_added, l * NIDX + j)
                        V_.scalar_tensor_tensor(out=s, in0=r_, scalar=w, in1=s, op0=ALU.mult, op1=ALU.add)\
                            .then_inc(idx_added, 1)
                    if h == HEADS - 1:
                        dve.wait_ge(idx_added, l * NIDX + j + 1)
                        d = score[t][:, DUMMIES + N_META + P * t:]
                        V_.tensor_tensor(d, d, future_score, ALU.add).then_inc(dve_step, k.one())

                def top_round():
                    dve.wait_ge(dve_step, k.now())
                    settle(dve, "dve")
                    for t in range(XT):
                        V_.max(top8[:, 8 * t:8 * t + 8], score[t][:, :]).then_inc(dve_step, k.one())
                    for t in range(XT):
                        dve.wait_ge(dve_step, k.now() - XT + 1)
                        settle(dve, "dve")
                        V_.match_replace(score[t][:, :], top8[:, 8 * t:8 * t + 8], score[t][:, :], TAKEN)\
                            .then_inc(dve_step, k.one())

                conv_marks = {}

                def conv_taps(first, end):
                    for u in range(first, end):
                        j, c = divmod(u, 4)
                        done = (conv_done, 1) if j == TAPS - 1 else (dve_step, k.one())
                        if j == 0:
                            V_.tensor_scalar(yT[:, c, :], uT[:, c, 0:L], convp[:, c, 0:1],
                                             convp[:, c, TAPS:TAPS + 1], ALU.mult, ALU.add).then_inc(*done)
                        else:
                            dve.wait_ge(dve_step, k.at(conv_marks[c]))
                            V_.scalar_tensor_tensor(out=yT[:, c, :], in0=uT[:, c, j:j + L],
                                                    scalar=convp[:, c, j:j + 1], in1=yT[:, c, :],
                                                    op0=ALU.mult, op1=ALU.add).then_inc(*done)
                        conv_marks[c] = k.n

                dve.wait_ge(params_in, 32 * (l + 1))
                rounds = 0
                for n in range(NI):
                    kind, c = ITEMS[n]
                    if kind == "g":
                        gate_item(c)
                    elif kind in ("q", "k"):
                        rope_item(ROPED.index(n))
                    else:
                        continue
                    for _ in range(2):
                        if rounds < ROUNDS:
                            top_round()
                            rounds += 1
                while rounds < ROUNDS:
                    top_round()
                    rounds += 1
                dve.wait_ge(dve_step, k.now())
                for t in range(XT):
                    V_.tensor_scalar(score[t][:, :], score[t][:, :], TAKEN, HIDDEN, ALU.not_equal, ALU.mult)\
                        .then_inc(dve_step, k.one())
                dve.wait_ge(dve_step, k.now())
                d = score[0][:, DUMMIES + N_META:]
                V_.tensor_tensor(d, d, future_hidden, ALU.add).then_inc(dve_step, k.one())

                conv_taps(0, 4 * TAPS)

                def masked(j):
                    t, h, n, q0, keys, _ = att(j)
                    dve.wait_ge(at_score, l * NATT + j + 1)
                    if j >= 4:
                        dve.wait_ge(at_turned, l * NATT + j - 3)
                    if j == 0:
                        dve.wait_ge(dve_step, k.now())
                    dst, src = span(pr[:, j % 4, :], 4 + 2 * (j % 2), n, keys)
                    m = score[t][0:n, DUMMIES:] if t < XT else future_hidden[0:n, 0:N_META]
                    if keys > 512:
                        m = halves(m)
                    settle(dve, "dve")
                    V_.tensor_tensor_reduce(dst, src, m, -(HEAD_DIM ** -0.5), 3.0e38, ALU.add, ALU.min,
                                            neg_max[0:n, j:j + 1]).then_inc(at_masked, 1)

                def scaled(j):
                    t, h, n, q0, keys, _ = att(j)
                    dve.wait_ge(at_exp, l * NATT + j + 1)
                    V_.reciprocal(row_inv[0:n, j:j + 1], row_sum[0:n, j:j + 1]).then_inc(dve_step, k.one())
                    dve.wait_ge(dve_step, k.now())
                    V_.tensor_scalar(pr[0:n, j % 4, 0:keys], pr[0:n, j % 4, 0:keys], row_inv[0:n, j:j + 1], None,
                                     ALU.mult).then_inc(at_prob, 1)

                def rest(j):
                    n = att(j)[2]
                    dve.wait_ge(at_turned, l * NATT + j + 1)
                    if j >= 2:
                        dve.wait_ge(at_value, l * NATT + j - 1)
                    V_.tensor_copy(prR[:, j % 2, 0:n], ps[0:N_META, 2, P * (j % 4):P * (j % 4) + n])\
                        .then_inc(at_rest, 1)

                for j in range(NATT + 4):
                    if j < NATT:
                        masked(j)
                    if 1 <= j <= NATT:
                        scaled(j - 1)
                    if 2 <= j < NATT + 2:
                        rest(j - 2)
                    if j >= 4 and (j - 4) % HEADS == HEADS - 1:
                        t = (j - 4) // HEADS
                        n, q0 = rows_of(t)
                        dve.wait_ge(at_value, l * NATT + HEADS * (t + 1))
                        dve.wait_ge(proj_out, l * NI + NI)
                        V_.tensor_tensor(yT[:, 4:8, q0:q0 + n],
                                         ps[:, 3, :].rearrange("p (c n) -> p c n", c=4)[:, :, 0:n],
                                         zaT[:, :, q0:q0 + n], ALU.mult).then_inc(attn_y, 1)

                dve.wait_ge(cn_mean, l + 1)
                for c in range(4):
                    V_.tensor_tensor(halves(yT[:, c, :]), halves(yT[:, c, :]), pair(0), ALU.subtract)\
                        .then_inc(cn_centred, 1)
                dve.wait_ge(cn_std, l + 1)
                V_.reciprocal(raw[:, 1, :], raw[:, 0, :]).then_inc(dve_step, k.one())
                dve.wait_ge(dve_step, k.now())
                for c in range(4):
                    V_.tensor_tensor(yT[:, c, :], yT[:, c, :], raw[:, 1, :], ALU.mult).then_inc(cn_scaled, 1)
                for c in range(4):
                    dve.wait_ge(cn_silu, 4 * l + c + 1)
                    V_.tensor_tensor(yT[:, c, :], yT[:, c, :], zcT[:, c, :], ALU.mult).then_inc(conv_y, 1)
                for t in range(TILES):
                    rows, _ = rows_of(t)
                    ht = H[0:rows, t, :]
                    for m in range(2):
                        i = 2 * t + m
                        hm = H[0:rows, t, 512 * m:512 * (m + 1)]
                        dve.wait_ge(wo_done, l * 2 * TILES + i + 1 + WO_FIRST)
                        V_.scalar_tensor_tensor(out=hm, in0=hm, scalar=ALPHA, in1=ps[0:rows, 4 + i % 4, :],
                                                op0=ALU.mult, op1=ALU.add).then_inc(wo_added, 1)
                    dve.wait_ge(wo_added, l * 2 * TILES + 2 * t + 2)
                    for a in range(2):
                        V_.bn_stats(stats[0:rows, 6 * a:6 * a + 6], H[0:rows, t, 512 * a:512 * (a + 1)])\
                            .then_inc(dve_step, k.one())
                    dve.wait_ge(dve_step, k.now())
                    settle(dve, "dve")
                    V_.bn_aggr(mean_var[0:rows, 2 * t:2 * t + 2], stats[0:rows, :]).then_inc(ln_var, 1)
                    dve.wait_ge(ln_std, l * TILES + t + 1)
                    V_.reciprocal(ln_inv[0:rows, t:t + 1], ln_std_v[0:rows, t:t + 1]).then_inc(dve_step, k.one())
                    dve.wait_ge(dve_step, k.now())
                    V_.tensor_scalar(ht, ht, mean_var[0:rows, 2 * t:2 * t + 1], ln_inv[0:rows, t:t + 1],
                                     ALU.subtract, ALU.mult).then_inc(dve_step, k.one())
                    dve.wait_ge(dve_step, k.now())
                    if t == 0:
                        dve.wait_ge(post_in, 16 * (l + 1))
                    V_.tensor_tensor(ht, ht, post[0:rows, 0, :], ALU.mult).then_inc(dve_step, k.one())
                    dve.wait_ge(dve_step, k.now())
                    V_.tensor_tensor(ht, ht, post[0:rows, 1, :], ALU.add).then_inc(h_done, 1)
                assert k.n == STEPS1, k.n

            k = Steps(DEPTH * STEPS1 + 2)
            TT, TS, STT = V_.tensor_tensor, V_.tensor_scalar, V_.scalar_tensor_tensor

            def step(instruction):
                instruction.then_inc(dve_step, k.one())
                dve.wait_ge(dve_step, k.now())

            def norm_scale(w, v, t, dst, src):
                dve.wait_ge(ns_done, XT * w + t + 1)
                inv = norm_inv[:, t:t + 1]
                step(V_.reciprocal(inv, norm_std[:, XT * w + t:XT * w + t + 1]))
                TS(dst, src, inv, None, ALU.mult).then_inc(xn_done if v is not None else dve_step,
                                                           1 if v is not None else k.one())

            def norm_out(v, dst, t):
                for hf in range(2):
                    dve.wait_ge(nt_done, 2 * XT * v + 2 * t + hf + 1)
                    TT(dst[:, 4 * hf:4 * hf + 4, P * t:P * (t + 1)],
                       ps[:, 4 + (2 * t + hf) % 4, :].rearrange("p (c n) -> p c n", c=4),
                       gains[:, v, 4 * hf:4 * hf + 4].unsqueeze(2).to_broadcast([P, 4, P]), ALU.mult)\
                        .then_inc(nt_out, 1)

            dve.wait_ge(h_done, TILES + DEPTH * TILES)
            TS(sink[:, 1, :], sink[:, 0, :], -1.0, None, ALU.mult).then_inc(dve_step, k.one())
            for t in range(XT):
                norm_scale(0, 0, t, xn[:, t % 2, :], H[:, t, :])
                norm_out(0, aT, t)
            dve.wait_ge(second_in, 32)
            step(V_.tensor_copy(pos[:, :], pos[:, :].bitcast(I32)))
            step(TS(angle[:, :], pos[:, :], cst[:, 14, 64:65], None, ALU.mult))
            step(TS(turns[:, :], angle[:, :], float(0.5 / np.pi), FAR, ALU.mult, ALU.add))
            step(TS(turns[:, :], turns[:, :], -FAR, None, ALU.add))
            for part in TURN:
                step(STT(out=angle[:, :], in0=turns[:, :], scalar=-part, in1=angle[:, :], op0=ALU.mult, op1=ALU.add))
            step(TS(angle[:, :], angle[:, :], 3.1415925, -3.1415925, ALU.min, ALU.max))
            dve.wait_ge(dve_step, k.now())
            STT(out=turns[:, :], in0=angle[:, :], scalar=-1.0, in1=angle[:, :], op0=ALU.mult, op1=ALU.min).then_inc(rt_arg, 1)
            dve.wait_ge(rt_sin, 2)
            for r, n in enumerate(ROPED2):
                kind, c = ITEMS2[n]
                dst = (akT if kind == "ak" else aqT)[:, c, :]
                dve.wait_ge(rot2_done, r + 1)
                TT(dst, ps[:, 4 + r % 2, :], rope2[:, 1, :], ALU.mult).then_inc(dve_step, k.one())
                step(TT(raw2[:, r % 2, :], raw2[:, r % 2, :], rope2[:, 0, :], ALU.mult))
                TT(dst, dst, raw2[:, r % 2, :], ALU.add).then_inc(raw2_used, 1)

            for j in range(NW + 4):
                if j < NW:
                    t, h, k0, cnt = win(j)
                    dve.wait_ge(w_score, j + 1)
                    if j >= 4:
                        dve.wait_ge(w_turned, j - 3)
                    m0 = P * (k0 - t + 1)
                    V_.tensor_tensor_reduce(pr2[:, j % 4, 0:P * cnt], ps[:, 4 + j % 2, 0:P * cnt],
                                            window[:, m0:m0 + P * cnt], -(HEAD_DIM ** -0.5), sink[:, 1, h:h + 1],
                                            ALU.add, ALU.min, neg_max2[:, j:j + 1]).then_inc(w_masked, 1)
                i = j - 1
                if 0 <= i < NW:
                    n = P * win(i)[3]
                    dve.wait_ge(w_exp, i + 1)
                    dve.wait_ge(w_sink, i + 1)
                    step(TT(den2[:, i:i + 1], sum2[:, i:i + 1], sink2[:, i:i + 1], ALU.add))
                    step(V_.reciprocal(inv2[:, i:i + 1], den2[:, i:i + 1]))
                    TS(pr2[:, i % 4, 0:n], pr2[:, i % 4, 0:n], inv2[:, i:i + 1], None, ALU.mult).then_inc(w_prob, 1)
                if j >= 4 and (j - 4) % HEADS == HEADS - 1:
                    t = (j - 4) // HEADS
                    dve.wait_ge(w_value, HEADS * (t + 1))
                    V_.tensor_copy(attT[:, :, P * t:P * (t + 1)], ps[:, t % 2, :].rearrange("p (c n) -> p c n", c=4))\
                        .then_inc(w_att, 1)

            def gate_set(i):
                dve.wait_ge(gl_log, i + 1)
                if i >= 1:
                    dve.wait_ge(gl_cum, i)
                STT(out=gate[:, 1, :], in0=ps[:, 0, :], scalar=0.0, in1=gate[:, 0, :], op0=ALU.min,
                    op1=ALU.subtract).then_inc(gl_set, 1)

            gate_set(0)
            for i, (t, d) in enumerate(TD):
                dve.wait_ge(gl_exp, i + 1)
                if i >= 1:
                    dve.wait_ge(gl_turn, i)
                edge = 0 if d else CHUNK - 1
                b = decay[0][:, :, :].rearrange("p h (c n) -> p (h c) n", c=2)
                TT(decay[3][:, :, :].rearrange("p h (c n) -> p (h c) n", c=2),
                   b[:, :, edge:edge + 1].to_broadcast([P, 8, CHUNK]), b, ALU.subtract).then_inc(gl_rest, 1)
                V_.tensor_copy(dec[:, d, t, :, :],
                               decay[1][:, :, :].rearrange("p h (c n) -> p h c n", c=2)[:, :, :, edge])\
                    .then_inc(dve_step, k.one())
                q = gqk[:, 0, :, P * t:P * (t + 1)]
                kk = gqk[:, 1, :, P * t:P * (t + 1)]
                TT(qB[:, :, P * t:P * (t + 1)] if d else q, q, decay[1][:, :, :], ALU.mult)\
                    .then_inc(dve_step, k.one())
                TT(decay[2][:, :, :], kk, decay[2][:, :, :], ALU.mult).then_inc(dve_step, k.one())
                dve.wait_ge(gl_rexp, i + 1)
                TT(decay[3][:, :, :], kk, decay[3][:, :, :], ALU.mult).then_inc(gl_qk, 1)
                if i + 1 < len(TD):
                    gate_set(i + 1)
                half, tv = divmod(i, XT)
                dve.wait_ge(gv_done, i + 1)
                V_.tensor_copy(GV[:, tv, 512 * half:512 * (half + 1)], ps[:, 1, :]).then_inc(gv_out, 1)
                dve.wait_ge(gl_att, i + 1)
                dve.wait_ge(gl_zero, 1)
                if i >= 1:
                    dve.wait_ge(gl_mask, i)
                V_.copy_predicated(AT[:, t, :, :],
                                   cst[:, 9 if d else 7, :].bitcast(U32).unsqueeze(1).to_broadcast([P, 4, P]),
                                   ps[:, 4 + i % 2, :].rearrange("p (h n) -> p h n", h=4)).then_inc(gl_mask, 1)
            for rnd, d in enumerate((1, 0)):
                if rnd:
                    dve.wait_ge(o_done, XT)
                step(V_.memset(S[:, 0, :, :], 0.0))

                def update(s):
                    t, c = SCAN[d][s]
                    dve.wait_ge(kv_done, 7 * rnd + s + 1)
                    if s >= 1:
                        dve.wait_ge(st_done, 7 * rnd + s)
                    if s >= 2:
                        dve.wait_ge(o_done, XT * rnd + (s - 2) // 2 + 1)
                    for h in range(G_HEADS):
                        last = STT(out=S[:, (s + 1) % 3, h, :], in0=S[:, s % 3, h, :], scalar=dec[:, d, t, h, c:c + 1],
                                   in1=ps[:, 2 * ((7 * rnd + s) % 2) + h // 2, G_DV * (h % 2):G_DV * (h % 2 + 1)],
                                   op0=ALU.mult, op1=ALU.add)
                        if h == G_HEADS - 1:
                            last.then_inc(st_done, 1)

                def output(i):
                    t = SCAN[d][2 * i][0]
                    n = XT * rnd + i
                    dve.wait_ge(o_done, n + 1)
                    src = ps[:, 4:6, :]
                    dst = O[:, t, :].rearrange("p (a n) -> p a n", a=2)
                    if d:
                        V_.tensor_copy(dst, src).then_inc(o_out, 1)
                    else:
                        TT(dst, src, dst, ALU.add).then_inc(o_out, 1)

                for s in range(7):
                    if s >= 2 and s % 2 == 0:
                        output(s // 2 - 1)
                    update(s)
                output(3)

            for t in range(XT):
                dve.wait_ge(o_stdd, t + 1)
                step(V_.reciprocal(o_inv[:, 4 * t:4 * t + 4], o_std[:, 4 * t:4 * t + 4]))
                for h in range(G_HEADS):
                    o = O[:, t, G_DV * h:G_DV * (h + 1)]
                    last = TS(o, o, o_inv[:, 4 * t + h:4 * t + h + 1], None, ALU.mult)
                last.then_inc(xn_done, 1)
                if t >= 1:
                    norm_out(1, OT, t - 1)
            norm_out(1, OT, XT - 1)
            dve.wait_ge(nt_out, 4 * XT)
            for c in range(KC):
                dve.wait_ge(gr_silu, c + 1)
                TT(OT[:, c, :], OT[:, c, :], zr[c], ALU.mult).then_inc(gr_out, 1)
            for c in range(KC):
                for m in range(2):
                    i = 2 * c + m
                    dve.wait_ge(mg_sig, i + 1)
                    dve.wait_ge(mg_done, 4 * c + 2 * m + 2)
                    s = side[:, 2 + i % 4, :]
                    y = ps[:, 4 * (c % 2) + 2 * m + 1, :]
                    if m == 0:
                        TT(mT[:, c, :], s, y, ALU.mult).then_inc(mg_out, 1)
                    else:
                        step(TT(s, s, y, ALU.mult))
                        TT(mT[:, c, :], mT[:, c, :], s, ALU.add).then_inc(mg_out, 1)
            for t in range(XT):
                for m in range(2):
                    i = 2 * t + m
                    hm = H[:, t, 512 * m:512 * (m + 1)]
                    dve.wait_ge(wo2_done, i + 1)
                    TT(hm, hm, ps[:, i % 4, :], ALU.add).then_inc(wo2_out, 1)
                norm_scale(1, 2, t, XN[:, t, :], H[:, t, :])
            for t in range(XT):
                norm_out(2, aT2, t)

            dve.wait_ge(rl_done, 1)
            lg = ps[:, 0, 0:EXPERTS * XT].rearrange("p (t e) -> p t e", t=XT)

            def wide(v):
                return v.unsqueeze(2).to_broadcast([P, XT, EXPERTS])

            step(V_.tensor_reduce(soft[:, 0:4], lg, AX.X, ALU.max))
            TT(logit, lg, wide(soft[:, 0:4]), ALU.subtract).then_inc(rl_sub, 1)
            dve.wait_ge(rl_exp, 1)
            step(V_.tensor_reduce(soft[:, 4:8], logit, AX.X, ALU.add))
            step(V_.reciprocal(soft[:, 8:12], soft[:, 4:8]))
            TT(aff, logit, wide(soft[:, 8:12]), ALU.mult).then_inc(aff_done, 1)
            dve.wait_ge(affT_done, 1)
            step(V_.tensor_copy(affT, ps[0:EXPERTS, 1, :]))
            for _ in range(CAP // 8):
                step(V_.max(max8[0:EXPERTS, :], affT))
                step(V_.match_replace(affT, max8[0:EXPERTS, :], affT, TAKEN_AFF))
            TS(takenT, affT, TAKEN_AFF, None, ALU.is_equal).then_inc(mark_done, 1)
            dve.wait_ge(markT_done, 1)
            V_.tensor_copy(mark, ps[:, 2, 0:EXPERTS * XT].rearrange("p (t e) -> p t e", t=XT)).then_inc(mk_done, 1)
            dve.wait_ge(rank_done, 1)
            dve.wait_ge(mk_done, 1)
            step(TT(rank, ps[:, 3, 0:EXPERTS * XT].rearrange("p (t e) -> p t e", t=XT), mark, ALU.mult))
            step(TS(rank, rank, -1.0, None, ALU.add))
            slots = cst[:, 14, 0:CAP].unsqueeze(1).to_broadcast([P, EXPERTS, CAP])
            dve.wait_ge(em_done, 2 * XT)
            for t in range(XT):
                TT(sel[:, t, :].rearrange("p (e c) -> p e c", c=CAP), slots,
                   rank[:, t, :].unsqueeze(2).to_broadcast([P, EXPERTS, CAP]), ALU.is_equal).then_inc(sel_done, 1)
            dve.wait_ge(sel_done, XT)

            def gathered(i):
                for hf in range(2):
                    dve.wait_ge(gather_done, 2 * i + hf + 1)
                    TT(xe[:, 4 * hf:4 * hf + 4, :], ps[:, hf, :].rearrange("p (c n) -> p c n", c=4),
                       gains[:, 2, 4 * hf:4 * hf + 4].unsqueeze(2).to_broadcast([P, 4, P]), ALU.mult).then_inc(xe_set, 1)

            def paired(i):
                for t in range(XT):
                    TT(selw[:, t, :].rearrange("p (e c) -> p e c", c=CAP),
                       sel_pair[:, t, i, :].rearrange("p (e c) -> p e c", c=CAP),
                       aff_pair[:, t, i, :].unsqueeze(2).to_broadcast([P, 2, CAP]), ALU.mult).then_inc(selw_done, 1)
                for u in range(2):
                    dve.wait_ge(e_silu, 2 * i + u + 1)
                    dve.wait_ge(e_up, 2 * i + u + 2)
                    TT(hid[:, u, :], hid[:, u, :], ps[:, 2 + u, :], ALU.mult).then_inc(e_hid, 1)
                    if u == 0:
                        dve.wait_ge(gt_done, i + 1)
                        V_.tensor_copy(GT[:, :], ps[:, 7, :]).then_inc(gt_out, 1)
                    dve.wait_ge(e_down, 2 * i + u + 2)
                    V_.tensor_copy(Y[64 * u:64 * u + 64, 0:512], ps[0:64, 5 + u, :]).then_inc(e_y, 1)

            def combined(i):
                for n in range(2 * XT):
                    t, a = divmod(n, 2)
                    hm = H[:, t, 512 * a:512 * (a + 1)]
                    dve.wait_ge(cb_done, 2 * XT * i + n + 1)
                    TT(hm, hm, ps[:, (2, 3, 4, 7)[n % 4], :], ALU.add).then_inc(cb_out, 1)

            gathered(0)
            with dve.Fori(0, PAIRS - 1) as i:
                paired(i)
                gathered(i + 1)
                combined(i)
            paired(PAIRS - 1)
            combined(PAIRS - 1)
            for t in range(XT):
                norm_scale(2, 3, t, xn3[:, t % 2, :], H[:, t, :])
                if t >= 1:
                    norm_out(3, aT3, t - 1)
            norm_out(3, aT3, XT - 1)
            dve.wait_ge(third_in, 48)
            dve.wait_ge(em_out, 2 * XT)
            for t in range(XT):
                for m in range(2):
                    i = 2 * t + m
                    hm = H[:, t, 512 * m:512 * (m + 1)]
                    e = emb[:, i % 2, :]
                    dve.wait_ge(pl_sig, i + 1)
                    step(TT(e, e, embedded[:, t, 512 * m:512 * (m + 1)], ALU.mult))
                    TT(hm, hm, e, ALU.add).then_inc(pl_out, 1)
            for t in range(XT):
                norm_scale(3, None, t, outb[:, t % 2, :], H[:, t, :])
                dve.wait_ge(dve_step, k.now())
                TT(outb[:, t % 2, :], outb[:, t % 2, :], final_g[:, :], ALU.mult).then_inc(y_set, 1)


def kernel(**inputs):
    import concourse.bacc as bacc
    from concourse.bass_utils import run_bass_kernel_spmd

    g = {n: np.asarray(v) for n, v in inputs.items()}
    nc = bacc.Bacc("TRN2", target_bir_lowering=False, num_devices=1)
    arrays = {}

    def dram(name, a):
        a = np.ascontiguousarray(a)
        arrays[f"in_{name}"] = a
        return nc.dram_tensor(f"in_{name}", a.shape, mybir.dt.from_np(a.dtype), kind="ExternalInput").ap()

    def chunked(name, a):
        return dram(name, a).rearrange("(k p) n -> p k n", p=P)

    w_in, w2 = g["w_in"], g["w_in_2"][0]
    ki = w_in[:, :, COL_KI:COL_WI]
    w_misc = np.concatenate([ki, ki, w_in[:, :, COL_WI:]], -1)
    conv = np.concatenate([g["conv_w"], g["conv_b"][:, None], g["conv_ln_g"][:, None], g["conv_ln_b"][:, None]], 1)
    conv = conv.transpose(0, 2, 1).reshape(DEPTH, 4, P, TAPS + 3).transpose(0, 2, 1, 3)
    post = np.broadcast_to(np.stack([g["post_ln_g"], g["post_ln_b"]], 1)[:, None], (DEPTH, P, 2, D_MODEL))
    cst, rope = constants()
    pad = np.zeros((D_MODEL, 16), np.float32)
    kv = [w2[:, 512 + 64 * i:512 + 64 * (i + 1)] for i in range(2)]
    misc2 = np.concatenate([kv[0], kv[0], kv[1], kv[1], w2[:, 640:768], w2[:, 3840:3856], pad, w2[:, 3856:3872], pad], 1)
    up = np.zeros((64, 512), np.float32)
    for d, n in enumerate(("fwd", "bwd")):
        up[32 * d:32 * d + 16] = g[f"gla_gate_up_{n}_2"][0]
        up[32 * d + 16] = g[f"gla_gate_bias_{n}_2"][0]
    gains = np.stack([g[n][0].reshape(KC, P).T for n in ("norm_mix_2", "gla_norm_2", "norm_ffn_2", "norm_ple_2")], 1)
    B = dict(
        up=dram("up", up), positions=dram("positions", g["positions_2"][0]).partition_broadcast(P),
        gains=dram("gains", gains), router=chunked("router", g["w_router_2"][0]), sink=dram("sink", g["attn_sink_2"][0]),
        w_misc=chunked("w_misc2", misc2), w_in=chunked("w_in2", w2), w_ba=chunked("w_ba", g["w_branch_attn_2"][0]),
        w_bg=chunked("w_bg", g["w_branch_gla_2"][0]), w_wo=chunked("w_wo", g["w_out_2"][0]),
        w_exp=[dram(f"exp_{n}", g[f"w_exp_{n}_2"][0]).rearrange("e (k p) n -> e p k n", p=P)
               for n in ("gate", "up", "down")],
        final=dram("final", g["norm_final_2"]), pT=chunked("pT", g["p_2"][0, 0].T),
        w_pg=chunked("w_pg", g["w_ple_gate_2"][0]), w_p=chunked("w_p", g["w_ple_2"][0]))
    out = nc.dram_tensor("out_0", (SEQ, D_MODEL), mybir.dt.float32, kind="ExternalOutput").ap()
    hybrid_kernel(nc, dram("x", g["x"][0]), dram("meta", g["meta_tokens"]), dram("w_in1", w_in), dram("w_misc", w_misc),
                  dram("conv", conv), dram("w_out", g["w_out"]), dram("post", post), dram("cst", cst), dram("rope", rope),
                  B, out)
    r = run_bass_kernel_spmd(nc, [arrays], core_ids=[0])
    return r.results[0]["out_0"][None]
```

```python
import numpy as np
import concourse.bass as bass
from concourse import mybir
from contextlib import ExitStack

P = 128
D_MODEL, SEQ, DEPTH, N_META = 1024, 512, 2, 16
L = SEQ + N_META
HALF = L // 2
KC = D_MODEL // P
D_CONV, TAPS = 512, 31
HEADS, HEAD_DIM = 8, 64
TOPK = min(256, L // 4)
DUMMIES = -TOPK % 8
ROUNDS = (TOPK + DUMMIES) // 8
ALPHA = (2.0 * DEPTH) ** 0.25
LN_EPS, RMS_EPS = 1e-5, 1e-6
COL_A, COL_G, COL_ZC, COL_Q, COL_K, COL_V, COL_ZA, COL_QI, COL_KI, COL_WI = (
    0, 512, 1024, 1536, 2048, 2560, 3072, 3584, 4096, 4160)
DUMMY_SCORE, FUTURE_SCORE, TAKEN = 3.0e38, -3.0e38, float(np.float32(-3.3e38))
HIDDEN = -1.0e30
XT = SEQ // P
TILES = XT + 1
ORDER = (0, 1, XT, 2, 3)
Q4 = 4
WCOLS = 256
SLOTS = 5
NC = 14


def constants():
    i = np.arange(P)
    c = np.zeros((NC, P, P), np.float32)
    c[0] = np.eye(P)
    c[1] = 1.0
    c[2] = 1.0 / D_CONV
    for base in (0, 64):
        for d in range(32):
            c[3][base + d + 32, base + d] = -1.0
            c[3][base + d, base + d + 32] = 1.0
        for d in range(8):
            c[4][base + d + 8, base + d] = -1.0
            c[4][base + d, base + d + 8] = 1.0
    later = i[None, :] > i[:, None]
    c[5] = np.where(later, FUTURE_SCORE, 0.0)
    c[6] = np.where(later, HIDDEN, 0.0)
    same = (i[:, None] // 64) == (i[None, :] // 64)
    c[7] = (same & (i[:, None] <= i[None, :])) / 16.0
    c[8] = (same & (i[:, None] >= i[None, :])) / 16.0
    c[9] = (same & (i[:, None] > i[None, :]))
    c[10] = np.where(i[None, :] >= i[:, None], 0.0, HIDDEN)
    c[12] = np.where(i[None, :] <= i[:, None], 0.0, HIDDEN)
    c[13][:, 0:64] = i[None, 0:64]
    inv2 = (np.float32(500000.0) ** (-np.arange(0, 16, 2, dtype=np.float32) / np.float32(16))).astype(np.float32)
    for base in (0, 64):
        c[13][base:base + 16, 64] = np.tile(inv2, 2)
    c[13][:, 65] = np.pi / 2
    c[13][[16, 48], 66] = 1.0
    inv = (np.float32(10000.0) ** (-np.arange(0, 64, 2, dtype=np.float32) / np.float32(64))).astype(np.float32)
    ang = np.arange(L, dtype=np.float32)[None, :] * inv[:, None]
    rope = np.stack([np.tile(np.cos(ang), (4, 1)), np.tile(np.sin(ang), (4, 1))], 1).astype(np.float32)
    return np.ascontiguousarray(c.transpose(1, 0, 2)), np.ascontiguousarray(rope)


G_HEADS, G_DK, G_DV, CHUNK = 4, 128, 256, 64
EXPERTS, CAP = 16, 2 * SEQ // 16
PAIRS = EXPERTS // 2
COL2 = dict(aq=0, gq=768, gk=1280, gv=1792, gr=2816, ga=3872, gg=4896)
PLE = 256
FAR = 1.5 * 2.0 ** 23
TURN = (6.28125, 0.0019350051879882812, 3.0199159819e-7)
TAKEN_AFF = -1.0
WO_FIRST = 1


class Steps:

    def __init__(self, base=0):
        self.base, self.n = base, 0

    def one(self):
        self.n += 1
        return 1

    def now(self):
        return self.base + self.n

    def at(self, n):
        return self.base + n


def hybrid_kernel(nc, x, meta, w_in, w_misc, conv_p, w_out, post_p, cst_d, rope_d, B, out):
    F32, U32, I32 = mybir.dt.float32, mybir.dt.uint32, mybir.dt.int32
    ALU, ACT, AX = mybir.AluOpType, mybir.ActivationFunctionType, mybir.AxisListType

    w_in_v = w_in.rearrange("l (k p) n -> l p k n", p=P)
    w_out_v = w_out.rearrange("l (k p) n -> l p k n", p=P)
    w_misc_v = w_misc.rearrange("l (k p) n -> l p k n", p=P)

    top = ExitStack()
    with top:
        def pool_of(stack):
            return lambda name, shape: stack.enter_context(nc.sbuf_tensor(name, shape, F32))

        def sem(name):
            return top.enter_context(nc.semaphore(name))

        keep = pool_of(top)
        H = keep("H", [P, TILES, D_MODEL])
        cst = keep("cst", [P, NC, P])
        ring = keep("ring", [P, SLOTS, KC, WCOLS])
        small = keep("small", [P, 512])
        few = keep("few", [P, 640])
        gains = keep("gains", [P, 4, KC])
        router = keep("router", [P, KC, EXPERTS])
        sink = keep("sink", [P, 2, HEADS])
        ident, ones, mean_w, rot = cst[:, 0, :], cst[:, 1, :], cst[:, 2, :], cst[:, 3, :]
        future_score, future_hidden = cst[:, 5, :], cst[:, 6, :]

        first = ExitStack()
        buf = pool_of(first)
        hT = buf("hT", [P, KC, L])
        rope = buf("rope", [P, 2, L])
        post = buf("post", [P, 2, D_MODEL])
        misc = buf("misc", [P, KC, 136])
        convp = buf("convp", [P, 4, TAPS + 3])
        qT = buf("qT", [P, 4, L])
        kT = buf("kT", [P, 4, L])
        zaT = buf("zaT", [P, 4, L])
        qiT = zaT
        kiT = buf("kiT", [P, L])
        V = buf("V", [P, TILES, 512])
        zcT = buf("zcT", [P, 4, L])
        uT = buf("uT", [P, 4, TAPS - 1 + L])
        yT = buf("yT", [P, 2 * 4, L])
        KEYS = [N_META + P * (t + 1) for t in range(XT)] + [N_META]
        score = [buf(f"score{t}", [P, DUMMIES + KEYS[t]]) for t in range(XT)]
        pr = buf("pr", [P, 4, L])
        prT = buf("prT", [P, 4, 4, P])
        prR = buf("prR", [N_META, 4, P])
        raw = buf("raw", [P, 2, L])
        first.close()


        second = ExitStack()
        buf = pool_of(second)
        aT = buf("aT", [P, KC, SEQ])
        attT = buf("attT", [P, 4, SEQ])
        gqk = buf("gqk", [P, 2, 4, SEQ])
        GV = buf("GV", [P, XT, D_MODEL])
        zT = buf("zT", [64, SEQ])
        up = buf("up", [64, 512])
        scope = ExitStack()
        buf = pool_of(scope)
        xn = buf("xn", [P, 2, D_MODEL])
        aqT = buf("aqT", [P, 4, SEQ])
        akT = buf("akT", [P, 2, SEQ])
        av = buf("av", [P, XT, P])
        pr2 = buf("pr2", [P, 4, 3 * P])
        pr2T = buf("pr2T", [P, 4, 3 * P])
        rope2 = buf("rope2", [P, 2, SEQ])
        raw2 = buf("raw2", [P, 2, SEQ])
        pos = buf("pos", [P, SEQ])
        angle = buf("angle", [P, SEQ])
        turns = buf("turns", [P, SEQ])
        scope.close()
        scope = ExitStack()
        buf = pool_of(scope)
        qB = buf("qB", [P, 4, SEQ])
        kE = buf("kE", [P, 2, XT, 512])
        AT = buf("AT", [P, XT, 4, P])
        O = buf("O", [P, XT, D_MODEL])
        S = buf("S", [P, 3, G_HEADS, G_DV])
        decay = [buf(n, [P, 4, P]) for n in ("cum", "exp_b", "k_t", "k_e")]
        gate = buf("gate", [P, 2, 512])
        squares = buf("squares", [P, 2, G_DV])
        zr = ([H[:, XT, 512 * a:512 * (a + 1)] for a in range(2)]
              + [b[:, :, :].rearrange("p h n -> p (h n)") for b in decay] + [gate[:, a, :] for a in range(2)])
        scope.close()
        scope = ExitStack()
        buf = pool_of(scope)
        side = buf("side", [P, 6, SEQ])
        scope.close()
        second.close()
        OT = gqk[:, :, :, :].rearrange("p a c n -> p (a c) n")
        mT = GV[:, :, :].rearrange("p t (a n) -> p (t a) n", a=2)

        third = ExitStack()
        buf = pool_of(third)
        MORE = 7
        ring_more = buf("ring_more", [P, MORE, KC, WCOLS])
        XN = buf("XN", [P, XT, D_MODEL])
        sel = buf("sel", [P, XT, EXPERTS * CAP])
        scope = ExitStack()
        aT2 = pool_of(scope)("aT2", [P, KC, SEQ])
        scope.close()
        selw = buf("selw", [P, XT, P])
        GT = buf("GT", [P, SEQ])
        xe = buf("xe", [P, KC, P])
        Y = buf("Y", [P, D_MODEL])
        hid = buf("hid", [P, 2, 512])
        hidT = buf("hidT", [P, 4, P])
        final_g = buf("final_g", [P, D_MODEL])
        embedded = buf("embedded", [P, XT, D_MODEL])
        xn3 = XN[:, 0:2, :]
        outb = XN[:, 2:4, :]
        aT3 = sel[:, :, :].rearrange("p t n -> p (t n)").rearrange("p (k n) -> p k n", k=KC)
        sel_flat = sel[:, :, :].rearrange("p t n -> p (t n)")
        w_p = sel_flat[:, 0:2 * D_MODEL].rearrange("p (k n) -> p k n", k=PLE // P)
        pT = sel_flat[:, 2 * D_MODEL:2 * D_MODEL + 2 * SEQ].rearrange("p (k n) -> p k n", k=PLE // P)
        emb = Y[:, :].rearrange("p (a n) -> p a n", a=2)
        third.close()

        def few_at(a, n):
            return few[:, a:a + n]

        norm_sq, norm_std, norm_inv = few_at(0, 20), few_at(20, 20), few_at(40, 8)
        neg_max2, sum2, sink2, inv2, den2 = (few_at(64 + 32 * i, 32) for i in range(5))
        o_sq, o_std, o_inv = few_at(224, 16), few_at(240, 16), few_at(256, 16)
        dec = few_at(272, 64).rearrange("p (d t h c) -> p d t h c", d=2, t=XT, h=G_HEADS)
        soft = few_at(336, 12)
        logit = few_at(348, 64).rearrange("p (t e) -> p t e", t=XT)
        aff = few_at(412, 64).rearrange("p (t e) -> p t e", t=XT)
        rank = few_at(540, 64).rearrange("p (t e) -> p t e", t=XT)
        max8 = few_at(604, 8)
        affT = hid[0:EXPERTS, 0, :]
        takenT = hid[0:EXPERTS, 1, :]
        rot2 = cst[:, 4, :]
        window = cst[:, 10:13, :].rearrange("p a n -> p (a n)")

        ps = top.enter_context(nc.psum_tensor("ps", [P, 8, 512], F32))

        wi = small[:, 0:32]
        wiT = pr[0:HEADS, 0, :]
        top8 = small[:, 32:64]
        neg_max = small[:, 64:104]
        row_sum = small[:, 104:144]
        row_inv = small[:, 144:184]
        stats = small[:, 184:196]
        mean_var = small[:, 196:206]
        ln_std_v = small[:, 206:211]
        ln_inv = small[:, 211:216]
        eps_ln = small[:, 216:217]
        eps_rms = small[:, 217:218]

        def rows_of(t):
            return (P, N_META + P * t) if t < XT else (N_META, 0)

        def halves(b):
            return b.rearrange("p (a n) -> p a n", a=2)

        def pair(p):
            return ps[:, 2 * p:2 * p + 2, 0:HALF]

        def span(b, banks, rows, n):
            if n <= 512:
                return b[0:rows, 0:n], ps[0:rows, banks, 0:n]
            return halves(b[0:rows, 0:n]), ps[0:rows, banks:banks + 2, 0:n // 2]

        consts_in = sem("consts_in")
        h_in = [sem(f"h_in{t}") for t in range(TILES)]
        turn_in = sem("turn_in")
        consts_set = sem("consts_set")
        params_in = sem("params_in")
        post_in = sem("post_in")
        slot_in = [sem(f"slot_in{s}") for s in range(SLOTS)]
        turned = sem("turned")
        turned_act = sem("turned_act")
        turned_dve = sem("turned_dve")
        proj_done = sem("proj_done")
        proj_out = sem("proj_out")
        zc_done = sem("zc_done")
        zc_out = sem("zc_out")
        zc_silu = sem("zc_silu")
        rot_done = sem("rot_done")
        raw_used = sem("raw_used")
        idx_done = sem("idx_done")
        idx_relu = sem("idx_relu")
        idx_added = sem("idx_added")
        conv_done = sem("conv_done")
        cn_mean = sem("cn_mean")
        cn_centred = sem("cn_centred")
        cn_square = sem("cn_square")
        cn_var = sem("cn_var")
        cn_std = sem("cn_std")
        cn_scaled = sem("cn_scaled")
        cn_silu = sem("cn_silu")
        conv_y = sem("conv_y")
        at_score = sem("at_score")
        at_masked = sem("at_masked")
        at_exp = sem("at_exp")
        at_prob = sem("at_prob")
        at_turned = sem("at_turned")
        at_full = sem("at_full")
        at_rest = sem("at_rest")
        at_value = sem("at_value")
        attn_y = sem("attn_y")
        wo_done = sem("wo_done")
        wo_added = sem("wo_added")
        ln_var = sem("ln_var")
        ln_std = sem("ln_std")
        h_done = sem("h_done")
        dve_step = sem("dve_step")
        pool_step = sem("pool_step")
        stored = [sem(f"stored{i}") for i in range(2)]

        ITEMS = ([("ki", 0)] + [("qi", c) for c in range(4)] + [("wi", 0), ("a", 0), ("wt", 0)]
                 + [("a", c) for c in range(1, 4)]
                 + [("g", c) for c in range(4)] + [("q", c) for c in range(4)] + [("k", c) for c in range(4)]
                 + [("v", b) for b in range(TILES)] + [("za", c) for c in range(4)])
        LATE_TAPS = 40
        NZ = 8
        NI = len(ITEMS)
        ITEM = {item: n for n, item in enumerate(ITEMS)}
        IDX_AFTER = ITEM[("a", 3)]
        GROUPS = [(COL, h) for COL in ("qi", "a", "g", "q", "k", "v", "za", "zc") for h in range(2)]
        NG = len(GROUPS) + D_MODEL // WCOLS
        COLS = dict(qi=COL_QI, a=COL_A, g=COL_G, q=COL_Q, k=COL_K, v=COL_V, zc=COL_ZC, za=COL_ZA)
        GROUP_END = [ITEM[(k, TILES - 1 if k == "v" else 2 * h + 1)] + 1 for k, h in GROUPS if k != "zc"]
        ROPED = [n for n, (k, _) in enumerate(ITEMS) if k in ("ki", "qi", "q", "k")]
        RAW = [n for n, (k, _) in enumerate(ITEMS) if k in ("ki", "qi", "g", "q", "k")]
        NROT, NRAW, NIDX, NATT = len(ROPED), len(RAW), XT * HEADS, TILES * HEADS

        def rows512(n):
            return ring[:, n % SLOTS, :, :].rearrange("p k n -> p (k n)").rearrange("p (k n) -> p k n", k=4)

        def rows256(n):
            return ring[:, n % SLOTS, :, :].rearrange("p k n -> p (k n)").rearrange("p (k n) -> p k n", k=2)

        UNITS = [(t, a) for t in ORDER for a in range(2 if t < XT else 1)]
        NU = len(UNITS)

        def group_of(item):
            kind, c = ITEMS[item]
            return GROUPS.index((kind, c // 2))

        def att(j):
            t, h = divmod(j, HEADS)
            n, q0 = rows_of(t)
            return t, h, n, q0, KEYS[t], KEYS[t] // P

        passed = {e: sem(f"passed_{e}") for e in ("sp", "pe", "act", "pool", "dve")}

        def settle(engine, name):
            engine.sem_inc(passed[name], 1)


        second_in = sem("second_in")
        third_in = sem("third_in")
        more_in = [sem(f"more_in{s}") for s in range(MORE)]
        nq_done = sem("nq_done")
        ns_done = sem("ns_done")
        xn_done = sem("xn_done")
        nt_done = sem("nt_done")
        nt_out = sem("nt_out")
        rt_arg = sem("rt_arg")
        rt_sin = sem("rt_sin")
        p2_done = sem("p2_done")
        p2_out = sem("p2_out")
        gv_done = sem("gv_done")
        gv_out = sem("gv_out")
        rot2_done = sem("rot2_done")
        raw2_used = sem("raw2_used")
        w_score = sem("w_score")
        w_masked = sem("w_masked")
        w_exp = sem("w_exp")
        w_sink = sem("w_sink")
        w_prob = sem("w_prob")
        w_turned = sem("w_turned")
        w_out_t = sem("w_out_t")
        w_value = sem("w_value")
        w_att = sem("w_att")
        gz_done = sem("gz_done")
        gl_log = sem("gl_log")
        gl_set = sem("gl_set")
        gl_cum = sem("gl_cum")
        gl_exp = sem("gl_exp")
        gl_rest = sem("gl_rest")
        gl_rexp = sem("gl_rexp")
        gl_qk = sem("gl_qk")
        gl_att = sem("gl_att")
        gl_mask = sem("gl_mask")
        gl_turn = sem("gl_turn")
        gl_kout = sem("gl_kout")
        gl_zero = sem("gl_zero")
        kv_done = sem("kv_done")
        st_done = sem("st_done")
        o_done = sem("o_done")
        o_out = sem("o_out")
        o_sqd = sem("o_sqd")
        o_stdd = sem("o_stdd")
        gr_done = sem("gr_done")
        gr_silu = sem("gr_silu")
        gr_out = sem("gr_out")
        mg_done = sem("mg_done")
        mg_sig = sem("mg_sig")
        mg_out = sem("mg_out")
        wo2_done = sem("wo2_done")
        wo2_out = sem("wo2_out")
        rt_done = sem("rt_done")
        rt_out = sem("rt_out")
        rl_done = sem("rl_done")
        rl_sub = sem("rl_sub")
        rl_exp = sem("rl_exp")
        aff_done = sem("aff_done")
        affT_done = sem("affT_done")
        rank_done = sem("rank_done")
        rankT_done = sem("rankT_done")
        sel_done = sem("sel_done")
        gather_done = sem("gather_done")
        selw_done = sem("selw_done")
        gt_done = sem("gt_done")
        gt_out = sem("gt_out")
        xe_set = sem("xe_set")
        e_gate = sem("e_gate")
        e_up = sem("e_up")
        e_silu = sem("e_silu")
        e_hid = sem("e_hid")
        e_turn = sem("e_turn")
        e_hidT = sem("e_hidT")
        e_down = sem("e_down")
        e_y = sem("e_y")
        e_y2 = sem("e_y2")
        cb_done = sem("cb_done")
        cb_out = sem("cb_out")
        em_done = sem("em_done")
        em_out = sem("em_out")
        pl_done = sem("pl_done")
        pl_sig = sem("pl_sig")
        pl_out = sem("pl_out")
        y_set = sem("y_set")
        act_step = sem("act_step")

        ITEMS2 = ([("av", 0)] + [("ak", c) for c in range(2)] + [("z", 0)] + [("aq", c) for c in range(4)]
                  + [("gq", c) for c in range(4)] + [("gk", c) for c in range(4)])
        WIN_FROM = 8
        NI2 = len(ITEMS2)
        AT2 = {item: n for n, item in enumerate(ITEMS2)}
        ROPED2 = [AT2[("ak", 0)], AT2[("ak", 1)]] + [AT2[("aq", c)] for c in range(4)]
        BEFORE = DEPTH * (NG // SLOTS)
        GROUPS2 = ([("m0", 0), ("m1", 0)] + [(g, c) for g in ("aq", "gq", "gk") for c in range(2)]
                   + [("gv", c) for c in range(4)] + [("gr", c) for c in range(4)]
                   + [(g, c) for c in range(4) for g in ("ga", "ba", "gg", "bg")]
                   + [("wo", c) for c in range(4)])
        NG2 = len(GROUPS2)
        G2 = {g: n for n, g in enumerate(GROUPS2)}

        def last_use(g):
            kind, c = g
            if kind in ("m0", "m1"):
                return p2_done, AT2[("ak", 1) if kind == "m0" else ("z", 0)] + 1
            if kind in ("aq", "gq", "gk"):
                return p2_done, AT2[(kind, 2 * c + 1)] + 1
            if kind == "gv":
                return gv_done, XT * (c // 2) + XT
            if kind == "gr":
                return gr_done, 2 * c + 2
            if kind == "wo":
                return wo2_done, 2 * XT
            return mg_done, 8 * c + 4 + ("ga", "ba", "gg", "bg").index(kind) + 1

        def gr_bank(c):
            return 6 + c % 2 if c else 1

        def win(j):
            t, h = divmod(j, HEADS)
            k0 = max(t - 1, 0)
            return t, h, k0, min(t + 1, XT - 1) - k0 + 1

        NW = XT * HEADS
        TD = [(t, d) for t in range(XT) for d in (1, 0)]
        SCAN = {1: [(t, c) for t in reversed(range(XT)) for c in (1, 0)],
                0: [(t, c) for t in range(XT) for c in (0, 1)]}

        PLACES = [SLOTS, SLOTS + 1, SLOTS + 2, SLOTS + 3, SLOTS + 4, G2[("bg", 3)] % SLOTS, SLOTS + 5, SLOTS + 6]
        PLACES += [s for s in range(SLOTS) if s not in PLACES]
        EARLY = 6
        sel_pair = sel[:, :, :].rearrange("p t (i n) -> p t i n", n=P)
        aff_pair = aff.rearrange("p t (i e) -> p t i e", e=2)

        def eslot(i):
            s = PLACES[i]
            b = ring[:, s, :, :] if s < SLOTS else ring_more[:, s - SLOTS, :, :]
            return b.rearrange("p k n -> p (k n)").rearrange("p (k n) -> p k n", k=2)

        def eslot_in(i):
            s = PLACES[i]
            return slot_in[s] if s < SLOTS else more_in[s - SLOTS]

        LOADED = [BEFORE + len(range(s, NG2, SLOTS)) if s < SLOTS else 0 for s in PLACES]

        block = top.enter_context(nc.Block())

        @block.sync
        def _(sp):
            sp.dma_start(cst[:, 0:4, :], cst_d[:, 0:4, :]).then_inc(turn_in, 16)
            for t in ORDER:
                if t < XT:
                    sp.dma_start(H[:, t, :], x[P * t:P * (t + 1), :]).then_inc(h_in[t], 16)
                else:
                    sp.dma_start(H[0:N_META, XT, :], meta).then_inc(h_in[XT], 16)

            with sp.Fori(0, DEPTH) as l:
                sp.wait_ge(wo_done, l * NU + WO_FIRST)
                settle(sp, "sp")
                sp.dma_start(misc[:, :, :], w_misc_v[l]).then_inc(params_in, 16)
                sp.dma_start(convp[:, :, :], conv_p[l]).then_inc(params_in, 16)
                for n in range(NG):
                    if n - SLOTS >= len(GROUP_END):
                        sp.wait_ge(zc_done, l * NZ + NZ // 2)
                    elif n >= SLOTS:
                        sp.wait_ge(proj_done, l * NI + GROUP_END[n - SLOTS])
                    if n == SLOTS:
                        settle(sp, "sp")
                        sp.dma_start(post[:, :, :], post_p[l]).then_inc(post_in, 16)
                    if n < len(GROUPS):
                        kind, h = GROUPS[n]
                        slot = ring[:, n % SLOTS, :, :]
                        src = w_in_v[l, :, :, COLS[kind] + WCOLS * h:COLS[kind] + WCOLS * (h + 1)]
                        if kind == "v":
                            slot, src = rows512(n), w_in_v[l, :, 4 * h:4 * h + 4, COL_V:COL_V + 512]
                    else:
                        m = n - len(GROUPS)
                        slot, src = rows256(n), w_out_v[l, :, 2 * m:2 * m + 2, :]
                    if n > SLOTS:
                        settle(sp, "sp")
                    sp.dma_start(slot, src).then_inc(slot_in[n % SLOTS], 16)
            sp.wait_ge(h_done, TILES + DEPTH * TILES)
            sp.dma_start(up[:, :], B["up"]).then_inc(second_in, 16)
            sp.dma_start(pos[:, :].bitcast(I32), B["positions"]).then_inc(second_in, 16)
            for n, (kind, c) in enumerate(GROUPS2):
                if n == 0:
                    sp.wait_ge(proj_done, DEPTH * NI)
                elif n < SLOTS:
                    sp.wait_ge(wo_done, DEPTH * NU + WO_FIRST)
                else:
                    sp.wait_ge(*last_use(GROUPS2[n - SLOTS]))
                slot = ring[:, n % SLOTS, :, :]
                if kind in ("m0", "m1"):
                    src = B["w_misc"][:, :, 0:WCOLS] if kind == "m0" else B["w_misc"][:, :, WCOLS:WCOLS + 192]
                    slot = slot if kind == "m0" else slot[:, :, 0:192]
                elif kind == "ba":
                    slot, src = slot[:, 0:4, :], B["w_ba"][:, :, WCOLS * c:WCOLS * (c + 1)]
                elif kind == "wo":
                    slot, src = rows256(n), B["w_wo"][:, 2 * c:2 * c + 2, :]
                elif kind == "gv":
                    col = COL2["gv"] + 512 * (c // 2)
                    src = B["w_in"][:, 4 * (c % 2):4 * (c % 2) + 4, col:col + 512]
                    slot = rows512(n)
                elif kind == "bg":
                    src = B["w_" + kind][:, :, WCOLS * c:WCOLS * (c + 1)]
                else:
                    src = B["w_in"][:, :, COL2[kind] + WCOLS * c:COL2[kind] + WCOLS * (c + 1)]
                sp.dma_start(slot, src).then_inc(slot_in[n % SLOTS], 16)
                if kind == "ga" and c == 2:
                    sp.dma_start(w_p, B["w_p"]).then_inc(third_in, 16)
                    sp.dma_start(pT, B["pT"]).then_inc(third_in, 16)
                    sp.dma_start(final_g[:, :], B["final"].partition_broadcast(P)).then_inc(third_in, 16)
            def expert_block(e, i):
                sp.dma_start(eslot(i), B["w_exp"][i // 4][e, :, 2 * (i % 4):2 * (i % 4) + 2, :])\
                    .then_inc(eslot_in(i), 16)

            sp.wait_ge(mg_out, 2 * KC)
            for i in range(EARLY):
                expert_block(0, i)
            sp.wait_ge(wo2_done, 2 * XT)
            for i in range(EARLY, 12):
                expert_block(0, i)
            with sp.Fori(0, EXPERTS - 1) as e:
                for i in range(12):
                    sp.wait_ge((e_gate, e_up, e_down)[i // 4], 4 * e + i % 4 + 1)
                    settle(sp, "sp")
                    expert_block(e + 1, i)
            sp.wait_ge(e_gate, 4 * EXPERTS)
            for c in range(4):
                sp.dma_start(eslot(c), B["w_pg"][:, 2 * c:2 * c + 2, :]).then_inc(eslot_in(c), 16)
            for t in range(XT):
                sp.wait_ge(y_set, t + 1)
                sp.dma_start(out[P * t:P * (t + 1), :], outb[:, t % 2, :]).then_inc(stored[t % 2], 16)
            sp.wait_ge(stored[0], 16 * (XT // 2))
            sp.wait_ge(stored[1], 16 * (XT // 2))

        @block.tensor
        def _(pe):
            mm = nc.tensor.matmul

            def slot_ready(l, n):
                pe.wait_ge(slot_in[n % SLOTS], 16 * (l * (NG // SLOTS) + n // SLOTS + 1))

            def item(l, n):
                kind, c = ITEMS[n]
                p = n % 2
                if n >= 2:
                    pe.wait_ge(proj_out, l * NI + n - 1)
                if kind not in ("ki", "wi", "wt") and (c % 2 == 0 or kind == "v") and not (kind == "v" and c > 0):
                    slot_ready(l, group_of(n))
                    if kind == "v":
                        slot_ready(l, group_of(n) + 1)
                if kind == "wi":
                    for k in range(KC):
                        for g in range(Q4):
                            last = mm(ps[32 * g:32 * g + HEADS, 2 * p, 0:L // Q4], misc[:, k, P:P + HEADS],
                                      hT[:, k, L // Q4 * g:L // Q4 * (g + 1)], start=(k == 0), stop=(k == KC - 1))
                elif kind == "wt":
                    pe.wait_ge(proj_out, l * NI + ITEM[("wi", 0)] + 1)
                    settle(pe, "pe")
                    for t in range(XT):
                        q0 = rows_of(t)[1]
                        last = nc.tensor.transpose(ps[:, 2 * p, HEADS * t:HEADS * (t + 1)], wiT[:, q0:q0 + P],
                                                   ident[0:HEADS, 0:HEADS])
                elif kind == "v" and c == XT:
                    for k in range(KC):
                        for g in range(Q4):
                            last = mm(ps[32 * g:32 * g + N_META, 2 * p, 0:P], hT[:, k, P * c:L],
                                      rows512(GROUPS.index(("v", k // 4)))[:, k % 4, P * g:P * (g + 1)],
                                      start=(k == 0), stop=(k == KC - 1))
                elif kind == "v":
                    for k in range(KC):
                        last = mm(ps[:, 2 * p, :], hT[:, k, P * c:P * (c + 1)],
                                  rows512(GROUPS.index(("v", k // 4)))[:, k % 4, :], start=(k == 0), stop=(k == KC - 1))
                else:
                    for k in range(KC):
                        if kind == "ki":
                            w = misc[:, k, 0:P]
                        else:
                            w = ring[:, group_of(n) % SLOTS, k, P * (c % 2):P * (c % 2 + 1)]
                        for a in range(2):
                            last = mm(ps[:, 2 * p + a, 0:HALF], w, hT[:, k, HALF * a:HALF * (a + 1)],
                                      start=(k == 0), stop=(k == KC - 1))
                last.then_inc(proj_done, 1)

            def rotate(l, r):
                n = ROPED[r]
                u = RAW.index(n)
                pe.wait_ge(proj_out, l * NI + n + 1)
                if r >= 2:
                    pe.wait_ge(raw_used, l * NRAW + RAW.index(ROPED[r - 2]) + 1)
                if r == 5:
                    pe.wait_ge(idx_relu, l * NIDX + NIDX)
                for a in range(2):
                    last = mm(ps[:, 4 + 2 * (r % 2) + a, 0:HALF], rot, raw[:, u % 2, HALF * a:HALF * (a + 1)],
                              start=True, stop=True)
                last.then_inc(rot_done, 1)

            def index_scores(l):
                pe.wait_ge(raw_used, l * NRAW + 5)
                for j in range(NIDX):
                    t, h = divmod(j, HEADS)
                    n, q0 = rows_of(t)
                    if j >= 2:
                        pe.wait_ge(idx_relu, l * NIDX + j - 1)
                    b0 = 64 * (h % 2)
                    for a in range(1 if KEYS[t] <= 512 else 2):
                        w = min(KEYS[t], 512) if KEYS[t] <= 512 else HALF
                        last = mm(ps[:, 4 + 2 * (j % 2) + a, 0:w], qiT[b0:b0 + 64, h // 2, q0:q0 + n],
                                  kiT[b0:b0 + 64, a * w:(a + 1) * w], start=True, stop=True)
                    last.then_inc(idx_done, 1)

            def at_scores(l, j):
                t, h, n, q0, keys, _ = att(j)
                if j >= 2:
                    pe.wait_ge(at_masked, l * NATT + j - 1)
                else:
                    pe.wait_ge(raw_used, l * NRAW + NRAW)
                settle(pe, "pe")
                b0 = 64 * (h % 2)
                for a in range(1 if keys <= 512 else 2):
                    w = keys if keys <= 512 else HALF
                    last = mm(ps[0:n, 4 + 2 * (j % 2) + a, 0:w], qT[b0:b0 + 64, h // 2, q0:q0 + n],
                              kT[b0:b0 + 64, h // 2, a * w:(a + 1) * w], start=True, stop=True)
                last.then_inc(at_score, 1)

            def at_turn(l, j):
                t, h, n, q0, keys, full = att(j)
                pe.wait_ge(at_prob, l * NATT + j + 1)
                if j == 0:
                    pe.wait_ge(proj_out, l * NI + NI)
                if 1 <= j < XT * HEADS:
                    pe.wait_ge(at_full, l * XT * HEADS + j)
                if j >= 1:
                    pe.wait_ge(at_rest, l * NATT + j)
                settle(pe, "pe")
                for b in range(full):
                    nc.tensor.transpose(ps[:, 0, P * b:P * b + n], pr[0:n, j % 4, P * b:P * (b + 1)],
                                        ident[0:n, 0:n])
                nc.tensor.transpose(ps[0:N_META, 2, P * (j % 4):P * (j % 4) + n],
                                    pr[0:n, j % 4, P * full:P * full + N_META], ident[0:n, 0:n]).then_inc(at_turned, 1)

            def at_values(l, j):
                t, h, n, q0, keys, full = att(j)
                if full:
                    pe.wait_ge(at_full, l * XT * HEADS + j + 2)
                pe.wait_ge(at_rest, l * NATT + j + 2)
                if h == 0 and t > 0:
                    pe.wait_ge(attn_y, l * TILES + t)
                o = [ps[64 * u:64 * u + 64, 3, P * (h // 2):P * (h // 2) + n] for u in range(2)]
                for b in range(full):
                    for u in range(2):
                        mm(o[u], V[:, b, 64 * (h + u):64 * (h + u + 1)], prT[:, (j + u) % 4, b, 0:n],
                           start=(b == 0), stop=False)
                for u in range(2):
                    mm(o[u], V[0:N_META, full, 64 * (h + u):64 * (h + u + 1)], prR[:, (j + u) % 4, 0:n],
                       start=(full == 0), stop=True).then_inc(at_value, 1)

            def zc_quarter(l, u, part):
                c, a = divmod(u, 2)
                if part == 0:
                    if u == 0:
                        pe.wait_ge(proj_out, l * NI + NI)
                    else:
                        pe.wait_ge(zc_out, l * NZ + u)
                    if u % 4 == 0:
                        slot_ready(l, GROUPS.index(("zc", c // 2)))
                    settle(pe, "pe")
                w = ring[:, GROUPS.index(("zc", c // 2)) % SLOTS, :, P * (c % 2):P * (c % 2 + 1)]
                for k in (2 * part, 2 * part + 1):
                    last = mm(ps[:, 1, 0:HALF], w[:, k, :], hT[:, k, HALF * a:HALF * (a + 1)],
                              start=(k == 0), stop=(k == KC - 1))
                if part == 3:
                    last.then_inc(zc_done, 1)

            def out_product(l, t, ks):
                rows, q0 = rows_of(t)
                first, end = (4, 3) if t < 2 else (0, KC - 1)
                for a in range(2 if t < XT else 1):
                    i = UNITS.index((t, a))
                    if i >= 4 and ks[0] == 0:
                        pe.wait_ge(wo_added, l * NU + i - 3)
                        settle(pe, "pe")
                    for k in ks:
                        w = rows256(len(GROUPS) + k // 2)[:, k % 2, :]
                        if t < XT:
                            last = mm(ps[0:rows, 4 + i % 4, :], yT[:, k, q0:q0 + rows], w[:, 512 * a:512 * (a + 1)],
                                      start=(k == first), stop=(k == end))
                        else:
                            for g in range(Q4):
                                last = mm(ps[32 * g:32 * g + rows, 4 + i % 4, 0:WCOLS], yT[:, k, q0:q0 + rows],
                                          w[:, WCOLS * g:WCOLS * (g + 1)], start=(k == first), stop=(k == end))
                    if end in ks:
                        last.then_inc(wo_done, 1)

            pe.sem_inc(wo_done, WO_FIRST)
            pe.wait_ge(turn_in, 16)
            with pe.Fori(0, DEPTH) as l:
                for o, t in enumerate(ORDER):
                    rows, _ = rows_of(t)
                    pe.wait_ge(h_done, l * TILES + o + 1)
                    settle(pe, "pe")
                    for hf, read in enumerate((turned_act, turned_dve)):
                        if o >= 2:
                            pe.wait_ge(read, l * TILES + o - 1)
                            settle(pe, "pe")
                        for c in range(4):
                            last = nc.tensor.transpose(
                                ps[:, 2 * (o % 2) + hf, P * c:P * c + rows],
                                H[0:rows, t, P * (4 * hf + c):P * (4 * hf + c + 1)], ident[0:rows, 0:rows])
                        last.then_inc(turned, 1)
                pe.wait_ge(turned_act, l * TILES + TILES)
                pe.wait_ge(turned_dve, l * TILES + TILES)
                pe.wait_ge(params_in, 32 * (l + 1))
                r = 0
                for n in range(NI):
                    item(l, n)
                    if n >= 1 and n - 1 in ROPED:
                        rotate(l, r)
                        r += 1
                    if n == IDX_AFTER:
                        index_scores(l)
                for j in range(NATT + 3):
                    if j < NATT:
                        at_scores(l, j)
                    if 2 <= j < NATT + 2:
                        at_turn(l, j - 2)
                    if j < 4 * NZ:
                        zc_quarter(l, j // 4, j % 4)
                    if j >= 4 and j % 2 == 0:
                        at_values(l, j - 4)
                pe.wait_ge(conv_done, 4 * l + 4)
                pe.wait_ge(attn_y, l * TILES + TILES)
                pe.wait_ge(zc_out, l * NZ + NZ)
                for a in range(2):
                    for c in range(4):
                        last = mm(ps[:, a, 0:HALF], mean_w, yT[:, c, HALF * a:HALF * (a + 1)],
                                  start=(c == 0), stop=(c == 3))
                last.then_inc(cn_mean, 1)
                for m in range(4):
                    slot_ready(l, len(GROUPS) + m)
                out_product(l, 0, range(4, KC))
                for c in range(4):
                    pe.wait_ge(cn_square, 4 * l + c + 1)
                    for a in range(2):
                        last = mm(ps[:, 2 + a, 0:HALF], mean_w, pr[:, c, HALF * a:HALF * (a + 1)],
                                  start=(c == 0), stop=(c == 3))
                last.then_inc(cn_var, 1)
                out_product(l, 1, range(4, KC))
                pe.wait_ge(conv_y, 4 * l + 4)
                out_product(l, 0, range(4))
                out_product(l, 1, range(4))
                for t in ORDER[2:]:
                    out_product(l, t, range(KC))

            T = nc.tensor.transpose

            def slot2(kind, c):
                n = G2[(kind, c)]
                pe.wait_ge(slot_in[n % SLOTS], 16 * (BEFORE + n // SLOTS + 1))
                return ring[:, n % SLOTS, :, :]

            def turn_norm(w, src, tiles=range(XT), between=None):
                for t in tiles:
                    pe.wait_ge(xn_done, XT * w + t + 1)
                    for hf in range(2):
                        i = 2 * t + hf
                        if i >= 4:
                            pe.wait_ge(nt_out, 2 * XT * w + i - 3)
                        for c in range(4):
                            last = T(ps[:, 4 + i % 4, P * c:P * (c + 1)],
                                     src(t)[:, P * (4 * hf + c):P * (4 * hf + c + 1)], ident)
                        last.then_inc(nt_done, 1)
                    if between and t >= 1:
                        between(t - 1)
                if tiles[-1] == XT - 1:
                    pe.wait_ge(nt_out, 2 * XT * (w + 1))

            def window_values(t):
                pe.wait_ge(nt_out, 2 * t + 2)
                w = slot2("m1", 0)
                for k in range(KC):
                    last = mm(ps[:, AT2[("av", 0)], P * t:P * (t + 1)], aT[:, k, P * t:P * (t + 1)], w[:, k, 0:P],
                              start=(k == 0), stop=(k == KC - 1))
                if t == XT - 1:
                    last.then_inc(p2_done, 1)

            turn_norm(0, lambda t: xn[:, t % 2, :], between=window_values)
            window_values(XT - 1)

            def rotate2(r):
                n = ROPED2[r]
                pe.wait_ge(p2_out, n + 1)
                if r >= 2:
                    pe.wait_ge(raw2_used, r - 1)
                mm(ps[:, 4 + r % 2, :], rot2, raw2[:, r % 2, :], start=True, stop=True).then_inc(rot2_done, 1)

            def item2(n):
                kind, c = ITEMS2[n]
                if n >= 4:
                    pe.wait_ge(p2_out, n - 3)
                o = ps[:, n % 4, :]
                if kind == "ak":
                    w = slot2("m0", 0)[:, :, P * c:P * (c + 1)]
                elif kind == "z":
                    w = slot2("m1", 0)
                else:
                    w = slot2(kind, c // 2)[:, :, P * (c % 2):P * (c % 2 + 1)]
                if kind == "z":
                    for k in range(KC):
                        last = mm(o[0:64, :], w[:, k, P:P + 64], aT[:, k, :], start=(k == 0), stop=(k == KC - 1))
                else:
                    for k in range(KC):
                        last = mm(o, w[:, k, :], aT[:, k, :], start=(k == 0), stop=(k == KC - 1))
                last.then_inc(p2_done, 1)

            for n in range(1, WIN_FROM):
                item2(n)
                if n - 1 in ROPED2:
                    rotate2(ROPED2.index(n - 1))
            rotate2(ROPED2.index(WIN_FROM - 1))

            def item2_quarter(n, part):
                kind, c = ITEMS2[n]
                if part == 0:
                    pe.wait_ge(p2_out, n - 1)
                w = slot2(kind, c // 2)[:, :, P * (c % 2):P * (c % 2 + 1)]
                for k in (2 * part, 2 * part + 1):
                    last = mm(ps[:, 2 + n % 2, :], w[:, k, :], aT[:, k, :], start=(k == 0), stop=(k == KC - 1))
                if part == 3:
                    last.then_inc(p2_done, 1)

            def w_scores(j):
                t, h, k0, cnt = win(j)
                pe.wait_ge(w_masked, j - 1) if j >= 2 else pe.wait_ge(raw2_used, len(ROPED2))
                b0 = 64 * (h % 2)
                mm(ps[:, 4 + j % 2, 0:P * cnt], aqT[b0:b0 + 64, h // 2, P * t:P * (t + 1)],
                   akT[b0:b0 + 64, h // 4, P * k0:P * (k0 + cnt)], start=True, stop=True).then_inc(w_score, 1)

            def w_turn(j):
                t, h, k0, cnt = win(j)
                pe.wait_ge(w_prob, j + 1)
                if j >= 2:
                    pe.wait_ge(w_out_t, j - 1)
                for b in range(cnt):
                    last = T(ps[:, 6 + j % 2, P * b:P * (b + 1)], pr2[:, j % 4, P * b:P * (b + 1)], ident)
                last.then_inc(w_turned, 1)

            def w_values(j):
                t, h, k0, cnt = win(j)
                pe.wait_ge(w_out_t, j + 2)
                if h == 0 and t >= 2:
                    pe.wait_ge(w_att, t - 1)
                if j == 0:
                    pe.wait_ge(p2_out, WIN_FROM)
                for b in range(cnt):
                    for u in range(2):
                        last = mm(ps[64 * u:64 * u + 64, t % 2, P * (h // 2):P * (h // 2 + 1)],
                                  av[:, k0 + b, 64 * (h // 4):64 * (h // 4 + 1)],
                                  pr2T[:, (j + u) % 4, P * b:P * (b + 1)], start=(b == 0), stop=(b == cnt - 1))
                last.then_inc(w_value, 2)

            for part in range(4):
                item2_quarter(WIN_FROM, part)
            for j in range(NW + 3):
                if j < NW:
                    w_scores(j)
                if j < NW - 4:
                    item2_quarter(WIN_FROM + 1 + j // 4, j % 4)
                if 2 <= j < NW + 2:
                    w_turn(j - 2)
                if j >= 4 and j % 2 == 0:
                    w_values(j - 4)

            pe.wait_ge(w_att, XT)

            def gate_z(i):
                t, d = TD[i]
                if i >= 1:
                    pe.wait_ge(gl_set, i)
                if i == 0:
                    pe.wait_ge(second_in, 32)
                mm(ps[:, 0, :], zT[32 * d:32 * d + 17, P * t:P * (t + 1)], up[32 * d:32 * d + 17, :],
                   start=True, stop=True).then_inc(gz_done, 1)

            def gate_sums(i):
                t, d = TD[i]
                pe.wait_ge(gl_set, i + 1)
                if i >= 2:
                    pe.wait_ge(gl_exp, i - 1)
                for h in range(G_HEADS):
                    last = mm(ps[:, 2 + i % 2, P * h:P * (h + 1)], gate[:, 1, P * h:P * (h + 1)], cst[:, 7 + d, :],
                              start=True, stop=True)
                last.then_inc(gl_cum, 1)

            def gate_scores(i):
                t, d = TD[i]
                q = qB if d else gqk[:, 0, :, :]
                pe.wait_ge(gl_qk, i + 1)
                if i >= 2:
                    pe.wait_ge(gl_mask, i - 1)
                for h in range(G_HEADS):
                    last = mm(ps[:, 4 + i % 2, P * h:P * (h + 1)], decay[2][:, h, :], q[:, h, P * t:P * (t + 1)],
                              start=True, stop=True)
                last.then_inc(gl_att, 1)
                if i >= 2:
                    pe.wait_ge(gl_kout, i - 1)
                for h in range(G_HEADS):
                    last = T(ps[:, 6 + i % 2, P * h:P * (h + 1)], decay[3][:, h, :], ident)
                last.then_inc(gl_turn, 1)

            def values_item(i):
                half, t = divmod(i, XT)
                if i >= 1:
                    pe.wait_ge(gv_out, i)
                for a in range(2):
                    slot2("gv", 2 * half + a)
                for k in range(KC):
                    last = mm(ps[:, 1, :], aT[:, k, P * t:P * (t + 1)],
                              rows512(G2[("gv", 2 * half + k // 4)])[:, k % 4, :], start=(k == 0), stop=(k == KC - 1))
                last.then_inc(gv_done, 1)

            def gr_item(c):
                w = slot2("gr", c // 2)
                if c >= 3:
                    pe.wait_ge(gr_silu, c - 1)
                for k in range(KC):
                    last = mm(ps[:, gr_bank(c), :], w[:, k, P * (c % 2):P * (c % 2 + 1)], aT[:, k, :],
                              start=(k == 0), stop=(k == KC - 1))
                last.then_inc(gr_done, 1)

            gate_z(0)
            values_item(0)
            pe.wait_ge(p2_out, NI2)
            for i in range(len(TD)):
                gate_sums(i)
                if i + 1 < len(TD):
                    gate_z(i + 1)
                    values_item(i + 1)
                else:
                    pe.wait_ge(gv_out, 2 * XT)
                    gr_item(0)
                gate_scores(i)

            pe.wait_ge(gl_mask, len(TD))
            pe.wait_ge(gl_kout, len(TD))
            pe.wait_ge(gr_silu, 1)
            for rnd, d in enumerate((1, 0)):
                q = qB if d else gqk[:, 0, :, :]

                def state(s):
                    t, c = SCAN[d][s]
                    if 7 * rnd + s >= 2:
                        pe.wait_ge(st_done, 7 * rnd + s - 1)
                    b0 = CHUNK * c
                    for h in range(G_HEADS):
                        last = mm(ps[:, 2 * ((7 * rnd + s) % 2) + h // 2, G_DV * (h % 2):G_DV * (h % 2 + 1)],
                                  kE[b0:b0 + CHUNK, d, t, P * h:P * (h + 1)],
                                  GV[b0:b0 + CHUNK, t, G_DV * h:G_DV * (h + 1)], start=True, stop=True)
                    last.then_inc(kv_done, 1)

                state(0)
                state(1)
                for i in range(XT):
                    for s in (2 * i + 2, 2 * i + 3):
                        if s < 7:
                            state(s)
                    t = SCAN[d][2 * i][0]
                    n = XT * rnd + i
                    pe.wait_ge(st_done, 7 * rnd + 2 * i + 1)
                    if n >= 1:
                        pe.wait_ge(o_out, n)
                    for h in range(G_HEADS):
                        o = ps[:, 4 + h // 2, G_DV * (h % 2):G_DV * (h % 2 + 1)]
                        if d == 0:
                            mm(o, AT[:, t, h, :], GV[:, t, G_DV * h:G_DV * (h + 1)], start=True, stop=False)
                        for s in (2 * i, 2 * i + 1):
                            c = SCAN[d][s][1]
                            q0 = P * t + CHUNK * c
                            last = mm(o[CHUNK * c:CHUNK * (c + 1), :], q[:, h, q0:q0 + CHUNK], S[:, s % 3, h, :],
                                      start=(d == 1), stop=True)
                    last.then_inc(o_done, 1)
                    if n + 1 < KC:
                        gr_item(n + 1)

            pe.wait_ge(o_out, 2 * XT)
            pe.wait_ge(gr_silu, KC)
            turn_norm(1, lambda t: O[:, t, :])
            for c in range(KC):
                for m, kind in enumerate(("ga", "ba", "gg", "bg")):
                    if c >= 2:
                        pe.wait_ge(*((mg_sig, 2 * (c - 2) + m // 2 + 1) if m % 2 == 0
                                     else (mg_out, 2 * (c - 2) + m // 2 + 1)))
                    if c == 0 and kind == "bg":
                        pe.wait_ge(gr_out, KC)
                    w = slot2(kind, c // 2)
                    src = dict(ga=aT, gg=aT, ba=attT, bg=OT)[kind]
                    nk = 4 if kind == "ba" else KC
                    for k in range(nk):
                        last = mm(ps[:, 4 * (c % 2) + m, :], w[:, k, P * (c % 2):P * (c % 2 + 1)], src[:, k, :],
                                  start=(k == 0), stop=(k == nk - 1))
                    last.then_inc(mg_done, 1)
            pe.wait_ge(mg_out, 2 * KC)
            for c in range(4):
                slot2("wo", c)
            for i in range(2 * XT):
                t, a = divmod(i, 2)
                if i >= 4:
                    pe.wait_ge(wo2_out, i - 3)
                for k in range(KC):
                    last = mm(ps[:, i % 4, :], mT[:, k, P * t:P * (t + 1)],
                              rows256(G2[("wo", k // 2)])[:, k % 2, 512 * a:512 * (a + 1)],
                              start=(k == 0), stop=(k == KC - 1))
                last.then_inc(wo2_done, 1)

            turn_norm(2, lambda t: XN[:, t, :])
            pe.wait_ge(wo2_out, 2 * XT)
            for k in range(KC):
                for t in range(XT):
                    last = mm(ps[32 * t:32 * t + EXPERTS, 1, 0:P], router[:, k, :], aT2[:, k, P * t:P * (t + 1)],
                              start=(k == 0), stop=(k == KC - 1))
            last.then_inc(rt_done, 1)
            pe.wait_ge(rt_out, 1)
            for t in range(XT):
                last = T(ps[:, 0, EXPERTS * t:EXPERTS * (t + 1)], affT[:, P * t:P * (t + 1)],
                         ident[0:EXPERTS, 0:EXPERTS])
            last.then_inc(rl_done, 1)
            pe.wait_ge(aff_done, 1)
            for t in range(XT):
                last = T(ps[0:EXPERTS, 1, P * t:P * (t + 1)], aff[:, t, :], ident)
            last.then_inc(affT_done, 1)
            pe.wait_ge(third_in, 48)
            for n in range(2 * XT):
                t, a = divmod(n, 2)
                if n >= 4:
                    pe.wait_ge(em_out, n - 3)
                for k in range(PLE // P):
                    last = mm(ps[:, 4 + n % 4, :], pT[:, k, P * t:P * (t + 1)], w_p[:, k, 512 * a:512 * (a + 1)],
                              start=(k == 0), stop=(k == PLE // P - 1))
                last.then_inc(em_done, 1)
            pe.wait_ge(rank_done, 1)
            for t in range(XT):
                last = T(ps[:, 2, EXPERTS * t:EXPERTS * (t + 1)], takenT[:, P * t:P * (t + 1)],
                         ident[0:EXPERTS, 0:EXPERTS])
            last.then_inc(rankT_done, 1)

            def gather(i):
                for c in range(KC):
                    for t in range(XT):
                        last = mm(ps[:, c // 4, P * (c % 4):P * (c % 4 + 1)], XN[:, t, P * c:P * (c + 1)],
                                  sel_pair[:, t, i, :], start=(t == 0), stop=(t == XT - 1))
                    if c % 4 == 3:
                        last.then_inc(gather_done, 1)

            def experts(i):
                for u in range(2):
                    if u == 0:
                        pe.wait_ge(xe_set, 2 * i + 2)
                    for m, (bank, done) in enumerate(((u, e_gate), (2 + u, e_up))):
                        if u == 0 and m == 1:
                            pe.wait_ge(selw_done, XT * i + XT)
                        for b in range(4):
                            pe.wait_ge(eslot_in(4 * m + b), 32 * i + 16 * (LOADED[4 * m + b] + u + 1))
                            settle(pe, "pe")
                            for k in (2 * b, 2 * b + 1):
                                for x_ in range(2):
                                    last = mm(ps[64 * x_:64 * x_ + 64, bank, :], xe[:, k, CAP * u:CAP * (u + 1)],
                                              eslot(4 * m + b)[:, k % 2, 512 * x_:512 * (x_ + 1)],
                                              start=(k == 0), stop=(k == KC - 1))
                            last.then_inc(done, 1)
                    if u == 0:
                        for t in range(XT):
                            last = T(ps[:, 7, P * t:P * (t + 1)], selw[:, t, :], ident)
                        last.then_inc(gt_done, 1)
                    pe.wait_ge(e_hid, 2 * i + u + 1)
                    for c in range(4):
                        last = T(ps[:, 4, P * c:P * (c + 1)], hid[:, u, P * c:P * (c + 1)], ident)
                    last.then_inc(e_turn, 1)
                    pe.wait_ge(e_hidT, 2 * i + u + 1)
                    for b in range(4):
                        pe.wait_ge(eslot_in(8 + b), 32 * i + 16 * (LOADED[8 + b] + u + 1))
                        settle(pe, "pe")
                        for k in (2 * b, 2 * b + 1):
                            for x_ in range(2):
                                last = mm(ps[64 * x_:64 * x_ + 64, 5 + u, :],
                                          hidT[:, k % 4, 64 * (k // 4):64 * (k // 4 + 1)],
                                          eslot(8 + b)[:, k % 2, 512 * x_:512 * (x_ + 1)],
                                          start=(k == 0), stop=(k == KC - 1))
                        last.then_inc(e_down, 1)

            def combine(i):
                pe.wait_ge(e_y, 2 * i + 2)
                pe.wait_ge(e_y2, 2 * i + 2)
                pe.wait_ge(gt_out, i + 1)
                for n in range(2 * XT):
                    t, a = divmod(n, 2)
                    if n >= 4:
                        pe.wait_ge(cb_out, 2 * XT * i + n - 3)
                        settle(pe, "pe")
                    mm(ps[:, (2, 3, 4, 7)[n % 4], :], GT[:, P * t:P * (t + 1)], Y[:, 512 * a:512 * (a + 1)],
                       start=True, stop=True).then_inc(cb_done, 1)

            pe.wait_ge(sel_done, XT)
            pe.wait_ge(em_out, 2 * XT)
            gather(0)
            with pe.Fori(0, PAIRS - 1) as i:
                experts(i)
                pe.wait_ge(sel_done, 2 * XT)
                gather(i + 1)
                combine(i)
            experts(PAIRS - 1)
            combine(PAIRS - 1)
            def ple_gate(t):
                pe.wait_ge(nt_out, 6 * XT + 2 * t + 2)
                for a in range(2):
                    n = 2 * t + a
                    if n >= 4:
                        pe.wait_ge(pl_out, n - 3)
                    for k in range(KC):
                        last = mm(ps[:, n % 4, :], aT3[:, k, P * t:P * (t + 1)],
                                  eslot(k // 2)[:, k % 2, 512 * a:512 * (a + 1)],
                                  start=(k == 0), stop=(k == KC - 1))
                    last.then_inc(pl_done, 1)

            turn_norm(3, lambda t: xn3[:, t % 2, :], tiles=(0, 1))
            pe.wait_ge(cb_out, 2 * XT * PAIRS)
            for c in range(4):
                pe.wait_ge(eslot_in(c), 16 * (LOADED[c] + EXPERTS + 1))
            ple_gate(0)
            turn_norm(3, lambda t: xn3[:, t % 2, :], tiles=(2, 3))
            for t in range(1, XT):
                ple_gate(t)

        @block.scalar
        def _(act):
            A = nc.scalar.activation
            act.wait_ge(consts_set, 1)
            act.wait_ge(h_in[ORDER[1]], 16)
            act.dma_start(rope[:, :, :], rope_d).then_inc(consts_in, 16)
            act.dma_start(cst[:, 4:NC, :], cst_d[:, 4:NC, :]).then_inc(consts_in, 16)
            act.dma_start(gains[:, :, :], B["gains"]).then_inc(consts_in, 16)
            act.dma_start(router[:, :, :], B["router"]).then_inc(consts_in, 16)
            act.dma_start(sink[:, 0, :], B["sink"].partition_broadcast(P)).then_inc(consts_in, 16)
            with act.Fori(0, DEPTH) as l:
                for o, t in enumerate(ORDER):
                    rows, q0 = rows_of(t)
                    act.wait_ge(turned, 2 * (l * TILES + o) + 1)
                    A(hT[:, 0:4, q0:q0 + rows],
                      ps[:, 2 * (o % 2), :].rearrange("p (c n) -> p c n", c=4)[:, :, 0:rows],
                      ACT.Copy).then_inc(turned_act, 1)

                def item(n):
                    kind, c = ITEMS[n]
                    act.wait_ge(proj_done, l * NI + n + 1)
                    src = pair(n % 2)
                    if n in RAW:
                        u = RAW.index(n)
                        if u >= 2:
                            act.wait_ge(raw_used, l * NRAW + u - 1)
                        A(halves(raw[:, u % 2, :]), src,
                          ACT.Sigmoid if kind == "g" else ACT.Copy).then_inc(proj_out, 1)
                    elif kind == "wi":
                        for g in range(Q4):
                            last = A(wiT[:, L // Q4 * g:L // Q4 * (g + 1)],
                                     ps[32 * g:32 * g + HEADS, 2 * (n % 2), 0:L // Q4],
                                     ACT.Copy, scale=float(HEADS ** -0.5))
                        last.then_inc(proj_out, 1)
                    elif kind == "wt":
                        A(wi, ps[:, 2 * (n % 2), 0:32], ACT.Copy).then_inc(proj_out, 1)
                    elif kind == "a":
                        A(halves(uT[:, c, TAPS - 1:TAPS - 1 + L]), src, ACT.Copy).then_inc(proj_out, 1)
                    elif kind == "v" and c == XT:
                        for g in range(Q4):
                            last = A(V[0:N_META, c, P * g:P * (g + 1)],
                                     ps[32 * g:32 * g + N_META, 2 * (n % 2), 0:P], ACT.Copy)
                        last.then_inc(proj_out, 1)
                    elif kind == "v":
                        A(V[:, c, :], ps[:, 2 * (n % 2), :], ACT.Copy).then_inc(proj_out, 1)
                    else:
                        A(halves(zaT[:, c, :]), src, ACT.Silu).then_inc(proj_out, 1)

                for n in range(NI):
                    item(n)
                    if n == IDX_AFTER:
                        for j in range(NIDX):
                            t = j // HEADS
                            act.wait_ge(idx_done, l * NIDX + j + 1)
                            if j >= 4:
                                act.wait_ge(idx_added, l * NIDX + j - 3)
                            dst, src = span(pr[:, j % 4, :], 4 + 2 * (j % 2), P, KEYS[t])
                            A(dst, src, ACT.Relu, scale=HEAD_DIM ** -0.5).then_inc(idx_relu, 1)
                for j in range(NATT + 2):
                    if j % 4 == 0 and 4 <= j <= 4 * NZ:
                        c, a = divmod(j // 4 - 1, 2)
                        act.wait_ge(zc_done, l * NZ + j // 4)
                        A(zcT[:, c, HALF * a:HALF * (a + 1)], ps[:, 1, 0:HALF], ACT.Copy).then_inc(zc_out, 1)
                    if j < NATT:
                        t, h, n, q0, keys, full = att(j)
                        act.wait_ge(at_masked, l * NATT + j + 1)
                        A(pr[0:n, j % 4, 0:keys], pr[0:n, j % 4, 0:keys], ACT.Exp, bias=neg_max[0:n, j:j + 1],
                          scale=-1.0, accum_out=row_sum[0:n, j:j + 1]).then_inc(at_exp, 1)
                    i = j - 2
                    if i >= 0 and att(i)[5]:
                        full = att(i)[5]
                        act.wait_ge(at_turned, l * NATT + i + 1)
                        if i >= 4:
                            act.wait_ge(at_value, l * NATT + i - 3)
                        A(prT[:, i % 4, 0:full, :], ps[:, 0, 0:P * full].rearrange("p (b n) -> p b n", n=P),
                          ACT.Copy).then_inc(at_full, 1)
                act.wait_ge(zc_out, l * NZ + NZ)
                for c in range(4):
                    A(zcT[:, c, :], zcT[:, c, :], ACT.Silu).then_inc(zc_silu, 1)
                for c in range(4):
                    act.wait_ge(cn_centred, 4 * l + c + 1)
                    A(pr[:, c, :], yT[:, c, :], ACT.Square).then_inc(cn_square, 1)
                act.wait_ge(cn_var, l + 1)
                A(halves(raw[:, 0, :]), pair(1), ACT.Sqrt, bias=eps_ln).then_inc(cn_std, 1)
                for c in range(4):
                    act.wait_ge(cn_scaled, 4 * l + c + 1)
                    A(yT[:, c, :], yT[:, c, :], ACT.Silu, bias=convp[:, c, TAPS + 2:TAPS + 3],
                      scale=convp[:, c, TAPS + 1:TAPS + 2]).then_inc(cn_silu, 1)
                for o, t in enumerate(ORDER):
                    rows, _ = rows_of(t)
                    act.wait_ge(ln_var, l * TILES + o + 1)
                    A(ln_std_v[0:rows, t:t + 1], mean_var[0:rows, 2 * t + 1:2 * t + 2], ACT.Sqrt,
                      bias=eps_ln[0:rows, :]).then_inc(ln_std, 1)

            steps = Steps()

            def norm_square(w, t, scratch, src):
                A(scratch, src, ACT.Square, accum_out=norm_sq[:, XT * w + t:XT * w + t + 1]).then_inc(nq_done, 1)
                act.wait_ge(nq_done, XT * w + t + 1)
                A(norm_std[:, XT * w + t:XT * w + t + 1], norm_sq[:, XT * w + t:XT * w + t + 1], ACT.Sqrt,
                  bias=eps_rms, scale=1.0 / D_MODEL).then_inc(ns_done, 1)

            for t in range(XT):
                act.wait_ge(h_done, DEPTH * TILES + ORDER.index(t) + 1)
                if t >= 2:
                    act.wait_ge(nt_done, 2 * (t - 1))
                norm_square(0, t, xn[:, t % 2, :], H[:, t, :])
            act.wait_ge(rt_arg, 1)
            A(rope2[:, 1, :], angle[:, :], ACT.Sin).then_inc(rt_sin, 1)
            A(rope2[:, 0, :], turns[:, :], ACT.Sin, bias=cst[:, 13, 65:66]).then_inc(rt_sin, 1)
            def item2_out(n):
                kind, c = ITEMS2[n]
                act.wait_ge(p2_done, n + 1)
                src = ps[:, n % 4, :]
                if n in ROPED2:
                    r = ROPED2.index(n)
                    if r >= 2:
                        act.wait_ge(raw2_used, r - 1)
                    A(raw2[:, r % 2, :], src, ACT.Copy).then_inc(p2_out, 1)
                elif kind == "av":
                    A(av[:, :, :], src.rearrange("p (t n) -> p t n", t=XT), ACT.Copy).then_inc(p2_out, 1)
                elif kind == "z":
                    A(zT[:, :], src[0:64, :], ACT.Identity, bias=cst[0:64, 13, 66:67]).then_inc(p2_out, 1)
                else:
                    g = 0 if kind == "gq" else 1
                    A(gqk[:, g, c, :], ps[:, 2 + n % 2, :], ACT.Copy,
                      scale=G_DK ** -0.5 if g == 0 else 1.0).then_inc(p2_out, 1)

            for n in range(WIN_FROM + 1):
                item2_out(n)
            for j in range(NW + 2):
                if j % 4 == 0 and 4 <= j < NW:
                    item2_out(WIN_FROM + j // 4)
                if j < NW:
                    t, h, k0, cnt = win(j)
                    act.wait_ge(w_masked, j + 1)
                    A(pr2[:, j % 4, 0:P * cnt], pr2[:, j % 4, 0:P * cnt], ACT.Exp, bias=neg_max2[:, j:j + 1],
                      scale=-1.0, accum_out=sum2[:, j:j + 1]).then_inc(w_exp, 1)
                    A(sink2[:, j:j + 1], sink[:, 0, h:h + 1], ACT.Exp, bias=neg_max2[:, j:j + 1])\
                        .then_inc(w_sink, 1)
                i = j - 2
                if i >= 0:
                    act.wait_ge(w_turned, i + 1)
                    if i >= 4:
                        act.wait_ge(w_value, i - 3)
                    n = P * win(i)[3]
                    A(pr2T[:, i % 4, 0:n], ps[:, 6 + i % 2, 0:n], ACT.Copy).then_inc(w_out_t, 1)

            def gate_log(i):
                act.wait_ge(gz_done, i + 1)
                if i >= 1:
                    act.wait_ge(gl_set, i)
                else:
                    act.wait_ge(w_att, XT)
                g = gate[:, 0, :]
                A(g, ps[:, 0, :], ACT.Abs).then_inc(act_step, steps.one())
                act.wait_ge(act_step, steps.now())
                A(g, g, ACT.Exp, scale=-1.0).then_inc(act_step, steps.one())
                act.wait_ge(act_step, steps.now())
                A(g, g, ACT.Ln, bias=ones[:, 0:1]).then_inc(gl_log, 1)

            def flat(b):
                return b[:, :, :].rearrange("p h n -> p (h n)")

            def gate_exp(i):
                act.wait_ge(gl_cum, i + 1)
                if i >= 1:
                    act.wait_ge(gl_qk, i)
                    act.wait_ge(gl_att, i)
                src = ps[:, 2 + i % 2, :]
                A(flat(decay[0]), src, ACT.Copy).then_inc(act_step, steps.one())
                A(flat(decay[1]), src, ACT.Exp).then_inc(act_step, steps.one())
                A(flat(decay[2]), src, ACT.Exp, scale=-1.0).then_inc(gl_exp, 1)

            gate_log(0)
            for i in range(len(TD)):
                gate_exp(i)
                act.wait_ge(gl_rest, i + 1)
                A(flat(decay[3]), flat(decay[3]), ACT.Exp).then_inc(gl_rexp, 1)
                if i + 1 < len(TD):
                    gate_log(i + 1)
                act.wait_ge(gl_turn, i + 1)
                t, d = TD[i]
                A(kE[:, d, t, :], ps[:, 6 + i % 2, :], ACT.Copy).then_inc(gl_kout, 1)
            for c in range(KC):
                act.wait_ge(gr_done, c + 1)
                A(zr[c], ps[:, gr_bank(c), :], ACT.Silu).then_inc(gr_silu, 1)
                n = c - XT
                if n >= 0:
                    act.wait_ge(o_out, XT + n + 1)
                    for h in range(G_HEADS):
                        A(squares[:, h % 2, :], O[:, n, G_DV * h:G_DV * (h + 1)], ACT.Square,
                          accum_out=o_sq[:, 4 * n + h:4 * n + h + 1]).then_inc(o_sqd, 1)
                        act.wait_ge(o_sqd, 4 * n + h + 1)
                    A(o_std[:, 4 * n:4 * n + 4], o_sq[:, 4 * n:4 * n + 4], ACT.Sqrt, bias=eps_rms, scale=1.0 / G_DV)\
                        .then_inc(o_stdd, 1)
            for c in range(KC):
                for m in range(2):
                    i = 2 * c + m
                    act.wait_ge(mg_done, 4 * c + 2 * m + 1)
                    if c >= 2:
                        act.wait_ge(mg_out, i - 3)
                    A(side[:, 2 + i % 4, :], ps[:, 4 * (c % 2) + 2 * m, :], ACT.Sigmoid).then_inc(mg_sig, 1)
            for t in range(XT):
                act.wait_ge(wo2_out, 2 * (t + 1))
                norm_square(1, t, XN[:, t, :], H[:, t, :])
            act.wait_ge(rl_sub, 1)
            A(logit, logit, ACT.Exp).then_inc(rl_exp, 1)
            for n in range(2 * XT):
                act.wait_ge(em_done, n + 1)
                t, a = divmod(n, 2)
                A(embedded[:, t, 512 * a:512 * (a + 1)], ps[:, 4 + n % 4, :], ACT.Copy).then_inc(em_out, 1)
            with act.Fori(0, PAIRS) as i:
                for u in range(2):
                    act.wait_ge(e_gate, 8 * i + 4 * u + 4)
                    A(hid[:, u, :], ps[:, u, :], ACT.Silu).then_inc(e_silu, 1)
                    act.wait_ge(e_turn, 2 * i + u + 1)
                    A(hidT[:, :, :], ps[:, 4, :].rearrange("p (c n) -> p c n", c=4), ACT.Copy).then_inc(e_hidT, 1)
                    act.wait_ge(e_down, 8 * i + 4 * u + 4)
                    A(Y[64 * u:64 * u + 64, 512:1024], ps[64:128, 5 + u, :], ACT.Copy).then_inc(e_y2, 1)
            for t in range(XT):
                act.wait_ge(cb_out, 2 * XT * (PAIRS - 1) + 2 * (t + 1))
                if t >= 2:
                    act.wait_ge(nt_done, 6 * XT + 2 * (t - 1))
                norm_square(2, t, xn3[:, t % 2, :], H[:, t, :])
            def final_square(t):
                act.wait_ge(pl_out, 2 * (t + 1))
                if t >= 2:
                    act.wait_ge(stored[t % 2], 16 * (t // 2))
                norm_square(3, t, outb[:, t % 2, :], H[:, t, :])

            for i in range(2 * XT):
                if i >= 2 and i % 2 == 0:
                    final_square(i // 2 - 1)
                act.wait_ge(pl_done, i + 1)
                if i >= 2:
                    act.wait_ge(pl_out, i - 1)
                A(emb[:, i % 2, :], ps[:, i % 4, :], ACT.Sigmoid).then_inc(pl_sig, 1)
            final_square(XT - 1)

        @block.gpsimd
        def _(pool):
            nc.gpsimd.memset(uT[:, :, 0:TAPS - 1], 0.0).then_inc(pool_step, 1)

            pool.wait_ge(w_att, XT)
            nc.gpsimd.memset(AT[:, :, :, :], 0.0).then_inc(gl_zero, 1)

        @block.vector
        def _(dve):
            vec = nc.vector
            nc.vector.memset(small[:, :], 0.0).then_inc(dve_step, 1)
            dve.wait_ge(dve_step, 1)
            nc.vector.memset(eps_rms, RMS_EPS).then_inc(dve_step, 1)
            nc.vector.memset(eps_ln, LN_EPS).then_inc(consts_set, 1)
            dve.wait_ge(consts_set, 1)
            for t in ORDER:
                dve.wait_ge(h_in[t], 16)
                dve.sem_inc(h_done, 1)
            dve.wait_ge(pool_step, 1)
            STEPS1 = 361
            with dve.Fori(0, DEPTH) as l:
                k = Steps(l * STEPS1 + 2)
                for o, t in enumerate(ORDER):
                    rows, q0 = rows_of(t)
                    dve.wait_ge(turned, 2 * (l * TILES + o) + 2)
                    vec.tensor_copy(hT[:, 4:8, q0:q0 + rows],
                                   ps[:, 1 + 2 * (o % 2), :].rearrange("p (c n) -> p c n", c=4)[:, :, 0:rows])\
                        .then_inc(turned_dve, 1)

                def rope_item(r):
                    n = ROPED[r]
                    kind, c = ITEMS[n]
                    if r == 0:
                        dve.wait_ge(consts_in, 80)
                    raw_r = raw[:, RAW.index(n) % 2, :]
                    dst = kiT[:, :] if kind == "ki" else dict(qi=qiT, q=qT, k=kT)[kind][:, c, :]
                    dve.wait_ge(rot_done, l * NROT + r + 1)
                    vec.tensor_tensor(halves(dst), pair(2 + r % 2), halves(rope[:, 1, :]), ALU.mult)\
                        .then_inc(dve_step, k.one())
                    vec.tensor_tensor(raw_r, raw_r, rope[:, 0, :], ALU.mult).then_inc(dve_step, k.one())
                    dve.wait_ge(dve_step, k.now())
                    vec.tensor_tensor(dst, dst, raw_r, ALU.add).then_inc(raw_used, 1)

                def gate_item(c):
                    n = ITEM[("g", c)]
                    dve.wait_ge(proj_out, l * NI + n + 1)
                    vec.tensor_tensor(uT[:, c, TAPS - 1:TAPS - 1 + L], uT[:, c, TAPS - 1:TAPS - 1 + L],
                                     raw[:, RAW.index(n) % 2, :], ALU.mult).then_inc(raw_used, 1)
                    if c == 3:
                        dve.wait_ge(raw_used, l * NRAW + RAW.index(n) + 1)
                        settle(dve, "dve")

                for r in range(5):
                    rope_item(r)
                for t in range(XT):
                    vec.memset(score[t][:, 0:DUMMIES], DUMMY_SCORE).then_inc(dve_step, k.one())
                for j in range(NIDX):
                    t, h = divmod(j, HEADS)
                    s = score[t][:, DUMMIES:]
                    r_ = pr[:, j % 4, 0:KEYS[t]]
                    w = wi[:, 8 * t + h:8 * t + h + 1]
                    dve.wait_ge(idx_relu, l * NIDX + j + 1)
                    if h == 0:
                        vec.tensor_scalar(s, r_, w, None, ALU.mult).then_inc(idx_added, 1)
                    else:
                        dve.wait_ge(idx_added, l * NIDX + j)
                        vec.scalar_tensor_tensor(out=s, in0=r_, scalar=w, in1=s, op0=ALU.mult, op1=ALU.add)\
                            .then_inc(idx_added, 1)
                    if h == HEADS - 1:
                        dve.wait_ge(idx_added, l * NIDX + j + 1)
                        d = score[t][:, DUMMIES + N_META + P * t:]
                        vec.tensor_tensor(d, d, future_score, ALU.add).then_inc(dve_step, k.one())

                def top_round():
                    dve.wait_ge(dve_step, k.now())
                    settle(dve, "dve")
                    for t in range(XT):
                        vec.max(top8[:, 8 * t:8 * t + 8], score[t][:, :]).then_inc(dve_step, k.one())
                    for t in range(XT):
                        dve.wait_ge(dve_step, k.now() - XT + 1)
                        settle(dve, "dve")
                        vec.match_replace(score[t][:, :], top8[:, 8 * t:8 * t + 8], score[t][:, :], TAKEN)\
                            .then_inc(dve_step, k.one())

                conv_marks = {}

                def conv_taps(first, end):
                    for u in range(first, end):
                        j, c = divmod(u, 4)
                        done = (conv_done, 1) if j == TAPS - 1 else (dve_step, k.one())
                        if j == 0:
                            vec.tensor_scalar(yT[:, c, :], uT[:, c, 0:L], convp[:, c, 0:1],
                                             convp[:, c, TAPS:TAPS + 1], ALU.mult, ALU.add).then_inc(*done)
                        else:
                            dve.wait_ge(dve_step, k.at(conv_marks[c]))
                            vec.scalar_tensor_tensor(out=yT[:, c, :], in0=uT[:, c, j:j + L],
                                                    scalar=convp[:, c, j:j + 1], in1=yT[:, c, :],
                                                    op0=ALU.mult, op1=ALU.add).then_inc(*done)
                        conv_marks[c] = k.n

                dve.wait_ge(params_in, 32 * (l + 1))
                rounds, taps = 0, 0
                for n in range(NI):
                    kind, c = ITEMS[n]
                    if kind == "g":
                        gate_item(c)
                    elif kind in ("q", "k"):
                        rope_item(ROPED.index(n))
                    else:
                        continue
                    for _ in range(2):
                        if rounds < ROUNDS:
                            top_round()
                            rounds += 1
                        elif n != ROPED[-1]:
                            conv_taps(taps, taps + 4)
                            taps += 4
                while rounds < ROUNDS:
                    top_round()
                    rounds += 1
                dve.wait_ge(dve_step, k.now())
                for t in range(XT):
                    vec.tensor_scalar(score[t][:, :], score[t][:, :], TAKEN, HIDDEN, ALU.not_equal, ALU.mult)\
                        .then_inc(dve_step, k.one())
                dve.wait_ge(dve_step, k.now())
                d = score[0][:, DUMMIES + N_META:]
                vec.tensor_tensor(d, d, future_hidden, ALU.add).then_inc(dve_step, k.one())

                conv_taps(taps, 4 * TAPS - LATE_TAPS)

                def masked(j):
                    t, h, n, q0, keys, _ = att(j)
                    dve.wait_ge(at_score, l * NATT + j + 1)
                    if j >= 4:
                        dve.wait_ge(at_turned, l * NATT + j - 3)
                    if j == 0:
                        dve.wait_ge(dve_step, k.now())
                    dst, src = span(pr[:, j % 4, :], 4 + 2 * (j % 2), n, keys)
                    m = score[t][0:n, DUMMIES:] if t < XT else future_hidden[0:n, 0:N_META]
                    if keys > 512:
                        m = halves(m)
                    settle(dve, "dve")
                    vec.tensor_tensor_reduce(dst, src, m, -(HEAD_DIM ** -0.5), 3.0e38, ALU.add, ALU.min,
                                            neg_max[0:n, j:j + 1]).then_inc(at_masked, 1)

                def scaled(j):
                    t, h, n, q0, keys, _ = att(j)
                    dve.wait_ge(at_exp, l * NATT + j + 1)
                    vec.reciprocal(row_inv[0:n, j:j + 1], row_sum[0:n, j:j + 1]).then_inc(dve_step, k.one())
                    dve.wait_ge(dve_step, k.now())
                    vec.tensor_scalar(pr[0:n, j % 4, 0:keys], pr[0:n, j % 4, 0:keys], row_inv[0:n, j:j + 1], None,
                                     ALU.mult).then_inc(at_prob, 1)

                def rest(j):
                    n = att(j)[2]
                    dve.wait_ge(at_turned, l * NATT + j + 1)
                    if j >= 4:
                        dve.wait_ge(at_value, l * NATT + j - 3)
                    vec.tensor_copy(prR[:, j % 4, 0:n], ps[0:N_META, 2, P * (j % 4):P * (j % 4) + n])\
                        .then_inc(at_rest, 1)

                for j in range(NATT + 4):
                    if j < NATT:
                        masked(j)
                    if 1 <= j <= NATT:
                        scaled(j - 1)
                    if 2 <= j < NATT + 2:
                        rest(j - 2)
                    if j < NATT:
                        conv_taps(4 * TAPS - LATE_TAPS + j * LATE_TAPS // NATT,
                                  4 * TAPS - LATE_TAPS + (j + 1) * LATE_TAPS // NATT)
                    if j >= 4 and (j - 4) % HEADS == HEADS - 1:
                        t = (j - 4) // HEADS
                        n, q0 = rows_of(t)
                        dve.wait_ge(at_value, l * NATT + HEADS * (t + 1))
                        dve.wait_ge(proj_out, l * NI + NI)
                        vec.tensor_tensor(yT[:, 4:8, q0:q0 + n],
                                         ps[:, 3, :].rearrange("p (c n) -> p c n", c=4)[:, :, 0:n],
                                         zaT[:, :, q0:q0 + n], ALU.mult).then_inc(attn_y, 1)

                dve.wait_ge(cn_mean, l + 1)
                for c in range(4):
                    vec.tensor_tensor(halves(yT[:, c, :]), halves(yT[:, c, :]), pair(0), ALU.subtract)\
                        .then_inc(cn_centred, 1)
                dve.wait_ge(cn_std, l + 1)
                vec.reciprocal(raw[:, 1, :], raw[:, 0, :]).then_inc(dve_step, k.one())
                dve.wait_ge(dve_step, k.now())
                for c in range(4):
                    vec.tensor_tensor(yT[:, c, :], yT[:, c, :], raw[:, 1, :], ALU.mult).then_inc(cn_scaled, 1)
                for c in range(4):
                    dve.wait_ge(cn_silu, 4 * l + c + 1)
                    if c == 0:
                        dve.wait_ge(zc_silu, 4 * l + 4)
                    vec.tensor_tensor(yT[:, c, :], yT[:, c, :], zcT[:, c, :], ALU.mult).then_inc(conv_y, 1)
                for o, t in enumerate(ORDER):
                    rows, _ = rows_of(t)
                    ht = H[0:rows, t, :]
                    for m in range(2 if t < XT else 1):
                        i = UNITS.index((t, m))
                        dve.wait_ge(wo_done, l * NU + i + 1 + WO_FIRST)
                        if t < XT:
                            hm = H[0:rows, t, 512 * m:512 * (m + 1)]
                            last = vec.scalar_tensor_tensor(out=hm, in0=hm, scalar=ALPHA, in1=ps[0:rows, 4 + i % 4, :],
                                                           op0=ALU.mult, op1=ALU.add)
                        else:
                            for g in range(Q4):
                                hm = H[0:rows, t, WCOLS * g:WCOLS * (g + 1)]
                                last = vec.scalar_tensor_tensor(out=hm, in0=hm, scalar=ALPHA,
                                                               in1=ps[32 * g:32 * g + rows, 4 + i % 4, 0:WCOLS],
                                                               op0=ALU.mult, op1=ALU.add)
                        last.then_inc(wo_added, 1)
                    dve.wait_ge(wo_added, l * NU + i + 1)
                    for a in range(2):
                        vec.bn_stats(stats[0:rows, 6 * a:6 * a + 6], H[0:rows, t, 512 * a:512 * (a + 1)])\
                            .then_inc(dve_step, k.one())
                    dve.wait_ge(dve_step, k.now())
                    settle(dve, "dve")
                    vec.bn_aggr(mean_var[0:rows, 2 * t:2 * t + 2], stats[0:rows, :]).then_inc(ln_var, 1)
                    dve.wait_ge(ln_std, l * TILES + o + 1)
                    vec.reciprocal(ln_inv[0:rows, t:t + 1], ln_std_v[0:rows, t:t + 1]).then_inc(dve_step, k.one())
                    dve.wait_ge(dve_step, k.now())
                    vec.tensor_scalar(ht, ht, mean_var[0:rows, 2 * t:2 * t + 1], ln_inv[0:rows, t:t + 1],
                                     ALU.subtract, ALU.mult).then_inc(dve_step, k.one())
                    dve.wait_ge(dve_step, k.now())
                    if t == 0:
                        dve.wait_ge(post_in, 16 * (l + 1))
                    vec.tensor_tensor(ht, ht, post[0:rows, 0, :], ALU.mult).then_inc(dve_step, k.one())
                    dve.wait_ge(dve_step, k.now())
                    vec.tensor_tensor(ht, ht, post[0:rows, 1, :], ALU.add).then_inc(h_done, 1)
                assert k.n == STEPS1, k.n

            k = Steps(DEPTH * STEPS1 + 2)
            TT, TS, STT = vec.tensor_tensor, vec.tensor_scalar, vec.scalar_tensor_tensor

            def step(instruction):
                instruction.then_inc(dve_step, k.one())
                dve.wait_ge(dve_step, k.now())

            def norm_scale(w, t, dst, src):
                dve.wait_ge(ns_done, XT * w + t + 1)
                inv = norm_inv[:, t:t + 1]
                step(vec.reciprocal(inv, norm_std[:, XT * w + t:XT * w + t + 1]))
                TS(dst, src, inv, None, ALU.mult).then_inc(xn_done, 1)

            def norm_out(v, dst, t):
                for hf in range(2):
                    dve.wait_ge(nt_done, 2 * XT * v + 2 * t + hf + 1)
                    TT(dst[:, 4 * hf:4 * hf + 4, P * t:P * (t + 1)],
                       ps[:, 4 + (2 * t + hf) % 4, :].rearrange("p (c n) -> p c n", c=4),
                       gains[:, v, 4 * hf:4 * hf + 4].unsqueeze(2).to_broadcast([P, 4, P]), ALU.mult)\
                        .then_inc(nt_out, 1)

            dve.wait_ge(h_done, TILES + DEPTH * TILES)
            TS(sink[:, 1, :], sink[:, 0, :], -1.0, None, ALU.mult).then_inc(dve_step, k.one())
            for t in range(XT):
                norm_scale(0, t, xn[:, t % 2, :], H[:, t, :])
                norm_out(0, aT, t)
            dve.wait_ge(second_in, 32)
            step(vec.tensor_copy(pos[:, :], pos[:, :].bitcast(I32)))
            step(TS(angle[:, :], pos[:, :], cst[:, 13, 64:65], None, ALU.mult))
            step(TS(turns[:, :], angle[:, :], float(0.5 / np.pi), FAR, ALU.mult, ALU.add))
            step(TS(turns[:, :], turns[:, :], -FAR, None, ALU.add))
            for part in TURN:
                step(STT(out=angle[:, :], in0=turns[:, :], scalar=-part, in1=angle[:, :], op0=ALU.mult, op1=ALU.add))
            step(TS(angle[:, :], angle[:, :], 3.1415925, -3.1415925, ALU.min, ALU.max))
            dve.wait_ge(dve_step, k.now())
            STT(out=turns[:, :], in0=angle[:, :], scalar=-1.0, in1=angle[:, :], op0=ALU.mult, op1=ALU.min)\
                .then_inc(rt_arg, 1)
            dve.wait_ge(rt_sin, 2)
            for r, n in enumerate(ROPED2):
                kind, c = ITEMS2[n]
                dst = (akT if kind == "ak" else aqT)[:, c, :]
                dve.wait_ge(rot2_done, r + 1)
                TT(dst, ps[:, 4 + r % 2, :], rope2[:, 1, :], ALU.mult).then_inc(dve_step, k.one())
                step(TT(raw2[:, r % 2, :], raw2[:, r % 2, :], rope2[:, 0, :], ALU.mult))
                TT(dst, dst, raw2[:, r % 2, :], ALU.add).then_inc(raw2_used, 1)

            for j in range(NW + 4):
                if j < NW:
                    t, h, k0, cnt = win(j)
                    dve.wait_ge(w_score, j + 1)
                    if j >= 4:
                        dve.wait_ge(w_turned, j - 3)
                    m0 = P * (k0 - t + 1)
                    vec.tensor_tensor_reduce(pr2[:, j % 4, 0:P * cnt], ps[:, 4 + j % 2, 0:P * cnt],
                                            window[:, m0:m0 + P * cnt], -(HEAD_DIM ** -0.5), sink[:, 1, h:h + 1],
                                            ALU.add, ALU.min, neg_max2[:, j:j + 1]).then_inc(w_masked, 1)
                i = j - 1
                if 0 <= i < NW:
                    n = P * win(i)[3]
                    dve.wait_ge(w_exp, i + 1)
                    dve.wait_ge(w_sink, i + 1)
                    step(TT(den2[:, i:i + 1], sum2[:, i:i + 1], sink2[:, i:i + 1], ALU.add))
                    step(vec.reciprocal(inv2[:, i:i + 1], den2[:, i:i + 1]))
                    TS(pr2[:, i % 4, 0:n], pr2[:, i % 4, 0:n], inv2[:, i:i + 1], None, ALU.mult).then_inc(w_prob, 1)
                if j >= 4 and (j - 4) % HEADS == HEADS - 1:
                    t = (j - 4) // HEADS
                    dve.wait_ge(w_value, HEADS * (t + 1))
                    vec.tensor_copy(attT[:, :, P * t:P * (t + 1)], ps[:, t % 2, :].rearrange("p (c n) -> p c n", c=4))\
                        .then_inc(w_att, 1)

            def gate_set(i):
                dve.wait_ge(gl_log, i + 1)
                if i >= 1:
                    dve.wait_ge(gl_cum, i)
                STT(out=gate[:, 1, :], in0=ps[:, 0, :], scalar=0.0, in1=gate[:, 0, :], op0=ALU.min,
                    op1=ALU.subtract).then_inc(gl_set, 1)

            def values_out(i):
                half, t = divmod(i, XT)
                dve.wait_ge(gv_done, i + 1)
                vec.tensor_copy(GV[:, t, 512 * half:512 * (half + 1)], ps[:, 1, :]).then_inc(gv_out, 1)

            gate_set(0)
            values_out(0)
            for i, (t, d) in enumerate(TD):
                dve.wait_ge(gl_exp, i + 1)
                if i >= 1:
                    dve.wait_ge(gl_turn, i)
                edge = 0 if d else CHUNK - 1
                b = decay[0][:, :, :].rearrange("p h (c n) -> p (h c) n", c=2)
                TT(decay[3][:, :, :].rearrange("p h (c n) -> p (h c) n", c=2),
                   b[:, :, edge:edge + 1].to_broadcast([P, 8, CHUNK]), b, ALU.subtract).then_inc(gl_rest, 1)
                vec.tensor_copy(dec[:, d, t, :, :],
                               decay[1][:, :, :].rearrange("p h (c n) -> p h c n", c=2)[:, :, :, edge])\
                    .then_inc(dve_step, k.one())
                q = gqk[:, 0, :, P * t:P * (t + 1)]
                kk = gqk[:, 1, :, P * t:P * (t + 1)]
                TT(qB[:, :, P * t:P * (t + 1)] if d else q, q, decay[1][:, :, :], ALU.mult)\
                    .then_inc(dve_step, k.one())
                TT(decay[2][:, :, :], kk, decay[2][:, :, :], ALU.mult).then_inc(dve_step, k.one())
                dve.wait_ge(gl_rexp, i + 1)
                TT(decay[3][:, :, :], kk, decay[3][:, :, :], ALU.mult).then_inc(gl_qk, 1)
                if i + 1 < len(TD):
                    gate_set(i + 1)
                if i + 1 < 2 * XT:
                    values_out(i + 1)
                dve.wait_ge(gl_att, i + 1)
                dve.wait_ge(gl_zero, 1)
                if i >= 1:
                    dve.wait_ge(gl_mask, i)
                vec.copy_predicated(AT[:, t, :, :],
                                   cst[:, 9 if d else 7, :].bitcast(U32).unsqueeze(1).to_broadcast([P, 4, P]),
                                   ps[:, 4 + i % 2, :].rearrange("p (h n) -> p h n", h=4)).then_inc(gl_mask, 1)
            for rnd, d in enumerate((1, 0)):
                if rnd:
                    dve.wait_ge(o_done, XT)
                step(vec.memset(S[:, 0, :, :], 0.0))

                def update(s):
                    t, c = SCAN[d][s]
                    dve.wait_ge(kv_done, 7 * rnd + s + 1)
                    if s >= 1:
                        dve.wait_ge(st_done, 7 * rnd + s)
                    if s >= 2:
                        dve.wait_ge(o_done, XT * rnd + (s - 2) // 2 + 1)
                    for h in range(G_HEADS):
                        last = STT(out=S[:, (s + 1) % 3, h, :], in0=S[:, s % 3, h, :], scalar=dec[:, d, t, h, c:c + 1],
                                   in1=ps[:, 2 * ((7 * rnd + s) % 2) + h // 2, G_DV * (h % 2):G_DV * (h % 2 + 1)],
                                   op0=ALU.mult, op1=ALU.add)
                        if h == G_HEADS - 1:
                            last.then_inc(st_done, 1)

                def output(i):
                    t = SCAN[d][2 * i][0]
                    n = XT * rnd + i
                    dve.wait_ge(o_done, n + 1)
                    src = ps[:, 4:6, :]
                    dst = O[:, t, :].rearrange("p (a n) -> p a n", a=2)
                    if d:
                        vec.tensor_copy(dst, src).then_inc(o_out, 1)
                    else:
                        TT(dst, src, dst, ALU.add).then_inc(o_out, 1)

                for s in range(7):
                    if s >= 2 and s % 2 == 0:
                        output(s // 2 - 1)
                    update(s)
                output(3)

            for t in range(XT):
                dve.wait_ge(o_stdd, t + 1)
                step(vec.reciprocal(o_inv[:, 4 * t:4 * t + 4], o_std[:, 4 * t:4 * t + 4]))
                for h in range(G_HEADS):
                    o = O[:, t, G_DV * h:G_DV * (h + 1)]
                    last = TS(o, o, o_inv[:, 4 * t + h:4 * t + h + 1], None, ALU.mult)
                last.then_inc(xn_done, 1)
                if t >= 1:
                    norm_out(1, OT, t - 1)
            norm_out(1, OT, XT - 1)
            dve.wait_ge(nt_out, 4 * XT)
            for c in range(KC):
                dve.wait_ge(gr_silu, c + 1)
                TT(OT[:, c, :], OT[:, c, :], zr[c], ALU.mult).then_inc(gr_out, 1)
            for c in range(KC):
                for m in range(2):
                    i = 2 * c + m
                    dve.wait_ge(mg_sig, i + 1)
                    dve.wait_ge(mg_done, 4 * c + 2 * m + 2)
                    s = side[:, 2 + i % 4, :]
                    y = ps[:, 4 * (c % 2) + 2 * m + 1, :]
                    if m == 0:
                        TT(mT[:, c, :], s, y, ALU.mult).then_inc(mg_out, 1)
                    else:
                        step(TT(s, s, y, ALU.mult))
                        TT(mT[:, c, :], mT[:, c, :], s, ALU.add).then_inc(mg_out, 1)
            for t in range(XT):
                for m in range(2):
                    i = 2 * t + m
                    hm = H[:, t, 512 * m:512 * (m + 1)]
                    dve.wait_ge(wo2_done, i + 1)
                    TT(hm, hm, ps[:, i % 4, :], ALU.add).then_inc(wo2_out, 1)
                norm_scale(1, t, XN[:, t, :], H[:, t, :])
                if t >= 1:
                    norm_out(2, aT2, t - 1)
            norm_out(2, aT2, XT - 1)

            dve.wait_ge(rt_done, 1)
            for t in range(XT):
                last = vec.tensor_copy(affT[:, P * t:P * (t + 1)], ps[32 * t:32 * t + EXPERTS, 1, 0:P])
            last.then_inc(rt_out, 1)
            dve.wait_ge(rl_done, 1)
            lg = ps[:, 0, 0:EXPERTS * XT].rearrange("p (t e) -> p t e", t=XT)

            def wide(v):
                return v.unsqueeze(2).to_broadcast([P, XT, EXPERTS])

            step(vec.tensor_reduce(soft[:, 0:4], lg, AX.X, ALU.max))
            TT(logit, lg, wide(soft[:, 0:4]), ALU.subtract).then_inc(rl_sub, 1)
            dve.wait_ge(rl_exp, 1)
            step(vec.tensor_reduce(soft[:, 4:8], logit, AX.X, ALU.add))
            step(vec.reciprocal(soft[:, 8:12], soft[:, 4:8]))
            TT(aff, logit, wide(soft[:, 8:12]), ALU.mult).then_inc(aff_done, 1)
            dve.wait_ge(affT_done, 1)
            step(vec.tensor_copy(affT, ps[0:EXPERTS, 1, :]))
            for _ in range(CAP // 8):
                step(vec.max(max8[0:EXPERTS, :], affT))
                step(vec.match_replace(affT, max8[0:EXPERTS, :], affT, TAKEN_AFF))
            step(TS(takenT, affT, TAKEN_AFF, None, ALU.is_equal))
            step(vec.tensor_tensor_scan(affT, ones[0:EXPERTS, 0:1].to_broadcast([EXPERTS, SEQ]), takenT, 0.0,
                                       ALU.mult, ALU.add))
            step(TT(takenT, affT, takenT, ALU.mult))
            TS(takenT, takenT, -1.0, None, ALU.add).then_inc(rank_done, 1)
            dve.wait_ge(rankT_done, 1)
            step(vec.tensor_copy(rank, ps[:, 2, 0:EXPERTS * XT].rearrange("p (t e) -> p t e", t=XT)))
            dve.wait_ge(em_done, 2 * XT)
            for e0, e1 in ((0, 2), (2, EXPERTS)):
                for t in range(XT):
                    TT(sel[:, t, CAP * e0:CAP * e1].rearrange("p (e c) -> p e c", c=CAP),
                       cst[:, 13, 0:CAP].unsqueeze(1).to_broadcast([P, e1 - e0, CAP]),
                       rank[:, t, e0:e1].unsqueeze(2).to_broadcast([P, e1 - e0, CAP]), ALU.is_equal)\
                        .then_inc(sel_done, 1)

            def gathered(i):
                for hf in range(2):
                    dve.wait_ge(gather_done, 2 * i + hf + 1)
                    TT(xe[:, 4 * hf:4 * hf + 4, :], ps[:, hf, :].rearrange("p (c n) -> p c n", c=4),
                       gains[:, 2, 4 * hf:4 * hf + 4].unsqueeze(2).to_broadcast([P, 4, P]), ALU.mult)\
                        .then_inc(xe_set, 1)

            def paired(i):
                for t in range(XT):
                    TT(selw[:, t, :].rearrange("p (e c) -> p e c", c=CAP),
                       sel_pair[:, t, i, :].rearrange("p (e c) -> p e c", c=CAP),
                       aff_pair[:, t, i, :].unsqueeze(2).to_broadcast([P, 2, CAP]), ALU.mult).then_inc(selw_done, 1)
                for u in range(2):
                    dve.wait_ge(e_silu, 2 * i + u + 1)
                    dve.wait_ge(e_up, 8 * i + 4 * u + 4)
                    TT(hid[:, u, :], hid[:, u, :], ps[:, 2 + u, :], ALU.mult).then_inc(e_hid, 1)
                    if u == 0:
                        dve.wait_ge(gt_done, i + 1)
                        vec.tensor_copy(GT[:, :], ps[:, 7, :]).then_inc(gt_out, 1)
                    dve.wait_ge(e_down, 8 * i + 4 * u + 4)
                    vec.tensor_copy(Y[64 * u:64 * u + 64, 0:512], ps[0:64, 5 + u, :]).then_inc(e_y, 1)

            def combined(i):
                for n in range(2 * XT):
                    t, a = divmod(n, 2)
                    hm = H[:, t, 512 * a:512 * (a + 1)]
                    dve.wait_ge(cb_done, 2 * XT * i + n + 1)
                    TT(hm, hm, ps[:, (2, 3, 4, 7)[n % 4], :], ALU.add).then_inc(cb_out, 1)

            gathered(0)
            dve.wait_ge(sel_done, 2 * XT)
            with dve.Fori(0, PAIRS - 1) as i:
                paired(i)
                gathered(i + 1)
                combined(i)
            paired(PAIRS - 1)
            combined(PAIRS - 1)
            for t in range(XT):
                norm_scale(2, t, xn3[:, t % 2, :], H[:, t, :])
                if t >= 1:
                    norm_out(3, aT3, t - 1)
            norm_out(3, aT3, XT - 1)
            dve.wait_ge(third_in, 48)
            dve.wait_ge(em_out, 2 * XT)

            def final_scale(t):
                dve.wait_ge(ns_done, XT * 3 + t + 1)
                inv = norm_inv[:, t:t + 1]
                step(vec.reciprocal(inv, norm_std[:, XT * 3 + t:XT * 3 + t + 1]))
                STT(out=outb[:, t % 2, :], in0=H[:, t, :], scalar=inv, in1=final_g[:, :], op0=ALU.mult, op1=ALU.mult)\
                    .then_inc(y_set, 1)

            for t in range(XT):
                if t >= 1:
                    final_scale(t - 1)
                for m in range(2):
                    i = 2 * t + m
                    hm = H[:, t, 512 * m:512 * (m + 1)]
                    e = emb[:, i % 2, :]
                    dve.wait_ge(pl_sig, i + 1)
                    step(TT(e, e, embedded[:, t, 512 * m:512 * (m + 1)], ALU.mult))
                    TT(hm, hm, e, ALU.add).then_inc(pl_out, 1)
            final_scale(XT - 1)


def kernel(**inputs):
    import concourse.bacc as bacc
    from concourse.bass_utils import run_bass_kernel_spmd

    g = {n: np.asarray(v) for n, v in inputs.items()}
    nc = bacc.Bacc("TRN2", target_bir_lowering=False, num_devices=1)
    arrays = {}

    def dram(name, a):
        a = np.ascontiguousarray(a)
        arrays[f"in_{name}"] = a
        return nc.dram_tensor(f"in_{name}", a.shape, mybir.dt.from_np(a.dtype), kind="ExternalInput").ap()

    def chunked(name, a):
        return dram(name, a).rearrange("(k p) n -> p k n", p=P)

    w_in, w2 = g["w_in"], g["w_in_2"][0]
    ki = w_in[:, :, COL_KI:COL_WI]
    w_misc = np.concatenate([ki, ki, w_in[:, :, COL_WI:]], -1)
    conv = np.concatenate([g["conv_w"], g["conv_b"][:, None], g["conv_ln_g"][:, None], g["conv_ln_b"][:, None]], 1)
    conv = conv.transpose(0, 2, 1).reshape(DEPTH, 4, P, TAPS + 3).transpose(0, 2, 1, 3)
    post = np.broadcast_to(np.stack([g["post_ln_g"], g["post_ln_b"]], 1)[:, None], (DEPTH, P, 2, D_MODEL))
    cst, rope = constants()
    pad = np.zeros((D_MODEL, 16), np.float32)
    kv = [w2[:, 512 + 64 * i:512 + 64 * (i + 1)] for i in range(2)]
    misc2 = np.concatenate([kv[0], kv[0], kv[1], kv[1], w2[:, 640:768], w2[:, 3840:3856], pad, w2[:, 3856:3872], pad], 1)
    up = np.zeros((64, 512), np.float32)
    for d, n in enumerate(("fwd", "bwd")):
        up[32 * d:32 * d + 16] = g[f"gla_gate_up_{n}_2"][0]
        up[32 * d + 16] = g[f"gla_gate_bias_{n}_2"][0]
    gains = np.stack([g[n][0].reshape(KC, P).T for n in ("norm_mix_2", "gla_norm_2", "norm_ffn_2", "norm_ple_2")], 1)
    B = dict(
        up=dram("up", up), positions=dram("positions", g["positions_2"][0]).partition_broadcast(P),
        gains=dram("gains", gains), router=chunked("router", g["w_router_2"][0]), sink=dram("sink", g["attn_sink_2"][0]),
        w_misc=chunked("w_misc2", misc2), w_in=chunked("w_in2", w2), w_ba=chunked("w_ba", g["w_branch_attn_2"][0]),
        w_bg=chunked("w_bg", g["w_branch_gla_2"][0]), w_wo=chunked("w_wo", g["w_out_2"][0]),
        w_exp=[dram(f"exp_{n}", g[f"w_exp_{n}_2"][0]).rearrange("e (k p) n -> e p k n", p=P)
               for n in ("gate", "up", "down")],
        final=dram("final", g["norm_final_2"]), pT=chunked("pT", g["p_2"][0, 0].T),
        w_pg=chunked("w_pg", g["w_ple_gate_2"][0]), w_p=chunked("w_p", g["w_ple_2"][0]))
    out = nc.dram_tensor("out_0", (SEQ, D_MODEL), mybir.dt.float32, kind="ExternalOutput").ap()
    hybrid_kernel(nc, dram("x", g["x"][0]), dram("meta", g["meta_tokens"]), dram("w_in1", w_in), dram("w_misc", w_misc),
                  dram("conv", conv), dram("w_out", g["w_out"]), dram("post", post), dram("cst", cst), dram("rope", rope),
                  B, out)
    r = run_bass_kernel_spmd(nc, [arrays], core_ids=[0])
    return r.results[0]["out_0"][None]
```
